# Optimizing a Trainium2 kernel written in Bass

```python
import jax
import jax.numpy as jnp
from jax import lax
import numpy as np

D_MODEL = 1024
BATCH = 1
SEQ = 256
DEPTH = 2

GRID_W = 64
CTX_LEN = 256
NORM_EPS = 1e-6
N_MOD = 6

MLA_HEADS = 8
MLA_NOPE = 64
MLA_ROPE = 32
MLA_V = 64
MLA_Q_LORA = 384
MLA_KV_LORA = 256
ROPE_THETA = 10000.0
Q_BLOCK = 128

ML_HEADS = 4
ML_QK = 32
ML_V = 64
ML_CHUNK = 64

RW_HEADS = 4
RW_N = 64
RW_W_LORA = 64
RW_A_LORA = 64
RW_G_LORA = 128
RW_LN_EPS = 64e-5

N_EXPERTS = 64
TOP_K = 8
N_GROUPS = 8
TOPK_GROUPS = 4
D_EXPERT = 256
D_SHARED = 256
ROUTED_SCALE = 2.5
MOE_BLOCK = 128

MLA_WIDTH = MLA_HEADS * MLA_V
ML_WIDTH = ML_HEADS * ML_V
RW_WIDTH = RW_HEADS * RW_N
N_BRANCHES = 3

MLA_IN = MLA_Q_LORA + MLA_KV_LORA + MLA_ROPE
ML_IN = 2 * ML_HEADS * ML_QK + 2 * ML_WIDTH + 4 * ML_HEADS
RW_IN = 3 * RW_WIDTH + 2 * RW_W_LORA + 2 * RW_A_LORA + RW_G_LORA
GATE_IN = N_BRANCHES * D_MODEL
D_IN = MLA_IN + ML_IN + RW_IN + GATE_IN
IN_SPLIT_IDX = (MLA_IN, MLA_IN + ML_IN, MLA_IN + ML_IN + RW_IN)
MLA_SPLIT_IDX = (MLA_Q_LORA, MLA_Q_LORA + MLA_KV_LORA)
ML_SPLIT_IDX = (ML_HEADS * ML_QK, 2 * ML_HEADS * ML_QK, 2 * ML_HEADS * ML_QK + ML_WIDTH,
                2 * ML_HEADS * ML_QK + 2 * ML_WIDTH, 2 * ML_HEADS * ML_QK + 2 * ML_WIDTH + 2 * ML_HEADS)
RW_SPLIT_IDX = (RW_WIDTH, 2 * RW_WIDTH, 3 * RW_WIDTH, 3 * RW_WIDTH + 2 * RW_W_LORA,
                3 * RW_WIDTH + 2 * RW_W_LORA + 2 * RW_A_LORA)

kernel_name = 'hybrid_mla_mlstm_rwkv7_moe_dit'

def rmsnorm(x, g):
    xf = x.astype(jnp.float32)
    y = xf * lax.rsqrt(jnp.mean(xf * xf, axis=-1, keepdims=True) + NORM_EPS)
    return (y * g.astype(jnp.float32)).astype(x.dtype)

def modulate(h, shift, scale):
    return h * (1 + scale) + shift

def flip_time(ts, axis):
    return tuple(jnp.flip(t, axis) for t in ts)

def swiglu(h, w_gate, w_up, w_down):
    return (jax.nn.silu(h @ w_gate) * (h @ w_up)) @ w_down

def axial_rope_tables(n_tokens):
    rows = n_tokens // GRID_W
    row, col = jnp.meshgrid(jnp.arange(rows, dtype=jnp.float32),
                            jnp.arange(GRID_W, dtype=jnp.float32), indexing='ij')
    half = MLA_ROPE // 2
    inv_freq = ROPE_THETA ** (-jnp.arange(0, half, 2, dtype=jnp.float32) / half)
    ang = jnp.concatenate([row.reshape(-1, 1) * inv_freq, col.reshape(-1, 1) * inv_freq], axis=-1)
    return jnp.cos(ang), jnp.sin(ang)

def apply_axial_rope(x, cos, sin):
    B, T, H, R = x.shape
    f = R // 4
    xs = x.reshape(B, T, H, 2, 2, f)
    x1, x2 = xs[..., 0, :], xs[..., 1, :]
    cs = cos.reshape(T, 1, 2, f).astype(x.dtype)
    sn = sin.reshape(T, 1, 2, f).astype(x.dtype)
    return jnp.stack([x1 * cs - x2 * sn, x1 * sn + x2 * cs], axis=-2).reshape(B, T, H, R)

def mla_qkv(z, g_cq, w_uq, g_ckv, w_uk, w_uv, rope):
    B, T, _ = z.shape
    c_q, c_kv, k_rope = jnp.split(z, MLA_SPLIT_IDX, axis=-1)
    q = (rmsnorm(c_q, g_cq) @ w_uq).reshape(B, T, MLA_HEADS, MLA_NOPE + MLA_ROPE)
    c_kv = rmsnorm(c_kv, g_ckv)
    k_nope = (c_kv @ w_uk).reshape(B, T, MLA_HEADS, MLA_NOPE)
    v = (c_kv @ w_uv).reshape(B, T, MLA_HEADS, MLA_V)
    q_nope, q_rope = q[..., :MLA_NOPE], q[..., MLA_NOPE:]
    k_rope = k_rope[:, :, None, :]
    if rope is not None:
        cos, sin = rope
        q_rope = apply_axial_rope(q_rope, cos, sin)
        k_rope = apply_axial_rope(k_rope, cos, sin)
    q = jnp.concatenate([q_nope, q_rope], axis=-1)
    k = jnp.concatenate([k_nope, jnp.broadcast_to(k_rope, (B, T, MLA_HEADS, MLA_ROPE))], axis=-1)
    return q, k, v

def attend(q, k, v):
    s = jnp.einsum('bqhd,bkhd->bhqk', q, k).astype(jnp.float32) * (MLA_NOPE + MLA_ROPE) ** -0.5
    p = jax.nn.softmax(s, axis=-1).astype(v.dtype)
    return jnp.einsum('bhqk,bkhd->bqhd', p, v)

def blocked_attend(q, k, v):
    B, T, H, dk = q.shape
    qb = q.reshape(B, T // Q_BLOCK, Q_BLOCK, H, dk).swapaxes(0, 1)
    ob = lax.map(lambda qi: attend(qi, k, v), qb)
    return ob.swapaxes(0, 1).reshape(B, T, H, -1)

def mlstm_chunkwise(q, k, v, i_pre, f_pre, state):
    B, H, T, _ = q.shape
    L = ML_CHUNK
    nc = T // L

    def chunk(t):
        return jnp.moveaxis(t.reshape((B, H, nc, L) + t.shape[3:]), 2, 0)

    xs = tuple(chunk(t) for t in (q, k, v, i_pre, f_pre))
    tril = jnp.tril(jnp.ones((L, L), dtype=bool))

    def step(carry, inp):
        C, n, m = carry
        qc, kc, vc, ic, fc = inp
        b = jnp.cumsum(jax.nn.log_sigmoid(fc), axis=-1)
        dlog = jnp.where(tril, b[..., :, None] - b[..., None, :] + ic[..., None, :], -jnp.inf)
        g = b + m[..., None]
        mj = jnp.maximum(g, dlog.max(-1))
        s = jnp.exp(dlog - mj[..., None]) * jnp.einsum('bhjd,bhsd->bhjs', qc, kc)
        inter = jnp.exp(g - mj)
        num = jnp.einsum('bhjs,bhsv->bhjv', s, vc) + inter[..., None] * jnp.einsum('bhvd,bhjd->bhjv', C, qc)
        den = s.sum(-1) + inter * jnp.einsum('bhd,bhjd->bhj', n, qc)
        h = num / jnp.maximum(jnp.abs(den), jnp.exp(-mj))[..., None]
        b_last = b[..., -1]
        lw = b_last[..., None] - b + ic
        m_new = jnp.maximum(b_last + m, lw.max(-1))
        carry_w = jnp.exp(b_last + m - m_new)
        we = jnp.exp(lw - m_new[..., None])
        C_new = carry_w[..., None, None] * C + jnp.einsum('bhs,bhsv,bhsd->bhvd', we, vc, kc)
        n_new = carry_w[..., None] * n + jnp.einsum('bhs,bhsd->bhd', we, kc)
        return (C_new, n_new, m_new), h

    state, h = lax.scan(step, state, xs)
    return jnp.moveaxis(h, 0, 2).reshape(B, H, T, -1), state

def mlstm_inputs(cols, b_i, b_f, d):
    q, k, v, o, i, f = cols
    B, T, _ = q.shape

    def heads(t, dh):
        return t.reshape(B, T, ML_HEADS, dh).transpose(0, 2, 1, 3).astype(jnp.float32)

    sl = slice(d * ML_HEADS, (d + 1) * ML_HEADS)
    i_pre = (i[..., sl] + b_i[d]).astype(jnp.float32).transpose(0, 2, 1)
    f_pre = (f[..., sl] + b_f[d]).astype(jnp.float32).transpose(0, 2, 1)
    return heads(q, ML_QK) * ML_QK ** -0.5, heads(k, ML_QK), heads(v, ML_V), i_pre, f_pre

def mlstm_out(h, o, g_norm):
    B, H, T, V = h.shape
    hn = rmsnorm(jnp.swapaxes(h, 1, 2), g_norm.reshape(H, V))
    return hn.reshape(B, T, H * V) * jax.nn.sigmoid(o.astype(jnp.float32))

def mlstm_mixer(zx, zc, b_i, b_f, g_norm, with_ctx):
    cols_x = jnp.split(zx, ML_SPLIT_IDX, axis=-1)
    cols_c = jnp.split(zc, ML_SPLIT_IDX, axis=-1)
    B = zx.shape[0]
    state0 = (jnp.zeros((B, ML_HEADS, ML_V, ML_QK), jnp.float32),
              jnp.zeros((B, ML_HEADS, ML_QK), jnp.float32),
              jnp.zeros((B, ML_HEADS), jnp.float32))
    hs_x, hs_c = [], []
    for d in range(2):
        in_x = mlstm_inputs(cols_x, b_i, b_f, d)
        in_c = mlstm_inputs(cols_c, b_i, b_f, d)
        if d == 1:
            in_x, in_c = flip_time(in_x, 2), flip_time(in_c, 2)
        h_c, state_ctx = mlstm_chunkwise(*in_c, state0)
        h_x, _ = mlstm_chunkwise(*in_x, state_ctx)
        if d == 1:
            h_x, h_c = jnp.flip(h_x, 2), jnp.flip(h_c, 2)
        hs_x.append(h_x)
        hs_c.append(h_c)
    out_x = mlstm_out(hs_x[0] + hs_x[1], cols_x[3], g_norm)
    if not with_ctx:
        return out_x, None
    return out_x, mlstm_out(hs_c[0] + hs_c[1], cols_c[3], g_norm)

def centred_shift(z, mu):
    zp = jnp.pad(z, ((0, 0), (1, 1), (0, 0)))
    return z + (0.5 * (zp[:, :-2] + zp[:, 2:]) - z) * mu

def rwkv7_scan(r, decay, k, v, kk, a, s0):
    def step(s, inp):
        r_t, w_t, k_t, v_t, kk_t, a_t = inp
        sa = jnp.einsum('bhij,bhj->bhi', s, -kk_t)
        s = (s * w_t[..., None, :] + sa[..., :, None] * (kk_t * a_t)[..., None, :]
             + v_t[..., :, None] * k_t[..., None, :])
        return s, jnp.einsum('bhij,bhj->bhi', s, r_t)

    xs = tuple(jnp.moveaxis(t, 1, 0) for t in (r, decay, k, v, kk, a))
    s, ys = lax.scan(step, s0, xs)
    return jnp.moveaxis(ys, 0, 1), s

def rwkv_direction(parts, d, w0, w2, a0, a2, k_a):
    r, k, v, wl, al, kk = parts
    B, T, _ = r.shape

    def heads(t):
        return t.reshape(B, T, RW_HEADS, RW_N)

    wl_d = wl[..., d * RW_W_LORA:(d + 1) * RW_W_LORA]
    al_d = al[..., d * RW_A_LORA:(d + 1) * RW_A_LORA]
    w = -jax.nn.softplus(-(w0[d] + jnp.tanh(wl_d) @ w2[d])) - 0.5
    decay = jnp.exp(-jnp.exp(w))
    a = jax.nn.sigmoid(a0[d] + al_d @ a2[d])
    kd = k * (1 + (a - 1) * k_a)
    return heads(r), heads(decay), heads(kd), heads(v), kk, heads(a)

def rwkv_bonus(inp, r_k):
    r, _, k, v, _, _ = inp
    return jnp.sum(r * k * r_k, axis=-1, keepdims=True) * v

def rwkv_out(y, bonus, gl, g2, lnx_w, lnx_b):
    B, T, H, N = y.shape
    mean = jnp.mean(y, axis=-1, keepdims=True)
    var = jnp.mean(jnp.square(y - mean), axis=-1, keepdims=True)
    yn = (y - mean) * lax.rsqrt(var + RW_LN_EPS) * lnx_w.reshape(H, N) + lnx_b.reshape(H, N)
    g = jax.nn.sigmoid(gl) @ g2
    return (yn + bonus).reshape(B, T, H * N) * g

def rwkv_mixer(zx, zc, mu, w0, w2, a0, a2, g2, k_k, k_a, r_k, lnx_w, lnx_b, with_ctx):
    def prep(z):
        B, T, _ = z.shape
        r, k, v, wl, al, gl = jnp.split(centred_shift(z, mu).astype(jnp.float32), RW_SPLIT_IDX, axis=-1)
        kk = (k * k_k).reshape(B, T, RW_HEADS, RW_N)
        kk = kk / jnp.maximum(jnp.linalg.norm(kk, axis=-1, keepdims=True), 1e-12)
        return (r, k, v, wl, al, kk), gl

    parts_x, gl_x = prep(zx)
    parts_c, gl_c = prep(zc)
    s_init = jnp.zeros((zx.shape[0], RW_HEADS, RW_N, RW_N), jnp.float32)
    ys_x, ys_c, bs_x, bs_c = [], [], [], []
    for d in range(2):
        in_x = rwkv_direction(parts_x, d, w0, w2, a0, a2, k_a)
        in_c = rwkv_direction(parts_c, d, w0, w2, a0, a2, k_a)
        bs_x.append(rwkv_bonus(in_x, r_k))
        if with_ctx:
            bs_c.append(rwkv_bonus(in_c, r_k))
        if d == 1:
            in_x, in_c = flip_time(in_x, 1), flip_time(in_c, 1)
        y_c, s_ctx = rwkv7_scan(*in_c, s_init)
        y_x, _ = rwkv7_scan(*in_x, s_ctx)
        if d == 1:
            y_x, y_c = jnp.flip(y_x, 1), jnp.flip(y_c, 1)
        ys_x.append(y_x)
        ys_c.append(y_c)
    out_x = rwkv_out(ys_x[0] + ys_x[1], bs_x[0] + bs_x[1], gl_x, g2, lnx_w, lnx_b)
    if not with_ctx:
        return out_x, None
    return out_x, rwkv_out(ys_c[0] + ys_c[1], bs_c[0] + bs_c[1], gl_c, g2, lnx_w, lnx_b)

def merge_branches(gate_cols, branches, w_brs, w_out):
    B, T, _ = gate_cols.shape
    g = jax.nn.sigmoid(gate_cols.astype(jnp.float32)).reshape(B, T, N_BRANCHES, D_MODEL)
    y = g[:, :, 0] * (branches[0] @ w_brs[0])
    for i in range(1, N_BRANCHES):
        y = y + g[:, :, i] * (branches[i] @ w_brs[i])
    return y @ w_out

def hybrid_mixer(hx, hc, rope, w_in, g_cq, w_uq, g_ckv, w_uk, w_uv,
                 ml_b_i, ml_b_f, ml_g_norm,
                 rw_mu, rw_w0, rw_w2, rw_a0, rw_a2, rw_g2, rw_k_k, rw_k_a, rw_r_k, rw_lnx_w, rw_lnx_b,
                 w_br_mla, w_br_ml, w_br_rw, w_out, with_ctx):
    B, T, _ = hx.shape
    mla_x, ml_x, rw_x, gate_x = jnp.split(hx @ w_in, IN_SPLIT_IDX, axis=-1)
    mla_c, ml_c, rw_c, gate_c = jnp.split(hc @ w_in, IN_SPLIT_IDX, axis=-1)
    q_x, k_x, v_x = mla_qkv(mla_x, g_cq, w_uq, g_ckv, w_uk, w_uv, rope)
    q_c, k_c, v_c = mla_qkv(mla_c, g_cq, w_uq, g_ckv, w_uk, w_uv, None)
    att_x = blocked_attend(q_x, jnp.concatenate([k_c, k_x], axis=1),
                           jnp.concatenate([v_c, v_x], axis=1)).reshape(B, T, MLA_WIDTH)
    ml_out_x, ml_out_c = mlstm_mixer(ml_x, ml_c, ml_b_i, ml_b_f, ml_g_norm, with_ctx)
    rw_out_x, rw_out_c = rwkv_mixer(rw_x, rw_c, rw_mu, rw_w0, rw_w2, rw_a0, rw_a2, rw_g2,
                                    rw_k_k, rw_k_a, rw_r_k, rw_lnx_w, rw_lnx_b, with_ctx)
    w_brs = (w_br_mla, w_br_ml, w_br_rw)
    y_x = merge_branches(gate_x, (att_x, ml_out_x, rw_out_x), w_brs, w_out)
    if not with_ctx:
        return y_x, None
    att_c = attend(q_c, k_c, v_c).reshape(B, q_c.shape[1], MLA_WIDTH)
    y_c = merge_branches(gate_c, (att_c, ml_out_c, rw_out_c), w_brs, w_out)
    return y_x, y_c

def routed_experts(xf, eidx, wts, w_g, w_u, w_d):
    N, D = xf.shape
    A = N * TOP_K
    flat_e = eidx.reshape(-1)
    order = jnp.argsort(flat_e)
    sorted_e = flat_e[order]
    tok = order // TOP_K
    counts = jnp.bincount(flat_e, length=N_EXPERTS)
    padded = (counts + MOE_BLOCK - 1) // MOE_BLOCK * MOE_BLOCK
    pad_end = jnp.cumsum(padded)
    pad_start = pad_end - padded
    start = jnp.cumsum(counts) - counts
    dest = pad_start[sorted_e] + jnp.arange(A) - start[sorted_e]
    n_blocks = -(-(A + N_EXPERTS * (MOE_BLOCK - 1)) // MOE_BLOCK)
    buf = jnp.zeros((n_blocks * MOE_BLOCK, D), xf.dtype).at[dest].set(xf[tok])
    block_e = jnp.minimum(jnp.searchsorted(pad_end, jnp.arange(n_blocks) * MOE_BLOCK, side='right'),
                          N_EXPERTS - 1)

    def expert_block(args):
        xb, e = args
        return swiglu(xb, w_g[e], w_u[e], w_d[e])

    yb = lax.map(expert_block, (buf.reshape(n_blocks, MOE_BLOCK, D), block_e))
    y = yb.reshape(-1, D)[dest]
    y = y * wts.reshape(-1)[order][:, None].astype(y.dtype)
    return jnp.zeros((N, D), y.dtype).at[tok].add(y)

def moe_ffn(xf, w_router, router_bias, w_e_gate, w_e_up, w_e_down, w_s_gate, w_s_up, w_s_down):
    N = xf.shape[0]
    scores = jax.nn.sigmoid((xf @ w_router).astype(jnp.float32))
    biased = scores + router_bias
    group_score = lax.top_k(biased.reshape(N, N_GROUPS, N_EXPERTS // N_GROUPS), 2)[0].sum(-1)
    _, gidx = lax.top_k(group_score, TOPK_GROUPS)
    gmask = jnp.any(gidx[..., None] == jnp.arange(N_GROUPS), axis=1)
    masked = jnp.where(jnp.repeat(gmask, N_EXPERTS // N_GROUPS, axis=1), biased, -jnp.inf)
    _, eidx = lax.top_k(masked, TOP_K)
    wts = jnp.take_along_axis(scores, eidx, axis=1)
    wts = wts / (wts.sum(-1, keepdims=True) + 1e-20) * ROUTED_SCALE
    routed = routed_experts(xf, eidx, wts, w_e_gate, w_e_up, w_e_down)
    return routed + swiglu(xf, w_s_gate, w_s_up, w_s_down)

def setup_inputs(seed: int = 0) -> dict:
    key = jax.random.key(seed)
    keys = iter(jax.random.split(key, 48))
    L = DEPTH
    f32 = jnp.float32

    def nrm(shape, scale):
        return jax.random.normal(next(keys), shape, f32) * scale

    def gain(shape):
        return 1.0 + nrm(shape, 0.02)

    def unif(shape, lo, hi):
        return jax.random.uniform(next(keys), shape, f32, lo, hi)

    return {
        'x': nrm((BATCH, SEQ, D_MODEL), 1.0),
        'c': nrm((BATCH, D_MODEL), 1.0),
        'ctx': nrm((BATCH, CTX_LEN, D_MODEL), 1.0),
        'c_ctx': nrm((D_MODEL,), 1.0),
        'w_mod': nrm((L, D_MODEL, N_MOD * D_MODEL), 0.5 * D_MODEL ** -0.5),
        'b_mod': nrm((L, N_MOD * D_MODEL), 0.02),
        'g_mix': gain((L, D_MODEL)),
        'g_ffn': gain((L, D_MODEL)),
        'w_in': nrm((L, D_MODEL, D_IN), D_MODEL ** -0.5),
        'g_cq': gain((L, MLA_Q_LORA)),
        'w_uq': nrm((L, MLA_Q_LORA, MLA_HEADS * (MLA_NOPE + MLA_ROPE)), MLA_Q_LORA ** -0.5),
        'g_ckv': gain((L, MLA_KV_LORA)),
        'w_uk': nrm((L, MLA_KV_LORA, MLA_HEADS * MLA_NOPE), MLA_KV_LORA ** -0.5),
        'w_uv': nrm((L, MLA_KV_LORA, MLA_WIDTH), MLA_KV_LORA ** -0.5),
        'ml_b_i': nrm((L, 2, ML_HEADS), 0.1),
        'ml_b_f': unif((L, 2, ML_HEADS), 3.0, 6.0),
        'ml_g_norm': gain((L, ML_WIDTH)),
        'rw_mu': unif((L, RW_IN), 0.0, 1.0),
        'rw_w0': unif((L, 2, RW_WIDTH), -6.0, -1.0),
        'rw_w2': nrm((L, 2, RW_W_LORA, RW_WIDTH), 0.1),
        'rw_a0': nrm((L, 2, RW_WIDTH), 0.1),
        'rw_a2': nrm((L, 2, RW_A_LORA, RW_WIDTH), 0.1),
        'rw_g2': nrm((L, RW_G_LORA, RW_WIDTH), RW_G_LORA ** -0.5),
        'rw_k_k': 0.85 + nrm((L, RW_WIDTH), 0.02),
        'rw_k_a': gain((L, RW_WIDTH)),
        'rw_r_k': nrm((L, RW_HEADS, RW_N), 0.1),
        'rw_lnx_w': gain((L, RW_WIDTH)),
        'rw_lnx_b': nrm((L, RW_WIDTH), 0.02),
        'w_br_mla': nrm((L, MLA_WIDTH, D_MODEL), MLA_WIDTH ** -0.5),
        'w_br_ml': nrm((L, ML_WIDTH, D_MODEL), ML_WIDTH ** -0.5),
        'w_br_rw': nrm((L, RW_WIDTH, D_MODEL), RW_WIDTH ** -0.5),
        'w_out': nrm((L, D_MODEL, D_MODEL), D_MODEL ** -0.5),
        'w_router': nrm((L, D_MODEL, N_EXPERTS), D_MODEL ** -0.5),
        'router_bias': nrm((L, N_EXPERTS), 0.01),
        'w_e_gate': nrm((L, N_EXPERTS, D_MODEL, D_EXPERT), D_MODEL ** -0.5),
        'w_e_up': nrm((L, N_EXPERTS, D_MODEL, D_EXPERT), D_MODEL ** -0.5),
        'w_e_down': nrm((L, N_EXPERTS, D_EXPERT, D_MODEL), D_EXPERT ** -0.5),
        'w_s_gate': nrm((L, D_MODEL, D_SHARED), D_MODEL ** -0.5),
        'w_s_up': nrm((L, D_MODEL, D_SHARED), D_MODEL ** -0.5),
        'w_s_down': nrm((L, D_SHARED, D_MODEL), D_SHARED ** -0.5),
        'g_final': gain((D_MODEL,)),
    }

def reference(x, c, ctx, c_ctx, w_mod, b_mod, g_mix, g_ffn, w_in, g_cq, w_uq, g_ckv, w_uk, w_uv,
              ml_b_i, ml_b_f, ml_g_norm, rw_mu, rw_w0, rw_w2, rw_a0, rw_a2, rw_g2, rw_k_k, rw_k_a,
              rw_r_k, rw_lnx_w, rw_lnx_b, w_br_mla, w_br_ml, w_br_rw, w_out, w_router, router_bias,
              w_e_gate, w_e_up, w_e_down, w_s_gate, w_s_up, w_s_down, g_final):
    B, T, D = x.shape
    rope = axial_rope_tables(T)
    cond_x = jax.nn.silu(c)
    cond_c = jax.nn.silu(c_ctx)[None, :]
    for l in range(DEPTH):
        last = l == DEPTH - 1
        mod_x = jnp.split((cond_x @ w_mod[l] + b_mod[l])[:, None, :], N_MOD, axis=-1)
        mod_c = jnp.split((cond_c @ w_mod[l] + b_mod[l])[:, None, :], N_MOD, axis=-1)
        hx = modulate(rmsnorm(x, g_mix[l]), mod_x[0], mod_x[1])
        hc = modulate(rmsnorm(ctx, g_mix[l]), mod_c[0], mod_c[1])
        y_x, y_c = hybrid_mixer(hx, hc, rope, w_in[l], g_cq[l], w_uq[l], g_ckv[l], w_uk[l], w_uv[l],
                                ml_b_i[l], ml_b_f[l], ml_g_norm[l],
                                rw_mu[l], rw_w0[l], rw_w2[l], rw_a0[l], rw_a2[l], rw_g2[l],
                                rw_k_k[l], rw_k_a[l], rw_r_k[l], rw_lnx_w[l], rw_lnx_b[l],
                                w_br_mla[l], w_br_ml[l], w_br_rw[l], w_out[l], not last)
        x = x + mod_x[2] * y_x
        hx = modulate(rmsnorm(x, g_ffn[l]), mod_x[3], mod_x[4]).reshape(-1, D)
        moe_w = (w_router[l], router_bias[l], w_e_gate[l], w_e_up[l], w_e_down[l],
                 w_s_gate[l], w_s_up[l], w_s_down[l])
        if last:
            x = x + mod_x[5] * moe_ffn(hx, *moe_w).reshape(B, T, D)
        else:
            ctx = ctx + mod_c[2] * y_c
            hc = modulate(rmsnorm(ctx, g_ffn[l]), mod_c[3], mod_c[4]).reshape(-1, D)
            f = moe_ffn(jnp.concatenate([hx, hc], axis=0), *moe_w)
            x = x + mod_x[5] * f[:B * T].reshape(B, T, D)
            ctx = ctx + mod_c[5] * f[B * T:].reshape(ctx.shape)
    return rmsnorm(x, g_final)


_drawn_inputs = setup_inputs


def setup_inputs(seed=0):
    import zlib

    import numpy as np

    out = dict(_drawn_inputs(seed))
    spreads = {}
    factors = {'g_cq': 4.56,
     'g_ckv': 3.778,
     'ml_b_i': 8.0,
     'ml_g_norm': 2.695,
     'rw_lnx_w': 2.926,
     'rw_lnx_b': 3.094}
    for name, (base, spread) in spreads.items():
        noise = np.random.default_rng([zlib.crc32(name.encode()), seed]).standard_normal(out[name].shape)
        drawn = base * np.exp(spread * noise) if base else spread * noise
        out[name] = jnp.asarray(drawn.astype(out[name].dtype))
    for name, factor in factors.items():
        out[name] = (out[name] * factor).astype(out[name].dtype)
    return out
```

```python
from contextlib import ExitStack

import numpy as np

import concourse.bass as bass
from concourse import mybir

ALU = mybir.AluOpType
ACT = mybir.ActivationFunctionType
F32 = mybir.dt.float32
AX_X = mybir.AxisListType.X

P = 128
L = 2
D = 1024
KD = D // P
TC = 256
TX = 256
T = TC + TX
TT = T // P
EPS = 1e-6
HEADS, NOPE, ROPE, DV = 8, 64, 32, 64
QL, KVL = 384, 256
ATT_SCALE = float(NOPE + ROPE) ** -0.5
MLH, MLQK = 4, 32
RWH, RN = 4, 64
C = 64
NC = T // C
RW_EPS = 64e-5
E, TOPK, NG, TOPG = 64, 8, 8, 4
FE = 256
ROUTED_SCALE = 2.5
BIG = 1e30

RING, CHUNK = 4, 4096
N_MOD_CH = 12
CH_MLA, CH_UQ, CH_ML, CH_RW, CH_MERGE, CH_OUT = 12, 14, 15, 17, 20, 28
N_CH = 30
CH_COLS = [CHUNK] * 12 + [4096, 4096, 3072, 4096, 3072, 4096, 4096, 1024] + [4096] * 10
EXPERT = 2 * KD * FE + 2 * D

WS_W2, WS_A2, WS_G2, WS_RT, WS_N = 0, 256, 512, 768, 1280

SM = {}
_at = 0
for _name, _n in (("g_mix", 8), ("g_ffn", 8), ("b_mod", 48), ("g_cq", 3), ("g_ckv", 2), ("ml_b", 1), ("ml_g", 2),
                  ("mu", 9), ("w0", 4), ("a0", 4), ("k_k", 2), ("k_a", 2), ("r_k", 2), ("lnx_w", 2), ("lnx_b", 2),
                  ("rb", 64)):
    SM[_name] = _at
    _at += _n
SM_N = _at

CN = {}
_at = 0
for _name, _n in (("ident", 128), ("ones", 128), ("bd", 128), ("mlmask", 256), ("rwmask", 256), ("lev", 384),
                  ("reset", 512), ("cs", 512), ("sel", 1024), ("dup", 64), ("tri", 64), ("eps", 2), ("cond", 16),
                  ("g_final", 8)):
    CN[_name] = _at
    _at += _n
CN_N = _at


class Chain:

    def __init__(self, eng, sem):
        self.eng, self.sem, self.n = eng, sem, 0

    def add(self, ins):
        self.n += 1
        ins.then_inc(self.sem, 1)

    def settle(self):
        self.eng.wait_ge(self.sem, self.n)

    def link(self, ins):
        self.add(ins)
        self.settle()


def bcast(ap, axis, n):
    a = ap.unsqueeze(axis)
    shape = list(a.shape)
    shape[axis] = n
    return a.broadcast_to(shape)


def build(nc, xin, consts, smalls, wsm, wst, wexp, out):
    es = ExitStack()
    with es:
        def sb(name, shape, dt=F32):
            return es.enter_context(nc.sbuf_tensor(name, shape, dt))

        def sem(name):
            return es.enter_context(nc.semaphore(name))

        def signals(stage, **per_layer):
            return {n: sem(f"{stage}_{n}") for n in per_layer}, per_layer

        R = sb("resid", [P, KD, T])
        H = sb("normed", [P, KD, T])
        BR = sb("branches", [P, KD, T])
        W = sb("ring", [P, RING * CHUNK])
        WS = sb("small_weights", [P, WS_N])
        S_ = sb("smalls", [P, SM_N])
        CT = sb("consts", [P, CN_N])
        MOD = sb("modv", [P, 48, 2])
        AMX = sb("mod_scale", [P, 2, KD, 2])
        COND = sb("condv", [P, KD, 2])
        ARENA = 18560
        A = sb("arena", [P, ARENA])
        ps = [es.enter_context(nc.psum_tensor(f"bank{i}", [P, 512], F32)) for i in range(8)]
        wrows = nc.dram_tensor("route_rows", (L, E + 1, T), F32, kind="Internal").ap()

        def cn(name, n, o=0):
            return CT[:, CN[name] + o:CN[name] + o + n]

        def sm(name, j=0, n=1):
            return S_[:, SM[name] + j:SM[name] + j + n]

        ident, ones, bd = cn("ident", P), cn("ones", P), cn("bd", P)

        def arena(at, *shape):
            n = int(np.prod(shape))
            v = A[:, at:at + n]
            if len(shape) == 2:
                v = v.rearrange("p (a b) -> p a b", b=shape[1])
            if len(shape) == 3:
                v = v.rearrange("p (a b c) -> p a b c", b=shape[1], c=shape[2])
            return v

        def chunk(j):
            return W[:, (j % RING) * CHUNK:(j % RING + 1) * CHUNK]

        consts_in, x_in = sem("consts_in"), sem("x_in")
        smalls_in = sem("smalls_in")
        chunk_in = [sem(f"chunk_in{j}") for j in range(RING)]
        xt_pe, resid_first = sem("xt_pe"), sem("resid_first")
        silu_done = sem("silu_done")
        cond_ready = sem("cond_ready")
        mod_mm = sem("mod_mm")
        mod_ready = sem("mod_ready")
        NORM = dict(sq=KD, mm=1, rs=1, n=KD, h=2 * KD)
        norm = {w: {n: sem(f"{w}_{n}") for n in ("sq", "mm", "rs", "n", "h")} for w in ("mix", "ffn", "fin")}
        act_sem, dve_sem, pool_sem = sem("act_chain"), sem("dve_chain"), sem("pool_chain")
        out_done = sem("out_done")

        def wait_chunk(pe, l, j):
            per = len(range(j % RING, N_CH, RING))
            pe.wait_ge(chunk_in[j % RING], 16 * (l * per + j // RING + 1))

        SQ, RS = arena(0, KD, T), arena(4096, T)

        def norm_act_square(act, l, w, c0):
            for k in range(KD):
                nc.scalar.activation(SQ[:, k, c0:], R[:, k, c0:], ACT.Square).then_inc(norm[w]["sq"], 1)

        def norm_pe(pe, l, w, c0):
            for k in range(KD):
                pe.wait_ge(norm[w]["sq"], l * NORM["sq"] + k + 1)
                last = nc.tensor.matmul(ps[7][:, c0:], ones, SQ[:, k, c0:], start=(k == 0), stop=(k == KD - 1))
            last.then_inc(norm[w]["mm"], 1)

        def norm_act_rs(act, ch, l, w, c0):
            act.wait_ge(norm[w]["mm"], l * NORM["mm"] + 1)
            ch.link(nc.scalar.activation(RS[:, c0:], ps[7][:, c0:], ACT.Ln, scale=1.0 / D, bias=cn("eps", 1)))
            nc.scalar.activation(RS[:, c0:], RS[:, c0:], ACT.Exp, scale=-0.5).then_inc(norm[w]["rs"], 1)

        def norm_dve(dve, l, w, c0):
            dve.wait_ge(norm[w]["rs"], l * NORM["rs"] + 1)
            for k in range(KD):
                nc.vector.tensor_tensor(H[:, k, c0:], R[:, k, c0:], RS[:, c0:], ALU.mult).then_inc(norm[w]["n"], 1)

        def norm_act_modulate(act, l, w, c0):
            v, shift = (0, 0) if w == "mix" else (1, 24)
            for k in range(KD):
                act.wait_ge(norm[w]["n"], l * NORM["n"] + k + 1)
                for half in range(2):
                    if half * TC < c0:
                        continue
                    part = H[:, k, half * TC:(half + 1) * TC]
                    nc.scalar.activation(part, part, ACT.Identity, scale=AMX[:, v, k, half:half + 1],
                                                          bias=MOD[:, shift + k, half:half + 1]).then_inc(norm[w]["h"], 1)

        def project(pe, bank, weights, j0, n):
            for k in range(KD):
                last = nc.tensor.matmul(bank, weights[:, k, j0:j0 + n], H[:, k, :], start=(k == 0), stop=(k == KD - 1))
            return last

        def cols(n, k):
            return chunk(n)[:, 0:CH_COLS[n]].rearrange("p (k m) -> p k m", k=k)

        def mod_pe(pe, l):
            if l == 0:
                pe.wait_ge(cond_ready, 1)
            base = l * len(range(0, N_CH, RING)), l * len(range(2, N_CH, RING))
            with pe.Fori(0, N_MOD_CH // RING) as i:
                for j in range(RING):
                    pe.wait_ge(chunk_in[j], (i + base[j // 2] + 1) * 16)
                    w = chunk(j).rearrange("p (k m) -> p k m", k=KD)
                    for m in range(4):
                        for k in range(KD):
                            last = nc.tensor.matmul(ps[0][:, bass.ds(i * 32 + (j * 4 + m) * 2, 2)], w[:, k, m * P:(m + 1) * P],
                                                    COND[:, k, :], start=(k == 0), stop=(k == KD - 1))
                    last.then_inc(mod_mm, 1)

        def mod_dve(dve, ch, l):
            dve.wait_ge(smalls_in, l * 32 + 32)
            dve.wait_ge(mod_mm, l * N_MOD_CH + N_MOD_CH)
            ch.link(nc.vector.tensor_tensor(MOD[:, :, :], ps[0][:, 0:96].rearrange("p (m c) -> p m c", c=2),
                                            bcast(sm("b_mod", 0, 48), 2, 2), ALU.add))
            for v, scale in ((0, 8), (1, 32)):
                ch.link(nc.vector.tensor_scalar(AMX[:, v, :, :], MOD[:, scale:scale + KD, :], 1.0, None, ALU.add))
                last = nc.vector.tensor_tensor(AMX[:, v, :, :], AMX[:, v, :, :],
                                               bcast(sm("g_mix" if v == 0 else "g_ffn", 0, KD), 2, 2), ALU.mult)
                if v == 0:
                    ch.link(last)
            last.then_inc(mod_ready, 1)

        Z, ZSQ = arena(0, 5, T), arena(2560, 5, T)
        KP = arena(5120, T)
        RSL = arena(5632, 2, T)
        qT, kT, vtok = arena(6656, HEADS, T), arena(10752, HEADS, T), arena(14848, TT, HEADS * DV)
        Pb, PT = arena(0, 2, 512), arena(1024, 2, 512)
        st_nm, st_sum, st_rec = arena(16896, 64), arena(16960, 64), arena(17024, 64)
        mla, MLA = signals("mla", z=6, zev=5, kp=1, kr=1, krc=1, ss=2, rs=2, zn=5, p=20, qe=8, kve=12,
                                                      s=32, nm=32, ex=32, pn=32, t=32, pte=32, o=32, oe=4)

        def units_mla(l):
            return [(h, q, 2 if q < 2 else 4) for h in range(HEADS) for q in range(4) if l == 0 or q >= 2]

        def mla_pe(pe, l):
            pe.wait_ge(norm["mix"]["h"], l * NORM["h"] + 2 * KD)
            for j in range(6):
                n = CH_MLA + j // 4
                if j % 4 == 0:
                    wait_chunk(pe, l, n)
                w = chunk(n).rearrange("p (k m) -> p k m", k=KD) if j < 4 else \
                    chunk(n)[:, 0:2048].rearrange("p (k m) -> p k m", k=KD)
                project(pe, ps[j][:, :], w, (j % 4) * P, P).then_inc(mla["z"], 1)
            pe.wait_ge(mla["kp"], l * MLA["kp"] + 1)
            nc.tensor.matmul(ps[5][64:128, :], cn("dup", 64)[0:64, :], KP[0:64, :], start=True, stop=True).then_inc(mla["kr"], 1)
            for g, (j0, j1) in enumerate(((0, 3), (3, 5))):
                pe.wait_ge(mla["zev"], l * MLA["zev"] + j1)
                for j in range(j0, j1):
                    last = nc.tensor.matmul(ps[6 + g][:, :], ones, ZSQ[:, j, :], start=(j == j0), stop=(j == j1 - 1))
                last.then_inc(mla["ss"], 1)
            pe.wait_ge(mla["zn"], l * MLA["zn"] + 5)
            ukv = chunk(CH_MLA + 1)[:, 2048:4096].rearrange("p (a k m) -> p a k m", a=2, k=2)
            wait_chunk(pe, l, CH_UQ)
            uq = cols(CH_UQ, 3)
            for j in range(20):
                if j >= 13:
                    pe.wait_ge(mla["kve"], l * MLA["kve"] + j - 5 - 7)
                elif j >= 5:
                    pe.wait_ge(mla["qe"], l * MLA["qe"] + j - 4)
                if j < 8:
                    for k in range(3):
                        last = nc.tensor.matmul(ps[j % 5][:, :], uq[:, k, j * P:(j + 1) * P], Z[:, k, :], start=(k == 0), stop=(k == 2))
                elif j < 16:
                    for k in range(2):
                        last = nc.tensor.matmul(ps[j % 5][0:64, :], ukv[:, 0, k, (j - 8) * 64:(j - 7) * 64], Z[:, 3 + k, :],
                                                start=(k == 0), stop=(k == 1))
                else:
                    t = j - 16
                    for k in range(2):
                        last = nc.tensor.matmul(ps[j % 5][:, :], Z[:, 3 + k, t * P:(t + 1) * P], ukv[:, 1, k, :],
                                                start=(k == 0), stop=(k == 1))
                last.then_inc(mla["p"], 1)
            pe.wait_ge(mla["krc"], l * MLA["krc"] + 1)
            pe.wait_ge(mla["kve"], l * MLA["kve"] + 12)
            units = units_mla(l)
            U = len(units)

            def score(u):
                h, q, nk = units[u]
                if u >= 2:
                    pe.wait_ge(mla["ex"], l * MLA["ex"] + u - 1)
                nc.tensor.matmul(ps[6 + u % 2][:, 0:nk * P], qT[:, h, q * P:(q + 1) * P], kT[:, h, 0:nk * P],
                                              start=True, stop=True).then_inc(mla["s"], 1)

            def flip(u):
                h, q, nk = units[u]
                pe.wait_ge(mla["pn"], l * MLA["pn"] + u + 1)
                if u >= 2:
                    pe.wait_ge(mla["pte"], l * MLA["pte"] + u - 1)
                for k in range(nk):
                    last = nc.tensor.transpose(ps[3 + u % 2][:, k * P:(k + 1) * P], Pb[:, u % 2, k * P:(k + 1) * P], ident)
                last.then_inc(mla["t"], 1)

            def weigh(u):
                h, q, nk = units[u]
                pe.wait_ge(mla["pte"], l * MLA["pte"] + u + 1)
                if h % 2 == 0 and h >= 4 and q == units[0][1]:
                    pe.wait_ge(mla["oe"], l * MLA["oe"] + h // 2 - 1)
                for k in range(nk):
                    last = nc.tensor.matmul(ps[h // 2 % 2][64 * (h % 2):64 * (h % 2) + 64, q * P:(q + 1) * P],
                                            vtok[:, k, h * DV:(h + 1) * DV], PT[:, u % 2, k * P:(k + 1) * P],
                                            start=(k == 0), stop=(k == nk - 1))
                last.then_inc(mla["o"], 1)

            score(0)
            for u in range(U):
                if u + 1 < U:
                    score(u + 1)
                flip(u)
                if u >= 1:
                    weigh(u - 1)
            weigh(U - 1)

        def mla_act(act, ch, l):
            for j in range(5):
                act.wait_ge(mla["z"], l * MLA["z"] + j + 1)
                ch.add(nc.scalar.activation(Z[:, j, :], ps[j][:, :], ACT.Copy))
                nc.scalar.activation(ZSQ[:, j, :], ps[j][:, :], ACT.Square).then_inc(mla["zev"], 1)
            act.wait_ge(mla["kr"], l * MLA["kr"] + 1)
            nc.scalar.activation(kT[64:128, :, :], bcast(ps[5][64:128, :], 1, HEADS), ACT.Copy).then_inc(mla["krc"], 1)
            for g, n in enumerate((QL, KVL)):
                act.wait_ge(mla["ss"], l * MLA["ss"] + g + 1)
                ch.link(nc.scalar.activation(RSL[:, g, :], ps[6 + g][:, :], ACT.Ln, scale=1.0 / n, bias=cn("eps", 1)))
                nc.scalar.activation(RSL[:, g, :], RSL[:, g, :], ACT.Exp, scale=-0.5).then_inc(mla["rs"], 1)
            for j in range(8, 20):
                act.wait_ge(mla["p"], l * MLA["p"] + j + 1)
                if j < 16:
                    nc.scalar.activation(kT[0:64, j - 8, :], ps[j % 5][0:64, :], ACT.Copy).then_inc(mla["kve"], 1)
                else:
                    nc.scalar.activation(vtok[:, j - 16, :], ps[j % 5][:, :], ACT.Copy).then_inc(mla["kve"], 1)
            units = units_mla(l)
            U = len(units)

            def copy_flipped(u):
                nk = units[u][2]
                act.wait_ge(mla["t"], l * MLA["t"] + u + 1)
                if u >= 2:
                    act.wait_ge(mla["o"], l * MLA["o"] + u - 1)
                nc.scalar.activation(PT[:, u % 2, 0:nk * P], ps[3 + u % 2][:, 0:nk * P], ACT.Copy).then_inc(mla["pte"], 1)

            for u in range(U):
                nk = units[u][2]
                act.wait_ge(mla["nm"], l * MLA["nm"] + u + 1)
                if u >= 2:
                    act.wait_ge(mla["t"], l * MLA["t"] + u - 1)
                nc.scalar.activation(Pb[:, u % 2, 0:nk * P], ps[6 + u % 2][:, 0:nk * P], ACT.Exp,
                                                   bias=st_nm[:, u:u + 1], accum_out=st_sum[:, u:u + 1]).then_inc(mla["ex"], 1)
                if u >= 1:
                    copy_flipped(u - 1)
            copy_flipped(U - 1)

        def mla_dve(dve, ch, l):
            dve.wait_ge(mla["z"], l * MLA["z"] + 6)
            nc.vector.tensor_tensor(KP[0:64, :], ps[5][0:64, :], cn("cs", T)[0:64, :], ALU.mult).then_inc(mla["kp"], 1)
            for j in range(5):
                g, col = (0, sm("g_cq", j)) if j < 3 else (1, sm("g_ckv", j - 3))
                dve.wait_ge(mla["rs"], l * MLA["rs"] + g + 1)
                nc.vector.scalar_tensor_tensor(Z[:, j, :], Z[:, j, :], col, RSL[:, g, :], ALU.mult, ALU.mult).then_inc(mla["zn"], 1)
            for h in range(HEADS):
                dve.wait_ge(mla["p"], l * MLA["p"] + h + 1)
                ch.add(nc.vector.tensor_scalar(qT[0:64, h, :], ps[h % 5][0:64, :], ATT_SCALE, None, ALU.mult))
                nc.vector.scalar_tensor_tensor(qT[64:128, h, :], ps[h % 5][64:128, :], ATT_SCALE,
                                                             cn("cs", T)[64:128, :], ALU.mult, ALU.mult).then_inc(mla["qe"], 1)
            units = units_mla(l)
            U, per = len(units), len(units) // 4

            def normalise(u):
                nk = units[u][2]
                dve.wait_ge(mla["ex"], l * MLA["ex"] + u + 1)
                ch.link(nc.vector.reciprocal(st_rec[:, u:u + 1], st_sum[:, u:u + 1]))
                nc.vector.tensor_scalar(Pb[:, u % 2, 0:nk * P], Pb[:, u % 2, 0:nk * P], st_rec[:, u:u + 1], None, ALU.mult).then_inc(mla["pn"], 1)

            def pair_out(j):
                c0 = units[0][1] * P
                dve.wait_ge(mla["o"], l * MLA["o"] + per * (j + 1))
                nc.vector.tensor_copy(BR[:, j, c0:], ps[j % 2][:, c0:]).then_inc(mla["oe"], 1)

            for u in range(U):
                nk = units[u][2]
                dve.wait_ge(mla["s"], l * MLA["s"] + u + 1)
                nc.vector.tensor_reduce(st_nm[:, u:u + 1], ps[6 + u % 2][:, 0:nk * P], AX_X, ALU.max, negate=True).then_inc(mla["nm"], 1)
                if u >= 1:
                    normalise(u - 1)
                if u >= per + 2 and (u - 2) % per == 0:
                    pair_out((u - 2) // per - 1)
            normalise(U - 1)
            pair_out(3)

        zq, zk, zv, so = arena(0, T), arena(512, T), arena(1024, 2, T), arena(2048, 2, T)
        gI, gF, g1, g2_, gB, gA, gM = (arena(3072 + 512 * i, T) for i in range(7))
        gOne = arena(6656, T)
        RT = arena(7168, 3, T)
        acol = arena(8704, TT, 64)
        VA = arena(8960, TT, MLH, P)
        EbS, MbS = arena(11008, 2, T), arena(17408, 2, T)
        Db, Sb, dtmp = arena(12032, 2, T), arena(13056, 2, T), arena(14080, 2, P)
        hd = arena(14336, 2, 2 * T)
        rec_, dn = arena(16384, T), arena(16896, T)
        ml, ML = signals("ml", z=7, zev=6, ab=1, ln=1, mb_in=1, e=2, rt=1, at=1, vt=1, ac=1, vev=1, mb=8,
                                                    eb=8, ebs=8, mbs=8, qk=36, dg=32, d=36, s=36, pv=36, h=8, hs=1, sq=1, ss=2, rs=2,
                                                    out=2)

        def pieces_ml(l):
            c0 = 0 if l == 0 else TC
            out_ = []
            for u in range(2 * MLH):
                if u < MLH:
                    per = [(s, s * P, T, s * P) for s in range(TT)]
                else:
                    per = [(1, 0, T, 128), (0, 0, 128, 0), (0, 256, 512, None), (3, 256, 512, 384), (2, 256, 384, 256)]
                for s, j0, j1, dg in per:
                    j0 = max(j0, c0)
                    dg = None if dg is not None and dg < c0 else dg
                    if j0 < j1:
                        out_.append((u, s, j0, j1, dg))
            return out_

        def ml_pe(pe, l):
            pe.wait_ge(mla["oe"], l * MLA["oe"] + 4)
            for j in range(7):
                n = CH_ML + j // 4
                if j % 4 == 0:
                    wait_chunk(pe, l, n)
                project(pe, ps[j][:, :], cols(n, KD), (j % 4) * P, P).then_inc(ml["z"], 1)
            pe.wait_ge(ml["zev"], l * ML["zev"] + 6)
            for i in range(2):
                for t in range(TT):
                    last = nc.tensor.transpose(ps[1 + i][:, t * P:(t + 1) * P], zv[:, i, t * P:(t + 1) * P], ident)
            last.then_inc(ml["vt"], 1)
            pe.wait_ge(ml["rt"], l * ML["rt"] + 1)
            for t in range(TT):
                last = nc.tensor.transpose(ps[0][:, t * 64:(t + 1) * 64], RT[0:64, 0, t * P:(t + 1) * P], ident[0:64, 0:64])
            last.then_inc(ml["at"], 1)
            pe.wait_ge(ml["vev"], l * ML["vev"] + 1)
            pe.wait_ge(ml["ac"], l * ML["ac"] + 1)
            pe.wait_ge(ml["e"], l * ML["e"] + 2)
            pcs = pieces_ml(l)
            N = len(pcs)
            firsts = [p for p in range(N) if p == 0 or pcs[p][0] != pcs[p - 1][0]]

            def rows(u):
                if u >= 2:
                    pe.wait_ge(ml["mbs"], l * ML["mbs"] + u - 1)
                r = u
                nc.tensor.matmul(ps[u % 2][:, :], cn("sel", P, r * P)[0:64, :], RT[0:64, 1, :], start=True, stop=True).then_inc(ml["mb"], 1)
                if u >= 1:
                    pe.wait_ge(ml["ebs"], l * ML["ebs"] + u)
                nc.tensor.matmul(ps[2][:, :], cn("sel", P, r * P)[0:64, :], RT[0:64, 2, :], start=True, stop=True).then_inc(ml["eb"], 1)

            def qk(p):
                u, s, j0, j1, dg = pcs[p]
                if p in firsts:
                    rows(u)
                h = u % MLH
                if p >= 3:
                    pe.wait_ge(ml["s"], l * ML["s"] + p - 2)
                q = slice(32 * h, 32 * h + 32)
                nc.tensor.matmul(ps[3 + p % 3][:, j0:j1], zk[q, s * P:(s + 1) * P], zq[q, j0:j1],
                                              start=True, stop=True, tile_position=(32 * h, 0)).then_inc(ml["qk"], 1)

            def pv(p):
                u, s, j0, j1, dg = pcs[p]
                pe.wait_ge(ml["s"], l * ML["s"] + p + 1)
                if p in firsts and u >= 2:
                    pe.wait_ge(ml["h"], l * ML["h"] + u - 1)
                nc.tensor.matmul(ps[6 + u % 2][:, j0:j1], VA[:, s, u % MLH, :], Sb[:, p % 2, j0:j1],
                                              start=(p in firsts), stop=(p + 1 in firsts or p == N - 1)).then_inc(ml["pv"], 1)

            qk(0)
            for p in range(N):
                if p + 1 < N:
                    qk(p + 1)
                pv(p)
            pe.wait_ge(ml["sq"], l * ML["sq"] + 1)
            for i in range(2):
                nc.tensor.matmul(ps[i][:, :], bd, hd[:, 1, i * T:(i + 1) * T], start=True, stop=True).then_inc(ml["ss"], 1)

        def ml_act(act, ch, l):
            for j in range(6):
                act.wait_ge(ml["z"], l * ML["z"] + j + 1)
                dst = (zq, zk, zv[:, 0, :], zv[:, 1, :], so[:, 0, :], so[:, 1, :])[j]
                if j < 4:
                    ins = nc.scalar.activation(dst, ps[j][:, :], ACT.Copy, scale=float(MLQK) ** -0.5 if j == 0 else 1.0)
                else:
                    ins = nc.scalar.activation(dst, ps[j][:, :], ACT.Sigmoid)
                ins.then_inc(ml["zev"], 1)
            act.wait_ge(ml["ab"], l * ML["ab"] + 1)
            ch.link(nc.scalar.activation(g1[0:64, :], gF[0:64, :], ACT.Abs))
            ch.link(nc.scalar.activation(g1[0:64, :], g1[0:64, :], ACT.Exp, scale=-1.0))
            nc.scalar.activation(g1[0:64, :], g1[0:64, :], ACT.Ln, bias=1.0).then_inc(ml["ln"], 1)
            act.wait_ge(ml["mb_in"], l * ML["mb_in"] + 1)
            nc.scalar.activation(RT[0:32, 2, :], g2_[0:32, :], ACT.Exp, scale=-1.0).then_inc(ml["e"], 1)
            nc.scalar.activation(seg(RT[32:64, 2, :]), rev(g2_[32:64, :]), ACT.Exp, scale=-1.0).then_inc(ml["e"], 1)
            act.wait_ge(ml["at"], l * ML["at"] + 1)
            nc.scalar.activation(acol[:, :, :], ps[0][:, 0:256].rearrange("p (t r) -> p t r", r=64), ACT.Copy).then_inc(ml["ac"], 1)
            pcs = pieces_ml(l)
            ndg = 0
            for p, (u, s, j0, j1, dg) in enumerate(pcs):
                if p == 0 or pcs[p - 1][0] != u:
                    act.wait_ge(ml["mb"], l * ML["mb"] + u + 1)
                    nc.scalar.activation(MbS[:, u % 2, :], ps[u % 2][:, :], ACT.Copy).then_inc(ml["mbs"], 1)
                    act.wait_ge(ml["eb"], l * ML["eb"] + u + 1)
                    if u >= 2:
                        act.wait_ge(ml["h"], l * ML["h"] + u - 1)
                    nc.scalar.activation(EbS[:, u % 2, :], ps[2][:, :], ACT.Copy).then_inc(ml["ebs"], 1)
                r = 32 * (u // MLH) + u % MLH
                a = acol[:, s, r:r + 1]
                if p >= 2:
                    act.wait_ge(ml["s"], l * ML["s"] + p - 1)
                if p == 0 or pcs[p - 1][0] != u:
                    act.wait_ge(ml["mbs"], l * ML["mbs"] + u + 1)
                spans = [(j0, j1)] if dg is None else [x for x in ((j0, dg), (dg + P, j1)) if x[0] < x[1]]
                todo = []
                for x0, x1 in spans:
                    todo.append((Db[:, p % 2, x0:x1], MbS[:, u % 2, x0:x1], -1.0))
                if dg is not None:
                    ndg += 1
                    todo.append((Db[:, p % 2, dg:dg + P], dtmp[:, (ndg - 1) % 2, :], 1.0))
                    act.wait_ge(ml["dg"], l * ML["dg"] + ndg)
                for n, (dst, src, sc) in enumerate(todo):
                    ins = nc.scalar.activation(dst, src, ACT.Exp, scale=sc, bias=a)
                    if n == len(todo) - 1:
                        ins.then_inc(ml["d"], 1)
            act.wait_ge(ml["hs"], l * ML["hs"] + 1)
            nc.scalar.activation(hd[:, 1, :], hd[:, 0, :], ACT.Square).then_inc(ml["sq"], 1)
            for i in range(2):
                act.wait_ge(ml["ss"], l * ML["ss"] + i + 1)
                ch.link(nc.scalar.activation(EbS[:, i, :], ps[i][:, :], ACT.Ln, scale=1.0 / 64, bias=cn("eps", 1)))
                nc.scalar.activation(EbS[:, i, :], EbS[:, i, :], ACT.Exp, scale=-0.5).then_inc(ml["rs"], 1)

        def seg(v):
            return v.rearrange("p (s t) -> p s t", s=2)

        def rev(v):
            return seg(v)[:, :, ::-1]

        def ml_dve(dve, ch, l):
            dve.wait_ge(ml["z"], l * ML["z"] + 7)
            b = sm("ml_b")
            ch.add(nc.vector.memset(gOne[0:64, :], 1.0))
            ch.add(nc.vector.memset(VA[:, :, :, 64:128], 1.0))
            ch.add(nc.vector.tensor_scalar(gI[0:32, :], ps[6][0:32, :], b[0:32, :], None, ALU.add))
            ch.add(nc.vector.tensor_scalar(seg(gI[32:64, :]), rev(ps[6][32:64, :]), b[32:64, :], None, ALU.add))
            ch.add(nc.vector.tensor_scalar(gF[0:32, :], ps[6][64:96, :], b[64:96, :], None, ALU.add))
            nc.vector.tensor_scalar(seg(gF[32:64, :]), rev(ps[6][96:128, :]), b[96:128, :], None, ALU.add).then_inc(ml["ab"], 1)
            dve.wait_ge(ml["vt"], l * ML["vt"] + 1)
            for i in range(2):
                last = nc.vector.tensor_copy(VA[:, :, 2 * i:2 * i + 2, 0:64], ps[1 + i][:, :].rearrange("p (t h v) -> p t h v", t=TT, h=2))
                if i == 1:
                    last.then_inc(ml["vev"], 1)
            dve.wait_ge(ml["ln"], l * ML["ln"] + 1)
            ch.link(nc.vector.scalar_tensor_tensor(g2_[0:64, :], gF[0:64, :], 0.0, g1[0:64, :], ALU.min, ALU.subtract))
            ch.link(nc.vector.tensor_tensor_scan(out=gB[0:64, :], data0=gOne[0:64, :], data1=g2_[0:64, :], initial=0.0, op0=ALU.mult, op1=ALU.add))
            ch.link(nc.vector.tensor_tensor(gA[0:64, :], gI[0:64, :], gB[0:64, :], ALU.subtract))
            ch.link(nc.vector.tensor_tensor_scan(out=gM[0:64, :], data0=gA[0:64, :], data1=gA[0:64, :], initial=0.0, op0=ALU.max, op1=ALU.max))
            nc.vector.tensor_tensor(g2_[0:64, :], gM[0:64, :], gB[0:64, :], ALU.add).then_inc(ml["mb_in"], 1)
            for v, src in ((0, gA), (1, gM)):
                ch.add(nc.vector.tensor_copy(RT[0:32, v, :], src[0:32, :]))
                last = nc.vector.tensor_copy(seg(RT[32:64, v, :]), rev(src[32:64, :]))
                if v == 0:
                    ch.add(last)
                else:
                    last.then_inc(ml["rt"], 1)
            pcs = pieces_ml(l)
            N = len(pcs)
            lasts = {p: pcs[p][0] for p in range(N) if p == N - 1 or pcs[p][0] != pcs[p + 1][0]}
            dgs = [0]

            def diagonal(p):
                u, s, j0, j1, dg = pcs[p]
                if dg is None:
                    return
                dve.wait_ge(ml["mbs"], l * ML["mbs"] + u + 1)
                if dgs[0] >= 2:
                    back = [x for x in range(p) if pcs[x][4] is not None][-2]
                    dve.wait_ge(ml["d"], l * ML["d"] + back + 1)
                nc.vector.scalar_tensor_tensor(dtmp[:, dgs[0] % 2, :], MbS[:, u % 2, dg:dg + P], -1.0,
                                                            cn("mlmask", P, P * (u // MLH)), ALU.mult, ALU.add).then_inc(ml["dg"], 1)
                dgs[0] += 1

            def finish(u):
                c0 = 0 if l == 0 else TC
                d, h = divmod(u, MLH)
                dve.wait_ge(ml["pv"], l * ML["pv"] + ([p for p in lasts if lasts[p] == u][0] + 1))
                dve.wait_ge(ml["ebs"], l * ML["ebs"] + u + 1)
                ch.link(nc.vector.scalar_tensor_tensor(dn[64:128, c0:], ps[6 + u % 2][64:128, c0:], -1.0, EbS[64:128, u % 2, c0:],
                                                       ALU.mult, ALU.max))
                ch.link(nc.vector.tensor_tensor(dn[64:128, c0:], ps[6 + u % 2][64:128, c0:], dn[64:128, c0:], ALU.max))
                ch.link(nc.vector.reciprocal(rec_[0:64, c0:], dn[64:128, c0:]))
                nc.vector.tensor_tensor(hd[64 * (h % 2):64 * (h % 2) + 64, d, (h // 2) * T + c0:(h // 2 + 1) * T],
                                                    ps[6 + u % 2][0:64, c0:], rec_[0:64, c0:], ALU.mult).then_inc(ml["h"], 1)

            if l == 0:
                pass
            else:
                ch.add(nc.vector.memset(hd[:, :, :], 0.0))
                ch.settle()
            diagonal(0)
            for p in range(N):
                if p + 1 < N:
                    diagonal(p + 1)
                u, s, j0, j1, dg = pcs[p]
                dve.wait_ge(ml["d"], l * ML["d"] + p + 1)
                dve.wait_ge(ml["qk"], l * ML["qk"] + p + 1)
                if p >= 2:
                    dve.wait_ge(ml["pv"], l * ML["pv"] + p - 1)
                nc.vector.tensor_tensor(Sb[:, p % 2, j0:j1], ps[3 + p % 3][:, j0:j1], Db[:, p % 2, j0:j1], ALU.mult).then_inc(ml["s"], 1)
                if p - 2 in lasts:
                    finish(lasts[p - 2])
            for p in (N - 2, N - 1):
                if p in lasts:
                    finish(lasts[p])
            dve.wait_ge(ml["h"], l * ML["h"] + 8)
            nc.vector.tensor_tensor(hd[:, 0, :], hd[:, 0, :], hd[:, 1, :], ALU.add).then_inc(ml["hs"], 1)
            for i in range(2):
                dve.wait_ge(ml["rs"], l * ML["rs"] + i + 1)
                ch.link(nc.vector.scalar_tensor_tensor(hd[:, 0, i * T:(i + 1) * T], hd[:, 0, i * T:(i + 1) * T], sm("ml_g", i),
                                                       EbS[:, i, :], ALU.mult, ALU.mult))
                nc.vector.tensor_tensor(BR[:, 4 + i, :], hd[:, 0, i * T:(i + 1) * T], so[:, i, :], ALU.mult).then_inc(ml["out"], 1)

        Zs = arena(0, 9, T)
        ZP = arena(4608, 2, 2 * 258)
        tsh = arena(5640, T)
        KK, KDS, YA = arena(6152, 2, T), arena(7176, 2, T), arena(8200, 2, T)
        sgm, Gc, Gp, ex1, ex2, ex3, aa = (arena(9224 + 512 * i, T) for i in range(7))
        NL, ZT, X, XT = sgm, Gc, Gp, ex1
        AR = arena(12808, NC, P)
        beta, kappa = arena(13832, T), arena(14344, T)
        VT, BT, KT = (arena(14856 + 512 * i, NC, 64) for i in range(3))
        MB, MK = arena(16392, NC, P), arena(17416, NC, P)
        ST, RH, UU = arena(4608, 2, 64), arena(4736, 2, 64), arena(4864, 2, 64)
        hmu, omu = arena(18440, 9), arena(18449, 9)
        rw, RW = signals("rw", z=9, zev=9, sh=9, tl=2, kk=1, kq=1, kn=1, kl=1, kf=1, lr=8, sg=8, gc=4, ex=12,
                                                    prep=4, tok=4, tokc=12, sc=16, msk=16, nl=24, pad=1, kx=1, yd=2, zt=24, ztc=24, xu=24, xd=24,
                                                    rh=32, rhc=32, uu=32, uc=32, sn=32, snc=32, y=4, yc=4,
                                                    bo=1, bs=2, bc=2, ym=2, yq=2, ys=2, yr=2, g=2, out=2)
        DEC = float(np.exp(-0.5))
        UNITS = [(d, pr) for d in range(2) for pr in range(2)]
        ORDER = [list(range(NC)), list(range(NC // 2 - 1, -1, -1)) + list(range(NC - 1, NC // 2 - 1, -1))]

        def each_head():
            return (slice(0, 64), slice(64, 128))

        def rw_pe(pe, l):
            pe.wait_ge(ml["out"], l * ML["out"] + 2)
            for j in range(9):
                n = CH_RW + j // 4
                if j % 4 == 0:
                    wait_chunk(pe, l, n)
                if j >= 4:
                    pe.wait_ge(rw["zev"], l * RW["zev"] + j - 3)
                project(pe, ps[j % 4][:, :], cols(n, KD), (j % 4) * P, P).then_inc(rw["z"], 1)
            pe.wait_ge(rw["kq"], l * RW["kq"] + 1)
            for i in range(2):
                last = nc.tensor.matmul(ps[4 + i][:, :], bd, YA[:, i, :], start=True, stop=True)
            last.then_inc(rw["kn"], 1)
            pe.wait_ge(rw["tl"], l * RW["tl"] + 2)
            pe.wait_ge(rw["kf"], l * RW["kf"] + 1)
            for n, (d, pr) in enumerate(UNITS):
                hd_ = slice(64 * d, 64 * d + 64)
                for i, (o, z) in enumerate(((WS_W2, 6), (WS_A2, 7))):
                    nc.tensor.matmul(ps[i][:, :], WS[hd_, o + pr * P:o + (pr + 1) * P], Zs[hd_, z, :], start=True, stop=True).then_inc(rw["lr"], 1)
                pe.wait_ge(rw["prep"], l * RW["prep"] + n + 1)
                for b, src in enumerate((Zs[:, 4 + pr, :], beta, kappa)):
                    for c in range(NC):
                        for h in each_head():
                            last = nc.tensor.matmul(ps[2 + b][h, c * C:(c + 1) * C], src[h, c * C:(c + 1) * C], ident[h, h],
                                                    start=True, stop=True)
                last.then_inc(rw["tok"], 1)
                banks = (5, 6, 7, 0)
                for g in range(4):
                    src = beta if g < 2 else kappa
                    for c in range(4 * (g % 2), 4 * (g % 2) + 4):
                        for h in each_head():
                            last = nc.tensor.matmul(ps[banks[g]][h, (c % 4) * P:(c % 4 + 1) * P], src[h, c * C:(c + 1) * C],
                                                    AR[h, c, :], start=True, stop=True)
                    last.then_inc(rw["sc"], 1)
                pe.wait_ge(rw["msk"], l * RW["msk"] + 4 * n + 4)
                pe.wait_ge(rw["tokc"], l * RW["tokc"] + 3 * n + 3)
                for v in range(6):
                    pe.wait_ge(rw["nl"], l * RW["nl"] + 6 * n + v + 1)
                    for c in range(NC):
                        for h in each_head():
                            last = nc.tensor.matmul(ps[1][h, c * C:(c + 1) * C], NL[h, c * C:(c + 1) * C], XT[h, c * C:(c + 1) * C],
                                                    start=True, stop=True)
                    last.then_inc(rw["zt"], 1)
                    pe.wait_ge(rw["ztc"], l * RW["ztc"] + 6 * n + v + 1)
                    for c in range(NC):
                        for h in each_head():
                            cc = slice(c * C, (c + 1) * C)
                            last = nc.tensor.matmul(ps[2][h, cc], ZT[h, cc], X[h, cc], start=True, stop=True)
                            if v < 5:
                                last = nc.tensor.matmul(ps[3][h, cc], X[h, cc], ZT[h, cc], start=True, stop=True)
                    last.then_inc(rw["xu"], 1)
                pe.wait_ge(rw["xd"], l * RW["xd"] + 6 * n + 6)
                for i, c in enumerate(ORDER[d]):
                    q = 8 * n + i
                    S0, S1 = ST[:, i % 2, :], ST[:, (i + 1) % 2, :]
                    cc = slice(c * C, (c + 1) * C)
                    if i:
                        pe.wait_ge(rw["snc"], l * RW["snc"] + q)
                    for h in each_head():
                        nc.tensor.matmul(ps[4][h, 0:64], MK[h, c, 0:64], VT[h, c, :], start=True, stop=False)
                        last = nc.tensor.matmul(ps[4][h, 0:64], AR[h, c, 0:64], S0[h, :], start=False, stop=True)
                    last.then_inc(rw["rh"], 1)
                    pe.wait_ge(rw["rhc"], l * RW["rhc"] + q + 1)
                    for h in each_head():
                        last = nc.tensor.matmul(ps[5][h, 0:64], X[h, cc], RH[h, i % 2, :], start=True, stop=True)
                    last.then_inc(rw["uu"], 1)
                    for h in each_head():
                        nc.tensor.matmul(ps[6][h, 0:64], ident[h, h], S0[h, :], start=True, stop=False)
                        nc.tensor.matmul(ps[6][h, 0:64], KT[h, c, :], VT[h, c, :], start=False, stop=False)
                        if h.start == 0:
                            pe.wait_ge(rw["uc"], l * RW["uc"] + q + 1)
                        last = nc.tensor.matmul(ps[6][h, 0:64], BT[h, c, :], UU[h, i % 2, :], start=False, stop=True)
                    last.then_inc(rw["sn"], 1)
                    for h in each_head():
                        nc.tensor.matmul(ps[7][h, cc], S0[h, :], AR[h, c, 64:128], start=True, stop=False)
                        nc.tensor.matmul(ps[7][h, cc], VT[h, c, :], MK[h, c, 64:128], start=False, stop=False)
                        last = nc.tensor.matmul(ps[7][h, cc], UU[h, i % 2, :], MB[h, c, 64:128], start=False, stop=True)
                    if i == NC - 1:
                        last.then_inc(rw["y"], 1)
            pe.wait_ge(rw["yc"], l * RW["yc"] + 4)
            pe.wait_ge(rw["snc"], l * RW["snc"] + 32)
            pe.wait_ge(rw["bo"], l * RW["bo"] + 1)
            for pr in range(2):
                nc.tensor.matmul(ps[pr][:, :], bd, KDS[:, pr, :], start=True, stop=True).then_inc(rw["bs"], 1)
            for pr in range(2):
                last = nc.tensor.matmul(ps[2 + pr][:, :], bd, YA[:, pr, :], start=True, stop=True)
                last.then_inc(rw["ym"], 1)
            for pr in range(2):
                nc.tensor.matmul(ps[6 + pr][:, :], WS[:, WS_G2 + pr * P:WS_G2 + (pr + 1) * P], Zs[:, 8, :], start=True, stop=True).then_inc(rw["g"], 1)
            for pr in range(2):
                pe.wait_ge(rw["yq"], l * RW["yq"] + pr + 1)
                nc.tensor.matmul(ps[4 + pr][:, :], bd, sq_[pr], start=True, stop=True).then_inc(rw["ys"], 1)

        sq_ = (beta, kappa)

        def rw_act(act, ch, l):
            for j in range(9):
                act.wait_ge(rw["z"], l * RW["z"] + j + 1)
                if j >= 2:
                    act.wait_ge(rw["sh"], l * RW["sh"] + j - 1)
                if j == 0:
                    act.wait_ge(rw["pad"], l * RW["pad"] + 1)
                dst = ZP[:, j % 2, :].rearrange("p (s t) -> p s t", s=2)[:, :, 1:257]
                nc.scalar.activation(dst, ps[j % 4][:, :].rearrange("p (s t) -> p s t", s=2), ACT.Copy).then_inc(rw["zev"], 1)
            act.wait_ge(rw["sh"], l * RW["sh"] + 9)
            nc.scalar.activation(Zs[:, 6, :], Zs[:, 6, :], ACT.Tanh).then_inc(rw["tl"], 1)
            nc.scalar.activation(Zs[:, 8, :], Zs[:, 8, :], ACT.Sigmoid).then_inc(rw["tl"], 1)
            act.wait_ge(rw["kk"], l * RW["kk"] + 1)
            nc.scalar.activation(YA[:, :, :], KK[:, :, :], ACT.Square).then_inc(rw["kq"], 1)
            act.wait_ge(rw["kl"], l * RW["kl"] + 1)
            ch.link(nc.scalar.activation(KDS[:, :, :], KDS[:, :, :], ACT.Ln))
            nc.scalar.activation(KDS[:, :, :], KDS[:, :, :], ACT.Exp, scale=-0.5).then_inc(rw["kx"], 1)
            for n, (d, pr) in enumerate(UNITS):
                if n:
                    act.wait_ge(rw["y"], l * RW["y"] + n)
                act.wait_ge(rw["lr"], l * RW["lr"] + 2 * n + 1)
                nc.scalar.activation(sgm, ps[0][:, :], ACT.Sigmoid, bias=sm("w0", 2 * d + pr)).then_inc(rw["sg"], 1)
                act.wait_ge(rw["lr"], l * RW["lr"] + 2 * n + 2)
                nc.scalar.activation(aa, ps[1][:, :], ACT.Sigmoid, bias=sm("a0", 2 * d + pr)).then_inc(rw["sg"], 1)
                act.wait_ge(rw["gc"], l * RW["gc"] + n + 1)
                nc.scalar.activation(ex1, Gp, ACT.Exp, scale=-DEC).then_inc(rw["ex"], 1)
                nc.scalar.activation(ex2, Gc, ACT.Exp, scale=DEC).then_inc(rw["ex"], 1)
                nc.scalar.activation(ex3, Gc, ACT.Exp, scale=-DEC).then_inc(rw["ex"], 1)
                act.wait_ge(rw["tok"], l * RW["tok"] + n + 1)
                for b, dst in enumerate((VT, BT, KT)):
                    nc.scalar.activation(dst[:, :, :], ps[2 + b][:, :].rearrange("p (c f) -> p c f", c=NC), ACT.Copy).then_inc(rw["tokc"], 1)
                for v in range(6):
                    act.wait_ge(rw["zt"], l * RW["zt"] + 6 * n + v + 1)
                    if v > 0 or n > 0:
                        act.wait_ge(rw["xu"], l * RW["xu"] + 6 * n + v)
                    nc.scalar.activation(ZT, ps[1][:, :], ACT.Copy).then_inc(rw["ztc"], 1)
                for i, c in enumerate(ORDER[d]):
                    q = 8 * n + i
                    act.wait_ge(rw["rh"], l * RW["rh"] + q + 1)
                    nc.scalar.activation(RH[:, i % 2, :], ps[4][:, 0:64], ACT.Copy, scale=-1.0).then_inc(rw["rhc"], 1)
                    act.wait_ge(rw["sn"], l * RW["sn"] + q + 1)
                    pl = c * C + (C - 1 if d == 0 else 0)
                    nc.scalar.activation(ST[:, (i + 1) % 2, :], ps[6][:, 0:64], ACT.Copy, scale=ex3[:, pl:pl + 1]).then_inc(rw["snc"], 1)
            for pr in range(2):
                act.wait_ge(rw["yd"], l * RW["yd"] + pr + 1)
                nc.scalar.activation(sq_[pr], YA[:, pr, :], ACT.Square).then_inc(rw["yq"], 1)
            for pr in range(2):
                act.wait_ge(rw["ys"], l * RW["ys"] + pr + 1)
                ch.link(nc.scalar.activation(sq_[pr], ps[4 + pr][:, :], ACT.Ln, scale=1.0 / RN, bias=cn("eps", 1, 1)))
                nc.scalar.activation(sq_[pr], sq_[pr], ACT.Exp, scale=-0.5).then_inc(rw["yr"], 1)

        def rw_dve(dve, ch, l):
            dve.wait_ge(ml["out"], l * ML["out"] + 2)
            ch.add(nc.vector.tensor_scalar(hmu, sm("mu", 0, 9), 0.5, None, ALU.mult))
            ch.link(nc.vector.tensor_scalar(omu, sm("mu", 0, 9), -1.0, 1.0, ALU.mult, ALU.add))
            nc.vector.memset(ZP[:, :, :], 0.0).then_inc(rw["pad"], 1)
            for j in range(9):
                z = ZP[:, j % 2, :].rearrange("p (s t) -> p s t", s=2)
                dve.wait_ge(rw["zev"], l * RW["zev"] + j + 1)
                t = seg(tsh)
                if j:
                    dve.wait_ge(rw["sh"], l * RW["sh"] + j)
                ch.link(nc.vector.tensor_tensor(t, z[:, :, 0:256], z[:, :, 2:258], ALU.add))
                ch.link(nc.vector.tensor_scalar(t, t, hmu[:, j:j + 1], None, ALU.mult))
                nc.vector.scalar_tensor_tensor(seg(Zs[:, j, :]), z[:, :, 1:257], omu[:, j:j + 1], t, ALU.mult, ALU.add).then_inc(rw["sh"], 1)
            dve.wait_ge(rw["sh"], l * RW["sh"] + 9)
            for pr in range(2):
                last = nc.vector.tensor_scalar(KK[:, pr, :], Zs[:, 2 + pr, :], sm("k_k", pr), None, ALU.mult)
                if pr == 0:
                    ch.add(last)
            last.then_inc(rw["kk"], 1)
            dve.wait_ge(rw["kn"], l * RW["kn"] + 1)
            for pr in range(2):
                last = nc.vector.tensor_scalar(KDS[:, pr, :], ps[4 + pr][:, :], 1e-24, None, ALU.max)
                if pr == 0:
                    ch.add(last)
            last.then_inc(rw["kl"], 1)
            dve.wait_ge(rw["kx"], l * RW["kx"] + 1)
            nc.vector.tensor_tensor(KK[:, :, :], KK[:, :, :], KDS[:, :, :], ALU.mult).then_inc(rw["kf"], 1)
            dve.wait_ge(rw["kf"], l * RW["kf"] + 1)
            for n, (d, pr) in enumerate(UNITS):
                step = 1 if d == 0 else -1
                dve.wait_ge(rw["sg"], l * RW["sg"] + 2 * n + 1)
                if n:
                    dve.wait_ge(rw["y"], l * RW["y"] + n)
                ch.link(nc.vector.tensor_tensor_scan(out=Gc[:, ::step], data0=cn("reset", T), data1=sgm[:, ::step], initial=0.0,
                                                     op0=ALU.mult, op1=ALU.add))
                nc.vector.tensor_tensor(Gp, Gc, sgm, ALU.subtract).then_inc(rw["gc"], 1)
                dve.wait_ge(rw["sg"], l * RW["sg"] + 2 * n + 2)
                ch.link(nc.vector.tensor_tensor(beta, KK[:, pr, :], aa, ALU.mult))
                ch.link(nc.vector.tensor_scalar(aa, aa, -1.0, sm("k_a", pr), ALU.add, ALU.mult))
                ch.link(nc.vector.scalar_tensor_tensor(kappa, aa, 1.0, Zs[:, 2 + pr, :], ALU.add, ALU.mult))
                if d == 0:
                    ch.add(nc.vector.tensor_copy(KDS[:, pr, :], kappa))
                else:
                    ch.add(nc.vector.tensor_tensor(KDS[:, pr, :], KDS[:, pr, :], kappa, ALU.add))
                ch.settle()

                def chunks(v):
                    return v.rearrange("p (c t) -> p c t", t=C)
                dve.wait_ge(rw["ex"], l * RW["ex"] + 3 * n + 3)
                ch.add(nc.vector.tensor_tensor(AR[:, :, 0:64], chunks(KK[:, pr, :]), chunks(ex1), ALU.mult))
                ch.add(nc.vector.tensor_tensor(AR[:, :, 64:128], chunks(Zs[:, pr, :]), chunks(ex3), ALU.mult))
                ch.add(nc.vector.tensor_tensor(beta, beta, ex2, ALU.mult))
                ch.add(nc.vector.memset(ST[:, 0, :], 0.0))
                nc.vector.tensor_tensor(kappa, kappa, ex2, ALU.mult).then_inc(rw["prep"], 1)
                dve.wait_ge(rw["prep"], l * RW["prep"] + n + 1)
                for x in (X, XT):
                    for h in each_head():
                        ch.add(nc.vector.tensor_copy(chunks(x)[h, :, :], bcast(ident[h, h], 1, NC)))
                mask = cn("rwmask", P, d * P)
                banks = (5, 6, 7, 0)
                for g in range(4):
                    dve.wait_ge(rw["sc"], l * RW["sc"] + 4 * n + g + 1)
                    dst = (MB if g < 2 else MK)[:, 4 * (g % 2):4 * (g % 2) + 4, :]
                    nc.vector.tensor_tensor(dst, ps[banks[g]][:, :].rearrange("p (c t) -> p c t", c=4),
                                                          bcast(mask, 1, 4), ALU.mult).then_inc(rw["msk"], 1)
                dve.wait_ge(rw["msk"], l * RW["msk"] + 4 * n + 4)
                for v in range(6):
                    if v:
                        dve.wait_ge(rw["zt"], l * RW["zt"] + 6 * n + v)
                    nc.vector.tensor_tensor(chunks(NL), MB[:, :, 0:64], bcast(cn("lev", 64, 64 * v), 1, NC), ALU.mult).then_inc(rw["nl"], 1)
                    dve.wait_ge(rw["xu"], l * RW["xu"] + 6 * n + v + 1)
                    if v < 5:
                        ch.add(nc.vector.tensor_tensor(XT, XT, ps[3][:, :], ALU.subtract))
                    nc.vector.tensor_tensor(X, X, ps[2][:, :], ALU.subtract).then_inc(rw["xd"], 1)
                    dve.wait_ge(rw["xd"], l * RW["xd"] + 6 * n + v + 1)
                for i in range(NC):
                    q = 8 * n + i
                    dve.wait_ge(rw["uu"], l * RW["uu"] + q + 1)
                    nc.vector.tensor_copy(UU[:, i % 2, :], ps[5][:, 0:64]).then_inc(rw["uc"], 1)
                dve.wait_ge(rw["y"], l * RW["y"] + n + 1)
                if d == 0:
                    nc.vector.tensor_copy(YA[:, pr, :], ps[7][:, :]).then_inc(rw["yc"], 1)
                else:
                    nc.vector.tensor_tensor(YA[:, pr, :], YA[:, pr, :], ps[7][:, :], ALU.add).then_inc(rw["yc"], 1)
            dve.wait_ge(rw["yc"], l * RW["yc"] + 4)
            for pr in range(2):
                last = nc.vector.scalar_tensor_tensor(KDS[:, pr, :], Zs[:, pr, :], sm("r_k", pr), KDS[:, pr, :], ALU.mult, ALU.mult)
                if pr == 0:
                    ch.add(last)
            last.then_inc(rw["bo"], 1)
            for pr in range(2):
                dve.wait_ge(rw["bs"], l * RW["bs"] + pr + 1)
                nc.vector.tensor_tensor(KK[:, pr, :], ps[pr][:, :], Zs[:, 4 + pr, :], ALU.mult).then_inc(rw["bc"], 1)
            for pr in range(2):
                dve.wait_ge(rw["ym"], l * RW["ym"] + 2)
                nc.vector.scalar_tensor_tensor(YA[:, pr, :], ps[2 + pr][:, :], -1.0 / RN, YA[:, pr, :], ALU.mult, ALU.add).then_inc(rw["yd"], 1)
            dve.wait_ge(rw["yd"], l * RW["yd"] + 2)
            for pr in range(2):
                dve.wait_ge(rw["yr"], l * RW["yr"] + pr + 1)
                ch.link(nc.vector.scalar_tensor_tensor(YA[:, pr, :], YA[:, pr, :], sm("lnx_w", pr), sq_[pr], ALU.mult, ALU.mult))
                dve.wait_ge(rw["bc"], l * RW["bc"] + 2)
                ch.link(nc.vector.scalar_tensor_tensor(YA[:, pr, :], YA[:, pr, :], sm("lnx_b", pr), KK[:, pr, :], ALU.add, ALU.add))
                dve.wait_ge(rw["g"], l * RW["g"] + pr + 1)
                nc.vector.tensor_tensor(BR[:, 6 + pr, :], YA[:, pr, :], ps[6 + pr][:, :], ALU.mult).then_inc(rw["out"], 1)

        YM = arena(0, KD, T)
        gate = arena(4096, 2, T)
        gprod = arena(5120, 2, T)
        mg, MG = signals("mg", g=24, b=24, sg=24, m=24, o=8, r=8)
        BR_TILES = ((0, 4), (4, 6), (6, 8))

        def mg_pe(pe, l):
            c0 = 0 if l == 0 else TC
            pe.wait_ge(rw["out"], l * RW["out"] + 2)
            for m in range(KD):
                wait_chunk(pe, l, CH_MERGE + m)
                w = chunk(CH_MERGE + m)
                wg = w[:, 0:3072].rearrange("p (k m) -> p k m", k=KD)
                wb = w[:, 3072:4096].rearrange("p (k m) -> p k m", k=KD)
                for i in range(3):
                    n = 3 * m + i
                    if n >= 4:
                        pe.wait_ge(mg["m"], l * MG["m"] + n - 3)
                    for k in range(KD):
                        last = nc.tensor.matmul(ps[2 * (n % 4)][:, c0:], wg[:, k, i * P:(i + 1) * P], H[:, k, c0:],
                                                start=(k == 0), stop=(k == KD - 1))
                    last.then_inc(mg["g"], 1)
                    b0, b1 = BR_TILES[i]
                    for k in range(b0, b1):
                        last = nc.tensor.matmul(ps[2 * (n % 4) + 1][:, c0:], wb[:, k, :], BR[:, k, c0:], start=(k == b0), stop=(k == b1 - 1))
                    last.then_inc(mg["b"], 1)
            pe.wait_ge(mg["m"], l * MG["m"] + 24)
            for m in range(KD):
                if m % 4 == 0:
                    wait_chunk(pe, l, CH_OUT + m // 4)
                w = cols(CH_OUT + m // 4, KD)
                if m >= 4:
                    pe.wait_ge(mg["r"], l * MG["r"] + m - 3)
                for k in range(KD):
                    last = nc.tensor.matmul(ps[m % 4][:, c0:], w[:, k, (m % 4) * P:(m % 4 + 1) * P], YM[:, k, c0:],
                                            start=(k == 0), stop=(k == KD - 1))
                last.then_inc(mg["o"], 1)

        def mg_act(act, l):
            c0 = 0 if l == 0 else TC
            for n in range(24):
                act.wait_ge(mg["g"], l * MG["g"] + n + 1)
                if n == 0:
                    act.wait_ge(rw["out"], l * RW["out"] + 2)
                if n >= 2:
                    act.wait_ge(mg["m"], l * MG["m"] + n - 1)
                nc.scalar.activation(gate[:, n % 2, c0:], ps[2 * (n % 4)][:, c0:], ACT.Sigmoid).then_inc(mg["sg"], 1)

        def mg_dve(dve, ch, l):
            c0 = 0 if l == 0 else TC
            dve.wait_ge(rw["out"], l * RW["out"] + 2)
            for n in range(24):
                m, i = divmod(n, 3)
                dve.wait_ge(mg["sg"], l * MG["sg"] + n + 1)
                dve.wait_ge(mg["b"], l * MG["b"] + n + 1)
                br = ps[2 * (n % 4) + 1][:, c0:]
                if i == 0:
                    nc.vector.tensor_tensor(YM[:, m, c0:], br, gate[:, n % 2, c0:], ALU.mult).then_inc(mg["m"], 1)
                else:
                    if n >= 2:
                        dve.wait_ge(mg["m"], l * MG["m"] + n - 1)
                    ch.link(nc.vector.tensor_tensor(gprod[:, n % 2, c0:], br, gate[:, n % 2, c0:], ALU.mult))
                    dve.wait_ge(mg["m"], l * MG["m"] + n)
                    nc.vector.tensor_tensor(YM[:, m, c0:], YM[:, m, c0:], gprod[:, n % 2, c0:], ALU.add).then_inc(mg["m"], 1)
            for m in range(KD):
                dve.wait_ge(mg["o"], l * MG["o"] + m + 1)
                for half in range(c0 // TC, 2):
                    part = slice(half * TC, (half + 1) * TC)
                    last = nc.vector.scalar_tensor_tensor(R[:, m, part], ps[m % 4][:, part], MOD[:, 16 + m, half:half + 1],
                                                          R[:, m, part], ALU.mult, ALU.add)
                    if half == 1:
                        last.then_inc(mg["r"], 1)
                    else:
                        ch.add(last)

        r_sc, r_bi = arena(8192, TT, E), arena(8448, TT, E)
        r_mx = arena(8704, TT * NG, 8)
        r_gs = arena(8960, TT, NG)
        r_cmp, r_eq = arena(8992, TT, NG * NG), arena(9248, TT, NG * NG)
        r_rank, r_pen = arena(9504, TT, NG), arena(9536, TT, NG)
        r_msk, r_rep = arena(9568, TT, E), arena(9824, TT, E)
        r_top, r_sum, r_rec = arena(10080, TT, 8), arena(10112, TT), arena(10116, TT)
        r_w = arena(10120, TT, E)
        r_wT = arena(10376, T)
        ro, RO = signals("ro", mm=1, sg=1, w=1, t=1, tc=1, st=16)

        def ro_pe(pe, l):
            t0 = 0 if l == 0 else TC // P
            pe.wait_ge(norm["ffn"]["h"], l * NORM["h"] + (2 * KD if l == 0 else KD))
            for t in range(t0, TT):
                for k in range(KD):
                    last = nc.tensor.matmul(ps[0][:, t * E:(t + 1) * E], H[:, k, t * P:(t + 1) * P],
                                            WS[:, WS_RT + k * E:WS_RT + (k + 1) * E], start=(k == 0), stop=(k == KD - 1))
            last.then_inc(ro["mm"], 1)
            pe.wait_ge(ro["w"], l * RO["w"] + 1)
            for t in range(t0, TT):
                last = nc.tensor.transpose(ps[1][0:E, t * P:(t + 1) * P], r_w[:, t, :], ident)
            last.then_inc(ro["t"], 1)

        def ro_act(act, l):
            t0 = 0 if l == 0 else TC // P
            act.wait_ge(ro["mm"], l * RO["mm"] + 1)
            nc.scalar.activation(r_sc[:, t0:, :], ps[0][:, t0 * E:TT * E].rearrange("p (t e) -> p t e", e=E), ACT.Sigmoid).then_inc(ro["sg"], 1)

        def ro_dve(dve, ch, l):
            t0 = 0 if l == 0 else TC // P
            n = TT - t0
            V = nc.vector
            dve.wait_ge(ro["sg"], l * RO["sg"] + 1)
            ch.link(V.tensor_tensor(r_bi[:, t0:, :], r_sc[:, t0:, :], bcast(sm("rb", 0, E), 1, n), ALU.add))
            for t in range(t0, TT):
                for g in range(NG):
                    ch.add(V.max(r_mx[:, t * NG + g, :], r_bi[:, t, g * 8:(g + 1) * 8]))
            ch.settle()
            ch.link(V.tensor_tensor(r_gs[:, t0:, :], r_mx[:, t0 * NG:, 0].rearrange("p (t g) -> p t g", g=NG),
                                    r_mx[:, t0 * NG:, 1].rearrange("p (t g) -> p t g", g=NG), ALU.add))
            for t in range(t0, TT):
                other, own = bcast(r_gs[:, t, :], 1, NG), bcast(r_gs[:, t, :], 2, NG)
                ch.add(V.tensor_tensor(r_cmp[:, t, :].rearrange("p (g o) -> p g o", o=NG), other, own, ALU.is_gt))
                ch.add(V.tensor_tensor(r_eq[:, t, :].rearrange("p (g o) -> p g o", o=NG), other, own, ALU.is_equal))
            ch.settle()
            ch.link(V.tensor_tensor(r_eq[:, t0:, :], r_eq[:, t0:, :], bcast(cn("tri", NG * NG), 1, n), ALU.mult))
            ch.link(V.tensor_tensor(r_cmp[:, t0:, :], r_cmp[:, t0:, :], r_eq[:, t0:, :], ALU.add))
            ch.link(V.tensor_reduce(r_rank[:, t0:, :], r_cmp[:, t0:, :].rearrange("p t (g o) -> p t g o", o=NG), AX_X, ALU.add))
            ch.link(V.tensor_scalar(r_rank[:, t0:, :], r_rank[:, t0:, :], float(TOPG), None, ALU.is_lt))
            ch.link(V.tensor_scalar(r_pen[:, t0:, :], r_rank[:, t0:, :], BIG, -BIG, ALU.mult, ALU.add))

            def wide(v):
                return bcast(v, 2, 8)
            for t in range(t0, TT):
                ch.link(V.tensor_tensor(r_msk[:, t, :].rearrange("p (g o) -> p g o", o=8), r_bi[:, t, :].rearrange("p (g o) -> p g o", o=8),
                                        wide(r_rank[:, t, :]), ALU.mult))
                ch.link(V.tensor_tensor(r_msk[:, t, :].rearrange("p (g o) -> p g o", o=8), r_msk[:, t, :].rearrange("p (g o) -> p g o", o=8),
                                        wide(r_pen[:, t, :]), ALU.add))
                ch.link(V.max(r_top[:, t, :], r_msk[:, t, :]))
                ch.link(V.match_replace(r_rep[:, t, :], r_top[:, t, :], r_msk[:, t, :], -2 * BIG))
            ch.link(V.tensor_tensor(r_w[:, t0:, :], r_rep[:, t0:, :], r_msk[:, t0:, :], ALU.not_equal))
            ch.link(V.tensor_tensor(r_w[:, t0:, :], r_w[:, t0:, :], r_sc[:, t0:, :], ALU.mult))
            ch.link(V.tensor_reduce(r_sum[:, t0:], r_w[:, t0:, :], AX_X, ALU.add))
            ch.link(V.tensor_scalar(r_sum[:, t0:], r_sum[:, t0:], 1e-20, None, ALU.add))
            ch.link(V.reciprocal(r_rec[:, t0:], r_sum[:, t0:]))
            ch.link(V.tensor_scalar(r_rec[:, t0:], r_rec[:, t0:], ROUTED_SCALE, None, ALU.mult))
            V.tensor_tensor(r_w[:, t0:, :], r_w[:, t0:, :], bcast(r_rec[:, t0:], 2, E), ALU.mult).then_inc(ro["w"], 1)
            dve.wait_ge(ro["t"], l * RO["t"] + 1)
            ch.add(V.memset(r_wT[E:E + 1, :], 1.0))
            V.tensor_copy(r_wT[0:E, t0 * P:], ps[1][0:E, t0 * P:]).then_inc(ro["tc"], 1)

        YE = arena(0, KD, T)
        hid = arena(4096, 2, 2 * T)
        sgl = arena(6144, 2, T)
        wb = arena(7168, 2, T)
        NE = E + 1
        expert_in = [sem(f"expert_in{j}") for j in range(2)]
        route_in = [sem(f"route_in{j}") for j in range(2)]
        ex = {n: sem(f"expert_{n}") for n in ("gate_up", "sig", "silu", "silu_up", "hidden", "down", "added")}
        resid2 = sem("resid2")

        def load_expert(sp, l, s, e):
            sp.dma_start(W[:, s * EXPERT:(s + 1) * EXPERT], wexp[l, bass.ds(e, 1), :, :].rearrange("a p n -> p (a n)")).then_inc(expert_in[s], 16)
            c0 = 0 if l == 0 else TC
            sp.dma_start(wb[:, s, c0:], wrows[l, bass.ds(e, 1), c0:].broadcast_to([P, T - c0])).then_inc(route_in[s], 16)

        def ex_sync(sp, l):
            c0 = 0 if l == 0 else TC
            sp.wait_ge(mg["o"], l * MG["o"] + KD)
            sp.wait_ge(ro["tc"], l * RO["tc"] + 1)
            sp.dma_start(wrows[l, :, c0:], r_wT[0:NE, c0:]).then_inc(ro["st"], 16)
            sp.wait_ge(ro["st"], l * RO["st"] + 16)
            o = l * NE

            def replace(n):
                sp.wait_ge(ex["down"], (n - 1 + o) * KD)

            load_expert(sp, l, 1, E)
            load_expert(sp, l, 0, 0)
            with sp.Fori(0, E // 2 - 1) as i:
                replace(i * 2 + 2)
                load_expert(sp, l, 1, i * 2 + 1)
                replace(i * 2 + 3)
                load_expert(sp, l, 0, i * 2 + 2)
            replace(E)
            load_expert(sp, l, 1, E - 1)

        def ex_pe(pe, l):
            c0 = 0 if l == 0 else TC
            o = l * NE

            def gate_up(n, s, use, first=False):
                pe.wait_ge(expert_in[s], use * 16)
                if not first:
                    pe.wait_ge(ex["hidden"], (n + o) * 2)
                w = W[:, s * EXPERT:s * EXPERT + 2 * KD * FE].rearrange("p (k m) -> p k m", k=KD)
                for m in range(2):
                    for up in range(2):
                        for k in range(KD):
                            last = nc.tensor.matmul(ps[2 * up + m][:, c0:], w[:, k, up * FE + m * P:up * FE + (m + 1) * P], H[:, k, c0:],
                                                    start=(k == 0), stop=(k == KD - 1))
                    last.then_inc(ex["gate_up"], 1)

            def down(n, s, first=False):
                pe.wait_ge(ex["hidden"], (n + o + 1) * 2)
                w = W[:, s * EXPERT + 2 * KD * FE:(s + 1) * EXPERT].rearrange("p (k m) -> p k m", k=2)
                for m in range(KD):
                    if m >= 4 or not first:
                        pe.wait_ge(ex["added"], (n + o) * KD + (m - 3))
                    for k in range(2):
                        last = nc.tensor.matmul(ps[4 + m % 4][:, c0:], w[:, k, m * P:(m + 1) * P], hid[:, s, k * T + c0:(k + 1) * T],
                                                start=(k == 0), stop=(k == 1))
                    last.then_inc(ex["down"], 1)

            u0, u1 = l * (NE // 2), l * (NE // 2 + 1)
            gate_up(0, 1, u1 + 1, first=True)
            gate_up(1, 0, u0 + 1)
            down(0, 1, first=True)
            with pe.Fori(0, E // 2 - 1) as i:
                gate_up(i * 2 + 2, 1, i + (u1 + 2))
                down(i * 2 + 1, 0)
                gate_up(i * 2 + 3, 0, i + (u0 + 2))
                down(i * 2 + 2, 1)
            gate_up(E, 1, u1 + NE // 2 + 1)
            down(E - 1, 0)
            down(E, 1)

        def ex_act(act, l):
            c0 = 0 if l == 0 else TC
            o = l * NE

            def sigmoid(n, first=False):
                for m in range(2):
                    act.wait_ge(ex["gate_up"], (n + o) * 2 + (m + 1))
                    if not first:
                        act.wait_ge(ex["hidden"], (n + o) * 2 + (m - 1))
                    nc.scalar.activation(sgl[:, m, c0:], ps[m][:, c0:], ACT.Sigmoid).then_inc(ex["sig"], 1)

            sigmoid(0, first=True)
            with act.Fori(0, E // 2) as i:
                sigmoid(i * 2 + 1)
                sigmoid(i * 2 + 2)

        def ex_dve(dve, ch, l):
            c0 = 0 if l == 0 else TC
            o = l * NE
            V = nc.vector

            def hidden(n, s, use, first=False):
                dve.wait_ge(route_in[s], use * 16)
                if not first:
                    dve.wait_ge(ex["down"], (n + o - 1) * KD)
                for m in range(2):
                    q = (n + o) * 2 + (m + 1)
                    dve.wait_ge(ex["sig"], q)
                    V.tensor_tensor(sgl[:, m, c0:], ps[m][:, c0:], sgl[:, m, c0:], ALU.mult).then_inc(ex["silu"], 1)
                    dve.wait_ge(ex["silu"], q)
                    V.tensor_tensor(sgl[:, m, c0:], ps[2 + m][:, c0:], sgl[:, m, c0:], ALU.mult).then_inc(ex["silu_up"], 1)
                    dve.wait_ge(ex["silu_up"], q)
                    V.tensor_tensor(hid[:, s, m * T + c0:(m + 1) * T], sgl[:, m, c0:], wb[:, s, c0:], ALU.mult).then_inc(ex["hidden"], 1)

            def add(n, first=False):
                for m in range(KD):
                    dve.wait_ge(ex["down"], (n + o) * KD + (m + 1))
                    if first:
                        V.tensor_copy(YE[:, m, c0:], ps[4 + m % 4][:, c0:]).then_inc(ex["added"], 1)
                    else:
                        dve.wait_ge(ex["added"], (n + o - 1) * KD + (m + 1))
                        V.tensor_tensor(YE[:, m, c0:], YE[:, m, c0:], ps[4 + m % 4][:, c0:], ALU.add).then_inc(ex["added"], 1)

            u0, u1 = l * (NE // 2), l * (NE // 2 + 1)
            hidden(0, 1, u1 + 1, first=True)
            hidden(1, 0, u0 + 1, first=True)
            add(0, first=True)
            with dve.Fori(0, E // 2 - 1) as i:
                hidden(i * 2 + 2, 1, i + (u1 + 2))
                add(i * 2 + 1)
                hidden(i * 2 + 3, 0, i + (u0 + 2))
                add(i * 2 + 2)
            hidden(E, 1, u1 + NE // 2 + 1)
            add(E - 1)
            add(E)
            dve.wait_ge(ex["added"], (o + NE) * KD)
            for m in range(KD):
                for half in range(c0 // TC, 2):
                    part = slice(half * TC, (half + 1) * TC)
                    last = V.scalar_tensor_tensor(R[:, m, part], YE[:, m, part], MOD[:, 40 + m, half:half + 1], R[:, m, part], ALU.mult, ALU.add)
                    if half == 0:
                        ch.add(last)
                last.then_inc(resid2, 1)

        XS = arena(0, TT, D)
        OUT = arena(8192, TX // P, D)
        fo = {n: sem(f"out_{n}") for n in ("t", "c", "d")}
        released = ([(mod_mm, N_MOD_CH, j + 1) for j in range(N_MOD_CH)] +
                    [(mla["z"], MLA["z"], 4), (mla["p"], MLA["p"], 20), (mla["p"], MLA["p"], 8), (ml["z"], ML["z"], 4), (ml["z"], ML["z"], 7),
                     (rw["z"], RW["z"], 4), (rw["z"], RW["z"], 8), (rw["z"], RW["z"], 9)] +
                    [(mg["b"], MG["b"], 3 * (m + 1)) for m in range(KD)] + [(mg["o"], MG["o"], 4), (mg["o"], MG["o"], 8)])
        block = es.enter_context(nc.Block())

        @block.sync
        def _(sp):
            sp.dma_start(CT[:, :], consts).then_inc(consts_in, 16)
            sp.dma_start(XS[:, :, :], xin.rearrange("(t p) d -> p t d", p=P)).then_inc(x_in, 16)
            for l in range(L):
                if l:
                    sp.wait_ge(resid2, (l - 1) * KD + KD)
                sp.dma_start(S_[:, :], smalls[l, :, :]).then_inc(smalls_in, 16)
                sp.dma_start(WS[:, :], wsm[l, :, :]).then_inc(smalls_in, 16)
                for j in range(N_CH):
                    if j >= RING:
                        used, per_layer, k = released[j - RING]
                        sp.wait_ge(used, l * per_layer + k)
                    sp.dma_start(chunk(j)[:, 0:CH_COLS[j]], wst[l, j, :, 0:CH_COLS[j]]).then_inc(chunk_in[j % RING], 16)
                ex_sync(sp, l)
            sp.wait_ge(fo["c"], KD)
            sp.dma_start(out.rearrange("(t p) d -> p t d", p=P), OUT[:, :, :]).then_inc(fo["d"], 16)
            sp.wait_ge(fo["d"], 16)

        @block.tensor
        def _(pe):
            pe.wait_ge(consts_in, 16)
            pe.wait_ge(x_in, 16)
            for k in range(KD):
                for t in range(TT):
                    last = nc.tensor.transpose(ps[k][:, t * P:(t + 1) * P], XS[:, t, k * P:(k + 1) * P], ident)
                last.then_inc(xt_pe, 1)
            pe.wait_ge(resid_first, KD)
            for l in range(L):
                pe.wait_ge(smalls_in, l * 32 + 32)
                mod_pe(pe, l)
                norm_pe(pe, l, "mix", 0)
                mla_pe(pe, l)
                ml_pe(pe, l)
                rw_pe(pe, l)
                mg_pe(pe, l)
                norm_pe(pe, l, "ffn", 0 if l == 0 else TC)
                ro_pe(pe, l)
                ex_pe(pe, l)
            norm_pe(pe, 0, "fin", TC)
            for k in range(KD):
                pe.wait_ge(norm["fin"]["n"], k + 1)
                if k >= 4:
                    pe.wait_ge(fo["c"], k - 3)
                for t in range(2):
                    last = nc.tensor.transpose(ps[k % 4][:, t * P:(t + 1) * P], H[:, k, TC + t * P:TC + (t + 1) * P], ident)
                last.then_inc(fo["t"], 1)

        @block.scalar
        def _(act):
            ch = Chain(act, act_sem)
            act.wait_ge(consts_in, 16)
            nc.scalar.activation(COND[:, :, :], cn("cond", 16).rearrange("p (k c) -> p k c", c=2), ACT.Sigmoid).then_inc(silu_done, 1)
            for k in range(0, KD, 2):
                act.wait_ge(xt_pe, k + 1)
                nc.scalar.activation(R[:, k, :], ps[k][:, :], ACT.Copy).then_inc(resid_first, 1)
            act.wait_ge(resid_first, KD)
            for l in range(L):
                if l:
                    act.wait_ge(resid2, (l - 1) * KD + KD)
                norm_act_square(act, l, "mix", 0)
                norm_act_rs(act, ch, l, "mix", 0)
                norm_act_modulate(act, l, "mix", 0)
                mla_act(act, ch, l)
                ml_act(act, ch, l)
                rw_act(act, ch, l)
                mg_act(act, l)
                act.wait_ge(mg["r"], l * MG["r"] + KD)
                c0 = 0 if l == 0 else TC
                norm_act_square(act, l, "ffn", c0)
                norm_act_rs(act, ch, l, "ffn", c0)
                norm_act_modulate(act, l, "ffn", c0)
                ro_act(act, l)
                ex_act(act, l)
            act.wait_ge(resid2, (L - 1) * KD + KD)
            norm_act_square(act, 0, "fin", TC)
            norm_act_rs(act, ch, 0, "fin", TC)

        @block.vector
        def _(dve):
            ch = Chain(dve, dve_sem)
            dve.wait_ge(silu_done, 1)
            nc.vector.tensor_tensor(COND[:, :, :], COND[:, :, :], cn("cond", 16).rearrange("p (k c) -> p k c", c=2), ALU.mult).then_inc(cond_ready, 1)
            for k in range(1, KD, 2):
                dve.wait_ge(xt_pe, k + 1)
                nc.vector.tensor_copy(R[:, k, :], ps[k][:, :]).then_inc(resid_first, 1)
            for l in range(L):
                mod_dve(dve, ch, l)
                norm_dve(dve, l, "mix", 0)
                mla_dve(dve, ch, l)
                ml_dve(dve, ch, l)
                rw_dve(dve, ch, l)
                mg_dve(dve, ch, l)
                norm_dve(dve, l, "ffn", 0 if l == 0 else TC)
                ro_dve(dve, ch, l)
                ex_dve(dve, ch, l)
            dve.wait_ge(norm["fin"]["rs"], 1)
            for k in range(KD):
                nc.vector.scalar_tensor_tensor(H[:, k, TC:], R[:, k, TC:], cn("g_final", 1, k), RS[:, TC:], ALU.mult, ALU.mult).then_inc(norm["fin"]["n"], 1)
            for k in range(KD):
                dve.wait_ge(fo["t"], k + 1)
                nc.vector.tensor_copy(OUT[:, :, k * P:(k + 1) * P], ps[k % 4][:, 0:2 * P].rearrange("p (t m) -> p t m", t=2)).then_inc(fo["c"], 1)


def constants(c, c_ctx, g_final):
    f = np.zeros((P, CN_N), np.float32)

    def put(name, v, r0=0):
        f[r0:r0 + v.shape[0], CN[name]:CN[name] + v.shape[1]] = v
    i = np.arange(P)
    put("ident", np.eye(P, dtype=np.float32))
    put("ones", np.ones((P, P), np.float32))
    put("bd", (i[:, None] // 64 == i[None, :] // 64).astype(np.float32))
    m = np.concatenate([np.where(i[:, None] <= i[None, :], 0, -BIG), np.where(i[:, None] >= i[None, :], 0, -BIG)], 1)
    put("mlmask", m.astype(np.float32))
    s, t = i[:, None] % 64, np.arange(64)[None, :]
    put("rwmask", np.concatenate([s < t, s <= t, s > t, s >= t], 1).astype(np.float32))
    put("lev", np.concatenate([(s // (2 * b) == t // (2 * b)) & (s // b != t // b) for b in (1, 2, 4, 8, 16, 32)], 1).astype(np.float32))
    put("reset", np.tile((np.arange(T) % C != 0).astype(np.float32), (P, 1)))
    n = np.arange(TX)
    half = ROPE // 2
    inv = (np.float32(10000.0) ** (-np.arange(0, half, 2, dtype=np.float32) / half)).astype(np.float32)
    ang = np.stack([(n // 64).astype(np.float32)[:, None] * inv, (n % 64).astype(np.float32)[:, None] * inv], 1)
    cos, sin = np.ones((ROPE, T), np.float32), np.zeros((ROPE, T), np.float32)
    for a in range(2):
        for b in range(2):
            rows = slice(a * 16 + b * 8, a * 16 + b * 8 + 8)
            cos[rows, TC:] = np.cos(ang[:, a, :]).T
            sin[rows, TC:] = np.sin(ang[:, a, :]).T * (1 if b else -1)
    put("cs", np.concatenate([cos, sin, cos, sin], 0))
    sel = np.zeros((64, 8, P), np.float32)
    for u in range(8):
        sel[32 * (u // 4) + u % 4, u, :] = 1
    put("sel", sel.reshape(64, 8 * P))
    put("dup", (i[:64, None] % 32 == i[None, :64] % 32).astype(np.float32))
    g = np.arange(NG)
    put("tri", np.tile((g[None, :] < g[:, None]).astype(np.float32).reshape(1, -1), (P, 1)))
    put("eps", np.tile(np.array([[EPS, RW_EPS]], np.float32), (P, 1)))
    put("cond", np.stack([c_ctx.reshape(KD, P).T, c.reshape(KD, P).T], 2).reshape(P, 16))
    put("g_final", g_final.reshape(KD, P).T)
    return f


def lay_out(q):
    z = np.zeros
    swap = np.arange(ROPE) ^ 8
    smalls, wsm, wst = z((L, P, SM_N), np.float32), z((L, P, WS_N), np.float32), z((L, N_CH, P, CHUNK), np.float32)
    wexp = z((L, E + 1, P, EXPERT), np.float32)

    def tiles(w, m):
        k, n = w.shape[0] // P, w.shape[1] // m
        return w.reshape(k, P, n, m).transpose(2, 1, 0, 3).reshape(n, P, k * m)

    for l in range(L):
        def col(name, v):
            v = np.asarray(v).reshape(-1, P).T
            smalls[l, :, SM[name]:SM[name] + v.shape[1]] = v
        for a, b in (("g_mix", "g_mix"), ("g_ffn", "g_ffn"), ("b_mod", "b_mod"), ("g_cq", "g_cq"), ("g_ckv", "g_ckv"), ("ml_g", "ml_g_norm"),
                     ("mu", "rw_mu"), ("w0", "rw_w0"), ("a0", "rw_a0"), ("k_k", "rw_k_k"), ("k_a", "rw_k_a"), ("r_k", "rw_r_k"),
                     ("lnx_w", "rw_lnx_w"), ("lnx_b", "rw_lnx_b")):
            col(a, q[b][l])
        for r, name in ((0, "ml_b_i"), (64, "ml_b_f")):
            for d in range(2):
                smalls[l, r + 32 * d:r + 32 * d + 4, SM["ml_b"]] = q[name][l, d]
        smalls[l, :, SM["rb"]:SM["rb"] + E] = q["router_bias"][l][None, :]
        wsm[l, :, WS_W2:WS_W2 + 256] = q["rw_w2"][l].reshape(P, 256)
        wsm[l, :, WS_A2:WS_A2 + 256] = q["rw_a2"][l].reshape(P, 256)
        wsm[l, :, WS_G2:WS_G2 + 256] = q["rw_g2"][l]
        wsm[l, :, WS_RT:WS_RT + KD * E] = q["w_router"][l].reshape(KD, P, E).transpose(1, 0, 2).reshape(P, KD * E)
        wst[l, 0:12] = tiles(q["w_mod"][l], 512)
        w = q["w_in"][l]
        rope = w[:, 640:672]
        small = np.concatenate([rope, rope[:, swap], z((D, 64), np.float32)], 1)
        mla = np.concatenate([w[:, 0:640], small], 1)
        wst[l, CH_MLA] = tiles(mla[:, 0:512], 512)[0]
        wst[l, CH_MLA + 1, :, 0:2048] = tiles(mla[:, 512:768], 256)[0]
        wst[l, CH_MLA + 1, :, 2048:3072] = tiles(q["w_uk"][l], 512)[0]
        wst[l, CH_MLA + 1, :, 3072:4096] = tiles(q["w_uv"][l], 512)[0]
        uq = q["w_uq"][l].reshape(QL, HEADS, NOPE + ROPE)
        uq = np.concatenate([uq, uq[:, :, NOPE:][:, :, swap]], 2).reshape(QL, HEADS * P)
        wst[l, CH_UQ, :, 0:3072] = tiles(uq, HEADS * P)[0]
        gates = z((D, P), np.float32)
        for r, c in ((0, 1440), (32, 1444), (64, 1448), (96, 1452)):
            gates[:, r:r + 4] = w[:, c:c + 4]
        mlw = np.concatenate([w[:, 672:1440], gates], 1)
        wst[l, CH_ML] = tiles(mlw[:, 0:512], 512)[0]
        wst[l, CH_ML + 1, :, 0:3072] = tiles(mlw[:, 512:896], 384)[0]
        wst[l, CH_RW:CH_RW + 2] = tiles(w[:, 1456:1456 + 1024], 512)
        wst[l, CH_RW + 2, :, 0:1024] = tiles(w[:, 2480:2608], 128)[0]
        gw = w[:, 2608:].reshape(KD, P, 3, KD, P)
        br = np.concatenate([q["w_br_mla"][l], q["w_br_ml"][l], q["w_br_rw"][l]], 0).reshape(KD, P, KD, P)
        wst[l, CH_MERGE:CH_MERGE + 8, :, 0:3072] = gw.transpose(3, 1, 0, 2, 4).reshape(KD, P, 3072)
        wst[l, CH_MERGE:CH_MERGE + 8, :, 3072:] = br.transpose(2, 1, 0, 3).reshape(KD, P, 1024)
        wst[l, CH_OUT:CH_OUT + 2] = tiles(q["w_out"][l], 512)
        half = 2 * KD * FE
        gu = wexp[l, :, :, 0:half].reshape(E + 1, P, KD, 2, FE)
        for at, names in ((0, ("w_e_gate", "w_s_gate")), (1, ("w_e_up", "w_s_up"))):
            gu[0:E, :, :, at] = q[names[0]][l].reshape(E, KD, P, FE).transpose(0, 2, 1, 3)
            gu[E, :, :, at] = q[names[1]][l].reshape(KD, P, FE).transpose(1, 0, 2)
        dn = np.concatenate([q["w_e_down"][l], q["w_s_down"][l][None]], 0)
        wexp[l, :, :, 0:half] = gu.reshape(E + 1, P, half)
        wexp[l, :, :, half:] = dn.reshape(E + 1, 2, P, D).transpose(0, 2, 1, 3).reshape(E + 1, P, 2 * D)
    x = np.concatenate([q["ctx"][0], q["x"][0]], 0)
    return dict(xin=x, consts=constants(q["c"][0], q["c_ctx"], q["g_final"]), smalls=smalls, wsm=wsm, wst=wst, wexp=wexp)


def kernel(**inputs):
    import concourse.bacc as _bacc
    from concourse.bass_utils import run_bass_kernel_spmd as _run

    arrays = lay_out({k: np.asarray(v) for k, v in inputs.items()})
    nc = _bacc.Bacc("TRN2", target_bir_lowering=False, num_devices=1)
    args = {n: nc.dram_tensor(f"in_{n}", a.shape, mybir.dt.from_np(a.dtype), kind="ExternalInput").ap() for n, a in arrays.items()}
    out = nc.dram_tensor("out_0", (TX, D), F32, kind="ExternalOutput").ap()
    build(nc, out=out, **args)
    r = _run(nc, [{f"in_{n}": a for n, a in arrays.items()}], core_ids=[0])
    return r.results[0]["out_0"].reshape(1, TX, D)
```

```python
from contextlib import ExitStack

import numpy as np

import concourse.bass as bass
from concourse import mybir

ALU = mybir.AluOpType
ACT = mybir.ActivationFunctionType
F32 = mybir.dt.float32
I32 = mybir.dt.int32
AX_X = mybir.AxisListType.X

P = 128
L = 2
D = 1024
KD = D // P
TC = 256
TX = 256
T = TC + TX
TT = T // P
EPS = 1e-6
HEADS, NOPE, ROPE, DV = 8, 64, 32, 64
QL, KVL = 384, 256
ATT_SCALE = float(NOPE + ROPE) ** -0.5
MLH, MLQK = 4, 32
RWH, RN = 4, 64
C = 64
NC = T // C
RW_EPS = 64e-5
E, TOPK, NG, TOPG = 64, 8, 8, 4
FE = 256
ROUTED_SCALE = 2.5
BLOCK = (128, 96)
NOV = 32
NBLK = E + NOV
TOKENS = (T, TX)
ID_N = 2 * (TT * TOPK + NBLK)
BIG = 1e30

RING, CHUNK = 4, 4096
N_MOD_CH = 12
CH_MLA, CH_UQ, CH_ML, CH_RW, CH_MERGE, CH_OUT = 12, 14, 15, 17, 20, 28
N_CH = 30
CH_COLS = [CHUNK] * 12 + [4096, 4096, 3072, 4096, 3072, 4096, 4096, 1024] + [4096] * 10
MOD_FIRST = 4
_late = [[(l, j) for j in range(MOD_FIRST, N_MOD_CH)] + [(l + 1, j) for j in range(MOD_FIRST) if l + 1 < L] for l in range(L)]
MOD_AT = [[v[n * len(v) // 4:(n + 1) * len(v) // 4] for n in range(4)] for v in _late]
ORDER_OF_USE = [[(l, j) for j in range(0 if l == 0 else MOD_FIRST, N_CH) if not MOD_FIRST <= j < N_MOD_CH] for l in range(L)]
for _l in range(L):
    _at = ORDER_OF_USE[_l].index((_l, CH_MERGE))
    ORDER_OF_USE[_l][_at:_at] = _late[_l]
ALL_CHUNKS = sum(ORDER_OF_USE, [])
MOD_CHUNKS = [c for c in ALL_CHUNKS if c[1] < N_MOD_CH]
EXPERT = 2 * KD * FE + 2 * D

WS_W2, WS_A2, WS_G2, WS_RT, WS_N = 0, 256, 512, 768, 1280

SM = {}
_at = 0
for _name, _n in (("g_cq", 3), ("g_ckv", 2), ("ml_b", 1), ("ml_g", 2),
                  ("mu", 9), ("w0", 4), ("a0", 4), ("k_k", 2), ("k_a", 2), ("r_k", 2), ("lnx_w", 2), ("lnx_b", 2),
                  ("rb", 64)):
    SM[_name] = _at
    _at += _n
SM_N = _at

CN = {}
_at = 0
for _name, _n in (("ident", 128), ("ones", 128), ("bd", 128), ("mlmask", 256), ("rwmask", 256), ("lev", 384),
                  ("reset", 512), ("cs", 512), ("sel", 1024), ("dup", 64), ("tri", 64), ("eps", 2), ("cond", 16),
                  ("g_final", 8), ("before", 128), ("e", 64), ("past", 64), ("j", 32),
                  ("b_mod", 48 * L), ("g_norm", 16 * L)):
    CN[_name] = _at
    _at += _n
CN_N = _at


class Chain:

    def __init__(self, eng, sem):
        self.eng, self.sem, self.n = eng, sem, 0

    def add(self, ins):
        self.n += 1
        ins.then_inc(self.sem, 1)

    def settle(self):
        self.eng.wait_ge(self.sem, self.n)

    def link(self, ins):
        self.add(ins)
        self.settle()


def bcast(ap, axis, n):
    a = ap.unsqueeze(axis)
    shape = list(a.shape)
    shape[axis] = n
    return a.broadcast_to(shape)


def build(nc, xin, ids, consts, smalls, wsm, wst, wexp, out):
    es = ExitStack()
    with es:
        def sb(name, shape, dt=F32):
            return es.enter_context(nc.sbuf_tensor(name, shape, dt))

        def sem(name):
            return es.enter_context(nc.semaphore(name))

        def signals(stage, **per_layer):
            return {n: sem(f"{stage}_{n}") for n in per_layer}, per_layer

        R = sb("resid", [P, KD, T])
        H = sb("normed", [P, KD, T])
        BR = sb("branches", [P, KD, T])
        W = sb("ring", [P, RING * CHUNK])
        WS = sb("small_weights", [P, WS_N])
        S_ = sb("smalls", [P, SM_N])
        CT = sb("consts", [P, CN_N])
        MOD = sb("modv", [P, 48, 2])
        AMX = sb("mod_scale", [P, 2, KD, 2])
        COND = sb("condv", [P, KD, 2])
        ARENA = 18560
        A = sb("arena", [P, ARENA])
        ps = [es.enter_context(nc.psum_tensor(f"bank{i}", [P, 512], F32)) for i in range(8)]
        hx = [nc.dram_tensor(f"hidden_rows{l}", (TOKENS[l], D), F32, kind="Internal").ap() for l in range(L)]
        slots = [nc.dram_tensor(f"slots{l}", (P * NBLK, 2), I32, kind="Internal").ap() for l in range(L)]
        yrows = [nc.dram_tensor(f"expert_rows{l}", (TOKENS[l] * TOPK + 2 * P, D), F32, kind="Internal").ap() for l in range(L)]
        WK = sb("choice_weights", [P, TT, TOPK])
        IDS = sb("choice_ids", [P, L, 2 * TT * TOPK], I32)
        IDX = sb("block_slots", [P, NBLK, 2], I32)
        IDG = sb("gather_ids", [P, 2], I32)
        IDY = sb("scatter_ids", [P, 2], I32)
        ADRI = sb("slot_ids", [P, TT * TOPK], I32)
        EJI = sb("block_experts", [P, NBLK], I32)
        BEYOND = sb("groups_beyond", [P, 1], I32)

        def cn(name, n, o=0):
            return CT[:, CN[name] + o:CN[name] + o + n]

        def sm(name, j=0, n=1):
            return S_[:, SM[name] + j:SM[name] + j + n]

        ident, ones, bd = cn("ident", P), cn("ones", P), cn("bd", P)

        def arena(at, *shape):
            n = int(np.prod(shape))
            v = A[:, at:at + n]
            if len(shape) == 2:
                v = v.rearrange("p (a b) -> p a b", b=shape[1])
            if len(shape) == 3:
                v = v.rearrange("p (a b c) -> p a b c", b=shape[1], c=shape[2])
            return v

        def chunk(j):
            return W[:, (j % RING) * CHUNK:(j % RING + 1) * CHUNK]

        consts_in, x_moved = sem("consts_in"), sem("x_in_and_out")
        smalls_in, ids_in = sem("smalls_in"), sem("ids_in")
        chunk_in = [sem(f"chunk_in{j}") for j in range(RING)]
        flipped, flip_copied = sem("flipped"), sem("flip_copied")
        cond_ready = sem("cond_ready")
        mod_mm, mod_row, mod_turned = sem("mod_mm"), sem("mod_row"), sem("mod_turned")
        NORM = dict(sq=KD, mm=1, rs=1, n=KD, h=2 * KD)
        norm = {n: sem(f"norm_{n}") for n in NORM}

        def nth(w, l):
            return {"mix": 2 * l, "ffn": 2 * l + 1, "fin": 2 * L}[w]

        act_sem, dve_sem = sem("act_chain"), sem("dve_chain")

        def wait_chunk(pe, l, j):
            before = [c for c in ALL_CHUNKS[:ALL_CHUNKS.index((l, j))] if c[1] % RING == j % RING]
            pe.wait_ge(chunk_in[j % RING], 16 * (len(before) + 1))

        SQ, RS = arena(0, KD, T), arena(4096, T)

        def norm_act_square(act, l, w, c0):
            for k in range(KD):
                nc.scalar.activation(SQ[:, k, c0:], R[:, k, c0:], ACT.Square).then_inc(norm["sq"], 1)

        def norm_pe(pe, l, w, c0):
            for k in range(KD):
                pe.wait_ge(norm["sq"], nth(w, l) * NORM["sq"] + k + 1)
                last = nc.tensor.matmul(ps[7][:, c0:], ones, SQ[:, k, c0:], start=(k == 0), stop=(k == KD - 1))
            last.then_inc(norm["mm"], 1)

        def norm_act_rs(act, ch, l, w, c0):
            act.wait_ge(norm["mm"], nth(w, l) * NORM["mm"] + 1)
            ch.link(nc.scalar.activation(RS[:, c0:], ps[7][:, c0:], ACT.Ln, scale=1.0 / D, bias=cn("eps", 1)))
            nc.scalar.activation(RS[:, c0:], RS[:, c0:], ACT.Exp, scale=-0.5).then_inc(norm["rs"], 1)

        def norm_dve(dve, l, w, c0):
            dve.wait_ge(norm["rs"], nth(w, l) * NORM["rs"] + 1)
            for k in range(KD):
                nc.vector.tensor_tensor(H[:, k, c0:], R[:, k, c0:], RS[:, c0:], ALU.mult).then_inc(norm["n"], 1)

        def norm_act_modulate(act, l, w, c0):
            v, shift = (0, 0) if w == "mix" else (1, 24)
            for k in range(KD):
                act.wait_ge(norm["n"], nth(w, l) * NORM["n"] + k + 1)
                for half in range(2):
                    if half * TC < c0:
                        continue
                    part = H[:, k, half * TC:(half + 1) * TC]
                    nc.scalar.activation(part, part, ACT.Identity, scale=AMX[:, v, k, half:half + 1],
                                                          bias=MOD[:, shift + k, half:half + 1]).then_inc(norm["h"], 1)

        def project(pe, bank, weights, j0, n):
            for k in range(KD):
                last = nc.tensor.matmul(bank, weights[:, k, j0:j0 + n], H[:, k, :], start=(k == 0), stop=(k == KD - 1))
            return last

        def cols(n, k):
            return chunk(n)[:, 0:CH_COLS[n]].rearrange("p (k m) -> p k m", k=k)

        MROW = [arena(4992, T), arena(5640, T), arena(12296, T), arena(11272, T)]

        def mod_rows(pe, l, j, k, bank):
            if k == 0:
                wait_chunk(pe, l, j)
            w = chunk(j).rearrange("p (k m) -> p k m", k=KD)
            last = nc.tensor.matmul(ps[bank][0:2, :], COND[:, k, :], w[:, k, :], start=(k == 0), stop=(k == KD - 1))
            if k == KD - 1:
                last.then_inc(mod_mm, 1)

        def mod_copy(act, l, j, i, bank):
            act.wait_ge(mod_mm, MOD_CHUNKS.index((l, j)) + 1)
            nc.scalar.activation(MROW[i][0:2, :], ps[bank][0:2, :], ACT.Copy).then_inc(mod_row, 1)

        def mod_turn(pe, chunks, bank):
            for i, (l, j) in enumerate(chunks):
                pe.wait_ge(mod_row, MOD_CHUNKS.index((l, j)) + 1)
                for m in range(4):
                    at = (4 * i + m) * 2
                    last = nc.tensor.matmul(ps[bank][:, at:at + 2], MROW[i][0:2, m * P:(m + 1) * P], ident[0:2, 0:2], start=True, stop=True)
                last.then_inc(mod_turned, 1)

        def mod_dve(dve, ch, chunks, bank):
            dve.wait_ge(mod_turned, MOD_CHUNKS.index(chunks[-1]) + 1)
            for i, (l, j) in enumerate(chunks):
                ch.add(nc.vector.tensor_tensor(MOD[:, 4 * j:4 * j + 4, :], ps[bank][:, 8 * i:8 * i + 8].rearrange("p (m c) -> p m c", c=2),
                                               bcast(cn("b_mod", 4, 48 * l + 4 * j), 2, 2), ALU.add))
            ch.settle()
            for l, j in chunks:
                for v, scale in ((0, 8), (1, 32)):
                    if j == scale // 4 + 1:
                        ch.link(nc.vector.scalar_tensor_tensor(AMX[:, v, :, :], MOD[:, scale:scale + KD, :], 1.0,
                                                               bcast(cn("g_norm", KD, 16 * l + 8 * v), 2, 2), ALU.add, ALU.mult))

        Z, ZSQ = arena(0, 5, T), arena(2560, 5, T)
        KP = arena(5120, T)
        RSL = arena(5632, 2, T)
        qT, kT, vtok = arena(6656, HEADS, T), arena(10752, HEADS, T), arena(14848, TT, HEADS * DV)
        Pb, PT = arena(0, 2, 512), arena(1024, 2, 512)
        st_nm, st_sum, st_rec = arena(16896, 64), arena(16960, 64), arena(17024, 64)
        mla, MLA = signals("mla", z=6, zev=5, kr=3, ss=2, rs=2, zn=5, p=20, qe=8, kve=12,
                                                      s=32, nm=32, ex=32, pn=32, t=32, pte=32, o=32, oe=4)

        def units_mla(l):
            return [(h, q, 2 if q < 2 else 4) for h in range(HEADS) for q in range(4) if l == 0 or q >= 2]

        def mla_pe(pe, l):
            for j in range(6):
                n = CH_MLA + j // 4
                if j % 4 == 0:
                    wait_chunk(pe, l, n)
                w = chunk(n).rearrange("p (k m) -> p k m", k=KD) if j < 4 else \
                    chunk(n)[:, 0:2048].rearrange("p (k m) -> p k m", k=KD)
                for k in range(KD):
                    if j == 0:
                        pe.wait_ge(norm["h"], nth("mix", l) * NORM["h"] + 2 * k + 2)
                    last = nc.tensor.matmul(ps[j][:, :], w[:, k, (j % 4) * P:(j % 4 + 1) * P], H[:, k, :], start=(k == 0), stop=(k == KD - 1))
                last.then_inc(mla["z"], 1)
            pe.wait_ge(mla["kr"], l * MLA["kr"] + 1)
            nc.tensor.matmul(ps[5][64:128, :], cn("dup", 64)[0:64, :], KP[0:64, :], start=True, stop=True).then_inc(mla["kr"], 1)
            for g, (j0, j1) in enumerate(((0, 3), (3, 5))):
                pe.wait_ge(mla["zev"], l * MLA["zev"] + j1)
                for j in range(j0, j1):
                    last = nc.tensor.matmul(ps[6 + g][:, :], ones, ZSQ[:, j, :], start=(j == j0), stop=(j == j1 - 1))
                last.then_inc(mla["ss"], 1)
            pe.wait_ge(mla["zn"], l * MLA["zn"] + 5)
            ukv = chunk(CH_MLA + 1)[:, 2048:4096].rearrange("p (a k m) -> p a k m", a=2, k=2)
            wait_chunk(pe, l, CH_UQ)
            uq = cols(CH_UQ, 3)
            for j in range(20):
                if j >= 13:
                    pe.wait_ge(mla["kve"], l * MLA["kve"] + j - 5 - 7)
                elif j >= 5:
                    pe.wait_ge(mla["qe"], l * MLA["qe"] + j - 4)
                if j < 8:
                    for k in range(3):
                        last = nc.tensor.matmul(ps[j % 5][:, :], uq[:, k, j * P:(j + 1) * P], Z[:, k, :], start=(k == 0), stop=(k == 2))
                elif j < 16:
                    for k in range(2):
                        last = nc.tensor.matmul(ps[j % 5][0:64, :], ukv[:, 0, k, (j - 8) * 64:(j - 7) * 64], Z[:, 3 + k, :],
                                                start=(k == 0), stop=(k == 1))
                else:
                    t = j - 16
                    for k in range(2):
                        last = nc.tensor.matmul(ps[j % 5][:, :], Z[:, 3 + k, t * P:(t + 1) * P], ukv[:, 1, k, :],
                                                start=(k == 0), stop=(k == 1))
                last.then_inc(mla["p"], 1)
            pe.wait_ge(mla["kr"], l * MLA["kr"] + 3)
            pe.wait_ge(mla["kve"], l * MLA["kve"] + 12)
            units = units_mla(l)
            U = len(units)

            def score(u):
                h, q, nk = units[u]
                if u >= 2:
                    pe.wait_ge(mla["ex"], l * MLA["ex"] + u - 1)
                nc.tensor.matmul(ps[6 + u % 2][:, 0:nk * P], qT[:, h, q * P:(q + 1) * P], kT[:, h, 0:nk * P],
                                              start=True, stop=True).then_inc(mla["s"], 1)

            def flip(u):
                h, q, nk = units[u]
                pe.wait_ge(mla["pn"], l * MLA["pn"] + u + 1)
                if u >= 2:
                    pe.wait_ge(mla["pte"], l * MLA["pte"] + u - 1)
                for k in range(nk):
                    last = nc.tensor.transpose(ps[3 + u % 2][:, k * P:(k + 1) * P], Pb[:, u % 2, k * P:(k + 1) * P], ident)
                last.then_inc(mla["t"], 1)

            def weigh(u):
                h, q, nk = units[u]
                pe.wait_ge(mla["pte"], l * MLA["pte"] + u + 1)
                if h % 2 == 0 and h >= 4 and q == units[0][1]:
                    pe.wait_ge(mla["oe"], l * MLA["oe"] + h // 2 - 1)
                for k in range(nk):
                    last = nc.tensor.matmul(ps[h // 2 % 2][64 * (h % 2):64 * (h % 2) + 64, q * P:(q + 1) * P],
                                            vtok[:, k, h * DV:(h + 1) * DV], PT[:, u % 2, k * P:(k + 1) * P],
                                            start=(k == 0), stop=(k == nk - 1))
                last.then_inc(mla["o"], 1)

            score(0)
            for u in range(U):
                if u + 1 < U:
                    score(u + 1)
                flip(u)
                if u >= 1:
                    weigh(u - 1)
            weigh(U - 1)

        def mla_act(act, ch, l):
            for j in range(5):
                act.wait_ge(mla["z"], l * MLA["z"] + j + 1)
                ch.add(nc.scalar.activation(Z[:, j, :], ps[j][:, :], ACT.Copy))
                nc.scalar.activation(ZSQ[:, j, :], ps[j][:, :], ACT.Square).then_inc(mla["zev"], 1)
            act.wait_ge(mla["kr"], l * MLA["kr"] + 2)
            nc.scalar.activation(kT[64:128, :, :], bcast(ps[5][64:128, :], 1, HEADS), ACT.Copy).then_inc(mla["kr"], 1)
            for g, n in enumerate((QL, KVL)):
                act.wait_ge(mla["ss"], l * MLA["ss"] + g + 1)
                ch.link(nc.scalar.activation(RSL[:, g, :], ps[6 + g][:, :], ACT.Ln, scale=1.0 / n, bias=cn("eps", 1)))
                nc.scalar.activation(RSL[:, g, :], RSL[:, g, :], ACT.Exp, scale=-0.5).then_inc(mla["rs"], 1)
            for j in range(8, 20):
                act.wait_ge(mla["p"], l * MLA["p"] + j + 1)
                if j < 16:
                    nc.scalar.activation(kT[0:64, j - 8, :], ps[j % 5][0:64, :], ACT.Copy).then_inc(mla["kve"], 1)
                else:
                    nc.scalar.activation(vtok[:, j - 16, :], ps[j % 5][:, :], ACT.Copy).then_inc(mla["kve"], 1)
            units = units_mla(l)
            U = len(units)

            def copy_flipped(u):
                nk = units[u][2]
                act.wait_ge(mla["t"], l * MLA["t"] + u + 1)
                if u >= 2:
                    act.wait_ge(mla["o"], l * MLA["o"] + u - 1)
                nc.scalar.activation(PT[:, u % 2, 0:nk * P], ps[3 + u % 2][:, 0:nk * P], ACT.Copy).then_inc(mla["pte"], 1)

            for u in range(U):
                nk = units[u][2]
                act.wait_ge(mla["nm"], l * MLA["nm"] + u + 1)
                if u >= 2:
                    act.wait_ge(mla["t"], l * MLA["t"] + u - 1)
                nc.scalar.activation(Pb[:, u % 2, 0:nk * P], ps[6 + u % 2][:, 0:nk * P], ACT.Exp,
                                                   bias=st_nm[:, u:u + 1], accum_out=st_sum[:, u:u + 1]).then_inc(mla["ex"], 1)
                if u >= 1:
                    copy_flipped(u - 1)
            copy_flipped(U - 1)

        def mla_dve(dve, ch, l):
            dve.wait_ge(mla["z"], l * MLA["z"] + 6)
            nc.vector.tensor_tensor(KP[0:64, :], ps[5][0:64, :], cn("cs", T)[0:64, :], ALU.mult).then_inc(mla["kr"], 1)
            for j in range(5):
                g, col = (0, sm("g_cq", j)) if j < 3 else (1, sm("g_ckv", j - 3))
                dve.wait_ge(mla["rs"], l * MLA["rs"] + g + 1)
                nc.vector.scalar_tensor_tensor(Z[:, j, :], Z[:, j, :], col, RSL[:, g, :], ALU.mult, ALU.mult).then_inc(mla["zn"], 1)
            for h in range(HEADS):
                dve.wait_ge(mla["p"], l * MLA["p"] + h + 1)
                ch.add(nc.vector.tensor_scalar(qT[0:64, h, :], ps[h % 5][0:64, :], ATT_SCALE, None, ALU.mult))
                nc.vector.scalar_tensor_tensor(qT[64:128, h, :], ps[h % 5][64:128, :], ATT_SCALE,
                                                             cn("cs", T)[64:128, :], ALU.mult, ALU.mult).then_inc(mla["qe"], 1)
            units = units_mla(l)
            U, per = len(units), len(units) // 4

            def normalise(u):
                nk = units[u][2]
                dve.wait_ge(mla["ex"], l * MLA["ex"] + u + 1)
                ch.link(nc.vector.reciprocal(st_rec[:, u:u + 1], st_sum[:, u:u + 1]))
                nc.vector.tensor_scalar(Pb[:, u % 2, 0:nk * P], Pb[:, u % 2, 0:nk * P], st_rec[:, u:u + 1], None, ALU.mult).then_inc(mla["pn"], 1)

            def pair_out(j):
                c0 = units[0][1] * P
                dve.wait_ge(mla["o"], l * MLA["o"] + per * (j + 1))
                nc.vector.tensor_copy(BR[:, j, c0:], ps[j % 2][:, c0:]).then_inc(mla["oe"], 1)

            for u in range(U):
                nk = units[u][2]
                dve.wait_ge(mla["s"], l * MLA["s"] + u + 1)
                nc.vector.tensor_reduce(st_nm[:, u:u + 1], ps[6 + u % 2][:, 0:nk * P], AX_X, ALU.max, negate=True).then_inc(mla["nm"], 1)
                if u >= 1:
                    normalise(u - 1)
                if u >= per + 2 and (u - 2) % per == 0:
                    pair_out((u - 2) // per - 1)
            normalise(U - 1)
            pair_out(3)

        zq, zk, zv, so = arena(0, T), arena(512, T), arena(1024, 2, T), arena(2048, 2, T)
        gI, gF, g1, g2_, gB, gA, gM = (arena(3072 + 512 * i, T) for i in range(7))
        gOne = arena(6656, T)
        RT = arena(7168, 3, T)
        acol = arena(8704, TT, 64)
        VA = arena(8960, TT, MLH, P)
        EbS, MbS = arena(11008, 2, T), arena(17408, 2, T)
        Db, Sb, dtmp = arena(12032, 2, T), arena(13056, 2, T), arena(14080, 2, P)
        hd = arena(14336, 2, 2 * T)
        rec_, dn = arena(16384, T), arena(16896, T)
        ml, ML = signals("ml", z=7, zev=6, ab=1, ln=1, mb_in=1, e=2, ra=3, vt=1, vev=1, mb=8,
                                                    eb=8, ebs=8, mbs=8, qk=36, dg=32, d=36, s=36, pv=36, h=8, hs=1, sq=1, ss=2, rs=2,
                                                    out=2)

        def pieces_ml(l):
            c0 = 0 if l == 0 else TC
            out_ = []
            for u in range(2 * MLH):
                if u < MLH:
                    per = [(s, s * P, T, s * P) for s in range(TT)]
                else:
                    per = [(1, 0, T, 128), (0, 0, 128, 0), (0, 256, 512, None), (3, 256, 512, 384), (2, 256, 384, 256)]
                for s, j0, j1, dg in per:
                    j0 = max(j0, c0)
                    dg = None if dg is not None and dg < c0 else dg
                    if j0 < j1:
                        out_.append((u, s, j0, j1, dg))
            return out_

        def ml_pe(pe, l):
            pe.wait_ge(mla["oe"], l * MLA["oe"] + 4)
            for j in range(7):
                n = CH_ML + j // 4
                if j % 4 == 0:
                    wait_chunk(pe, l, n)
                project(pe, ps[j][:, :], cols(n, KD), (j % 4) * P, P).then_inc(ml["z"], 1)
            pe.wait_ge(ml["zev"], l * ML["zev"] + 6)
            for i in range(2):
                for t in range(TT):
                    last = nc.tensor.transpose(ps[1 + i][:, t * P:(t + 1) * P], zv[:, i, t * P:(t + 1) * P], ident)
            last.then_inc(ml["vt"], 1)
            pe.wait_ge(ml["ra"], l * ML["ra"] + 1)
            for t in range(TT):
                last = nc.tensor.transpose(ps[0][:, t * 64:(t + 1) * 64], RT[0:64, 0, t * P:(t + 1) * P], ident[0:64, 0:64])
            last.then_inc(ml["ra"], 1)
            pe.wait_ge(ml["vev"], l * ML["vev"] + 1)
            pe.wait_ge(ml["ra"], l * ML["ra"] + 3)
            pe.wait_ge(ml["e"], l * ML["e"] + 2)
            pcs = pieces_ml(l)
            N = len(pcs)
            firsts = [p for p in range(N) if p == 0 or pcs[p][0] != pcs[p - 1][0]]

            def rows(u):
                if u >= 2:
                    pe.wait_ge(ml["mbs"], l * ML["mbs"] + u - 1)
                r = u
                nc.tensor.matmul(ps[u % 2][:, :], cn("sel", P, r * P)[0:64, :], RT[0:64, 1, :], start=True, stop=True).then_inc(ml["mb"], 1)
                if u >= 1:
                    pe.wait_ge(ml["ebs"], l * ML["ebs"] + u)
                nc.tensor.matmul(ps[2][:, :], cn("sel", P, r * P)[0:64, :], RT[0:64, 2, :], start=True, stop=True).then_inc(ml["eb"], 1)

            def qk(p):
                u, s, j0, j1, dg = pcs[p]
                if p in firsts:
                    rows(u)
                h = u % MLH
                if p >= 3:
                    pe.wait_ge(ml["s"], l * ML["s"] + p - 2)
                q = slice(32 * h, 32 * h + 32)
                nc.tensor.matmul(ps[3 + p % 3][:, j0:j1], zk[q, s * P:(s + 1) * P], zq[q, j0:j1],
                                              start=True, stop=True, tile_position=(32 * h, 0)).then_inc(ml["qk"], 1)

            def pv(p):
                u, s, j0, j1, dg = pcs[p]
                pe.wait_ge(ml["s"], l * ML["s"] + p + 1)
                if p in firsts and u >= 2:
                    pe.wait_ge(ml["h"], l * ML["h"] + u - 1)
                nc.tensor.matmul(ps[6 + u % 2][:, j0:j1], VA[:, s, u % MLH, :], Sb[:, p % 2, j0:j1],
                                              start=(p in firsts), stop=(p + 1 in firsts or p == N - 1)).then_inc(ml["pv"], 1)

            qk(0)
            for p in range(N):
                if p + 1 < N:
                    qk(p + 1)
                pv(p)

        def ml_act(act, ch, l):
            for j in range(6):
                act.wait_ge(ml["z"], l * ML["z"] + j + 1)
                dst = (zq, zk, zv[:, 0, :], zv[:, 1, :], so[:, 0, :], so[:, 1, :])[j]
                if j < 4:
                    ins = nc.scalar.activation(dst, ps[j][:, :], ACT.Copy, scale=float(MLQK) ** -0.5 if j == 0 else 1.0)
                else:
                    ins = nc.scalar.activation(dst, ps[j][:, :], ACT.Sigmoid)
                ins.then_inc(ml["zev"], 1)
            act.wait_ge(ml["ab"], l * ML["ab"] + 1)
            ch.link(nc.scalar.activation(g1[0:64, :], gF[0:64, :], ACT.Abs))
            ch.link(nc.scalar.activation(g1[0:64, :], g1[0:64, :], ACT.Exp, scale=-1.0))
            nc.scalar.activation(g1[0:64, :], g1[0:64, :], ACT.Ln, bias=1.0).then_inc(ml["ln"], 1)
            act.wait_ge(ml["mb_in"], l * ML["mb_in"] + 1)
            nc.scalar.activation(RT[0:32, 2, :], g2_[0:32, :], ACT.Exp, scale=-1.0).then_inc(ml["e"], 1)
            nc.scalar.activation(seg(RT[32:64, 2, :]), rev(g2_[32:64, :]), ACT.Exp, scale=-1.0).then_inc(ml["e"], 1)
            act.wait_ge(ml["ra"], l * ML["ra"] + 2)
            nc.scalar.activation(acol[:, :, :], ps[0][:, 0:256].rearrange("p (t r) -> p t r", r=64), ACT.Copy).then_inc(ml["ra"], 1)
            pcs = pieces_ml(l)
            ndg = 0
            for p, (u, s, j0, j1, dg) in enumerate(pcs):
                if p == 0 or pcs[p - 1][0] != u:
                    act.wait_ge(ml["mb"], l * ML["mb"] + u + 1)
                    nc.scalar.activation(MbS[:, u % 2, :], ps[u % 2][:, :], ACT.Copy).then_inc(ml["mbs"], 1)
                    act.wait_ge(ml["eb"], l * ML["eb"] + u + 1)
                    if u >= 2:
                        act.wait_ge(ml["h"], l * ML["h"] + u - 1)
                    nc.scalar.activation(EbS[:, u % 2, :], ps[2][:, :], ACT.Copy).then_inc(ml["ebs"], 1)
                r = 32 * (u // MLH) + u % MLH
                a = acol[:, s, r:r + 1]
                if p >= 2:
                    act.wait_ge(ml["s"], l * ML["s"] + p - 1)
                if p == 0 or pcs[p - 1][0] != u:
                    act.wait_ge(ml["mbs"], l * ML["mbs"] + u + 1)
                spans = [(j0, j1)] if dg is None else [x for x in ((j0, dg), (dg + P, j1)) if x[0] < x[1]]
                todo = []
                for x0, x1 in spans:
                    todo.append((Db[:, p % 2, x0:x1], MbS[:, u % 2, x0:x1], -1.0))
                if dg is not None:
                    ndg += 1
                    todo.append((Db[:, p % 2, dg:dg + P], dtmp[:, (ndg - 1) % 2, :], 1.0))
                    act.wait_ge(ml["dg"], l * ML["dg"] + ndg)
                for n, (dst, src, sc) in enumerate(todo):
                    ins = nc.scalar.activation(dst, src, ACT.Exp, scale=sc, bias=a)
                    if n == len(todo) - 1:
                        ins.then_inc(ml["d"], 1)
            act.wait_ge(ml["hs"], l * ML["hs"] + 1)
            nc.scalar.activation(hd[:, 1, :], hd[:, 0, :], ACT.Square).then_inc(ml["sq"], 1)
            for i in range(2):
                act.wait_ge(ml["ss"], l * ML["ss"] + i + 1)
                ch.link(nc.scalar.activation(EbS[:, i, :], ps[4 + i][:, :], ACT.Ln, scale=1.0 / 64, bias=cn("eps", 1)))
                nc.scalar.activation(EbS[:, i, :], EbS[:, i, :], ACT.Exp, scale=-0.5).then_inc(ml["rs"], 1)

        def seg(v):
            return v.rearrange("p (s t) -> p s t", s=2)

        def rev(v):
            return seg(v)[:, :, ::-1]

        def ml_dve(dve, ch, l):
            dve.wait_ge(ml["z"], l * ML["z"] + 7)
            b = sm("ml_b")
            ch.add(nc.vector.memset(gOne[0:64, :], 1.0))
            ch.add(nc.vector.memset(VA[:, :, :, 64:128], 1.0))
            ch.add(nc.vector.tensor_scalar(gI[0:32, :], ps[6][0:32, :], b[0:32, :], None, ALU.add))
            ch.add(nc.vector.tensor_scalar(seg(gI[32:64, :]), rev(ps[6][32:64, :]), b[32:64, :], None, ALU.add))
            ch.add(nc.vector.tensor_scalar(gF[0:32, :], ps[6][64:96, :], b[64:96, :], None, ALU.add))
            nc.vector.tensor_scalar(seg(gF[32:64, :]), rev(ps[6][96:128, :]), b[96:128, :], None, ALU.add).then_inc(ml["ab"], 1)
            dve.wait_ge(ml["vt"], l * ML["vt"] + 1)
            for i in range(2):
                last = nc.vector.tensor_copy(VA[:, :, 2 * i:2 * i + 2, 0:64], ps[1 + i][:, :].rearrange("p (t h v) -> p t h v", t=TT, h=2))
                if i == 1:
                    last.then_inc(ml["vev"], 1)
            dve.wait_ge(ml["ln"], l * ML["ln"] + 1)
            ch.link(nc.vector.scalar_tensor_tensor(g2_[0:64, :], gF[0:64, :], 0.0, g1[0:64, :], ALU.min, ALU.subtract))
            ch.link(nc.vector.tensor_tensor_scan(out=gB[0:64, :], data0=gOne[0:64, :], data1=g2_[0:64, :], initial=0.0, op0=ALU.mult, op1=ALU.add))
            ch.link(nc.vector.tensor_tensor(gA[0:64, :], gI[0:64, :], gB[0:64, :], ALU.subtract))
            ch.link(nc.vector.tensor_tensor_scan(out=gM[0:64, :], data0=gA[0:64, :], data1=gA[0:64, :], initial=0.0, op0=ALU.max, op1=ALU.max))
            nc.vector.tensor_tensor(g2_[0:64, :], gM[0:64, :], gB[0:64, :], ALU.add).then_inc(ml["mb_in"], 1)
            for v, src in ((0, gA), (1, gM)):
                ch.add(nc.vector.tensor_copy(RT[0:32, v, :], src[0:32, :]))
                last = nc.vector.tensor_copy(seg(RT[32:64, v, :]), rev(src[32:64, :]))
                if v == 0:
                    ch.add(last)
                else:
                    last.then_inc(ml["ra"], 1)
            pcs = pieces_ml(l)
            N = len(pcs)
            lasts = {p: pcs[p][0] for p in range(N) if p == N - 1 or pcs[p][0] != pcs[p + 1][0]}
            dgs = [0]

            def diagonal(p):
                u, s, j0, j1, dg = pcs[p]
                if dg is None:
                    return
                dve.wait_ge(ml["mbs"], l * ML["mbs"] + u + 1)
                if dgs[0] >= 2:
                    back = [x for x in range(p) if pcs[x][4] is not None][-2]
                    dve.wait_ge(ml["d"], l * ML["d"] + back + 1)
                nc.vector.scalar_tensor_tensor(dtmp[:, dgs[0] % 2, :], MbS[:, u % 2, dg:dg + P], -1.0,
                                                            cn("mlmask", P, P * (u // MLH)), ALU.mult, ALU.add).then_inc(ml["dg"], 1)
                dgs[0] += 1

            def finish(u):
                c0 = 0 if l == 0 else TC
                d, h = divmod(u, MLH)
                dve.wait_ge(ml["pv"], l * ML["pv"] + ([p for p in lasts if lasts[p] == u][0] + 1))
                dve.wait_ge(ml["ebs"], l * ML["ebs"] + u + 1)
                ch.link(nc.vector.scalar_tensor_tensor(dn[64:128, c0:], ps[6 + u % 2][64:128, c0:], -1.0, EbS[64:128, u % 2, c0:],
                                                       ALU.mult, ALU.max))
                ch.link(nc.vector.tensor_tensor(dn[64:128, c0:], ps[6 + u % 2][64:128, c0:], dn[64:128, c0:], ALU.max))
                ch.link(nc.vector.reciprocal(rec_[0:64, c0:], dn[64:128, c0:]))
                nc.vector.tensor_tensor(hd[64 * (h % 2):64 * (h % 2) + 64, d, (h // 2) * T + c0:(h // 2 + 1) * T],
                                                    ps[6 + u % 2][0:64, c0:], rec_[0:64, c0:], ALU.mult).then_inc(ml["h"], 1)

            if l:
                ch.add(nc.vector.memset(hd[:, :, :], 0.0))
                ch.settle()
            diagonal(0)
            for p in range(N):
                if p + 1 < N:
                    diagonal(p + 1)
                u, s, j0, j1, dg = pcs[p]
                dve.wait_ge(ml["d"], l * ML["d"] + p + 1)
                dve.wait_ge(ml["qk"], l * ML["qk"] + p + 1)
                if p >= 2:
                    dve.wait_ge(ml["pv"], l * ML["pv"] + p - 1)
                nc.vector.tensor_tensor(Sb[:, p % 2, j0:j1], ps[3 + p % 3][:, j0:j1], Db[:, p % 2, j0:j1], ALU.mult).then_inc(ml["s"], 1)
                if p - 2 in lasts:
                    finish(lasts[p - 2])
            for p in (N - 2, N - 1):
                if p in lasts:
                    finish(lasts[p])
            dve.wait_ge(ml["h"], l * ML["h"] + 8)
            nc.vector.tensor_tensor(hd[:, 0, :], hd[:, 0, :], hd[:, 1, :], ALU.add).then_inc(ml["hs"], 1)
            for i in range(2):
                dve.wait_ge(ml["rs"], l * ML["rs"] + i + 1)
                ch.link(nc.vector.scalar_tensor_tensor(hd[:, 0, i * T:(i + 1) * T], hd[:, 0, i * T:(i + 1) * T], sm("ml_g", i),
                                                       EbS[:, i, :], ALU.mult, ALU.mult))
                nc.vector.tensor_tensor(BR[:, 4 + i, :], hd[:, 0, i * T:(i + 1) * T], so[:, i, :], ALU.mult).then_inc(ml["out"], 1)

        Zs = arena(0, 9, T)
        ZP = arena(4608, 2, 2 * 258)
        tsh = arena(5640, T)
        KK, KDS, YA = arena(6152, 2, T), arena(7176, 2, T), arena(8200, 2, T)
        sgm, Gc, Gp, ex1, ex2, ex3, aa = (arena(9224 + 512 * i, T) for i in range(7))
        NL, ZT, X, XT = sgm, Gc, Gp, ex1
        AR = arena(12808, NC, P)
        beta, kappa = arena(13832, T), arena(14344, T)
        VT, BT, KT = (arena(14856 + 512 * i, NC, 64) for i in range(3))
        MB, MK = arena(16392, NC, P), arena(17416, NC, P)
        ST, RH, UU = arena(4608, 2, 64), arena(4736, 2, 64), arena(4864, 2, 64)
        hmu, omu = arena(18440, 9), arena(18449, 9)
        rw, RW = signals("rw", z=9, zev=9, sh=9, tl=2, kc=6, lr=8, sg=8, gc=4, ex=12,
                                                    prep=4, tok=4, tokc=12, sc=16, msk=16, nl=48, pad=1, yd=2, zt=48, ztc=40, xu=40, xd=48,
                                                    rh=32, rhc=32, uu=32, uc=32, sn=32, snc=32, y=4, yc=4,
                                                    bo=1, bs=2, bc=2, ym=2, yq=2, ys=2, yr=2, g=2, out=2)
        DEC = float(np.exp(-0.5))
        MOD_BANKS = (5, 0, 4)
        ZT_BANK = (1, 6)
        HALF = (slice(0, 4 * C), slice(4 * C, 8 * C))
        UNITS = [(d, pr) for d in range(2) for pr in range(2)]
        ORDER = [list(range(NC)), list(range(NC // 2 - 1, -1, -1)) + list(range(NC - 1, NC // 2 - 1, -1))]

        def each_head():
            return (slice(0, 64), slice(64, 128))

        def rw_pe(pe, l):
            for j in range(9):
                n = CH_RW + j // 4
                if j % 4 == 0:
                    wait_chunk(pe, l, n)
                if j >= 4:
                    pe.wait_ge(rw["zev"], l * RW["zev"] + j - 3)
                project(pe, ps[j % 4][:, :], cols(n, KD), (j % 4) * P, P).then_inc(rw["z"], 1)
                if j == 0:
                    pe.wait_ge(ml["sq"], l * ML["sq"] + 1)
                    for i in range(2):
                        nc.tensor.matmul(ps[4 + i][:, :], bd, hd[:, 1, i * T:(i + 1) * T], start=True, stop=True).then_inc(ml["ss"], 1)
            pe.wait_ge(rw["kc"], l * RW["kc"] + 2)
            for i in range(2):
                last = nc.tensor.matmul(ps[4 + i][:, :], bd, YA[:, i, :], start=True, stop=True)
            last.then_inc(rw["kc"], 1)
            pe.wait_ge(rw["tl"], l * RW["tl"] + 2)
            for n, (d, pr) in enumerate(UNITS):
                hd_ = slice(64 * d, 64 * d + 64)
                for i, (o, z) in enumerate(((WS_W2, 6), (WS_A2, 7))):
                    nc.tensor.matmul(ps[i][:, :], WS[hd_, o + pr * P:o + (pr + 1) * P], Zs[hd_, z, :], start=True, stop=True).then_inc(rw["lr"], 1)
                todo = [(m, j, k, MOD_BANKS[i]) for i, (m, j) in enumerate(MOD_AT[l][n]) for k in range(KD)]

                def late(steps):
                    for _ in range(min(steps, len(todo))):
                        mod_rows(pe, *todo.pop(0))
                if n == 0:
                    pe.wait_ge(rw["kc"], l * RW["kc"] + 4)
                late(KD)
                pe.wait_ge(rw["prep"], l * RW["prep"] + n + 1)
                for b, src in enumerate((Zs[:, 4 + pr, :], beta, kappa)):
                    for c in range(NC):
                        for h in each_head():
                            last = nc.tensor.matmul(ps[2 + b][h, c * C:(c + 1) * C], src[h, c * C:(c + 1) * C], ident[h, h],
                                                    start=True, stop=True)
                last.then_inc(rw["tok"], 1)
                banks = (5, 6, 7, 0)
                pe.wait_ge(mod_row, MOD_CHUNKS.index(MOD_AT[l][n][0]) + 1)
                for g in range(4):
                    src = beta if g < 2 else kappa
                    for c in range(4 * (g % 2), 4 * (g % 2) + 4):
                        for h in each_head():
                            last = nc.tensor.matmul(ps[banks[g]][h, (c % 4) * P:(c % 4 + 1) * P], src[h, c * C:(c + 1) * C],
                                                    AR[h, c, :], start=True, stop=True)
                    last.then_inc(rw["sc"], 1)
                pe.wait_ge(rw["msk"], l * RW["msk"] + 4 * n + 4)
                pe.wait_ge(rw["tokc"], l * RW["tokc"] + 3 * n + 3)
                for v in range(6):
                    for b in range(2):
                        pe.wait_ge(rw["nl"], l * RW["nl"] + 12 * n + 2 * v + b + 1)
                        if v:
                            pe.wait_ge(rw["xd"], l * RW["xd"] + 12 * n + 2 * v + b - 1)
                        for c in range(4 * b, 4 * b + 4):
                            for h in each_head():
                                cc = slice(c * C, (c + 1) * C)
                                last = nc.tensor.matmul(ps[ZT_BANK[b]][h, (c % 4) * C:(c % 4 + 1) * C], NL[h, cc], XT[h, cc], start=True, stop=True)
                        last.then_inc(rw["zt"], 1)
                    if v == 0:
                        continue
                    late(2)
                    for b in range(2):
                        pe.wait_ge(rw["ztc"], l * RW["ztc"] + 10 * n + 2 * v + b - 1)
                        for c in range(4 * b, 4 * b + 4):
                            for h in each_head():
                                cc = slice(c * C, (c + 1) * C)
                                last = nc.tensor.matmul(ps[2 + b][h, (c % 4) * C:(c % 4 + 1) * C], ZT[h, cc], X[h, cc], start=True, stop=True)
                                if v < 5:
                                    last = nc.tensor.matmul(ps[2 + b][h, (c % 4 + 4) * C:(c % 4 + 5) * C], X[h, cc], ZT[h, cc], start=True, stop=True)
                        last.then_inc(rw["xu"], 1)
                    late(2)
                if len(MOD_AT[l][n]) > 2:
                    pe.wait_ge(mod_row, MOD_CHUNKS.index(MOD_AT[l][n][2]) + 1)
                pe.wait_ge(rw["xd"], l * RW["xd"] + 12 * n + 12)
                for i, c in enumerate(ORDER[d]):
                    q = 8 * n + i
                    S0, S1 = ST[:, i % 2, :], ST[:, (i + 1) % 2, :]
                    cc = slice(c * C, (c + 1) * C)
                    if i == 2:
                        mod_turn(pe, MOD_AT[l][n], 1)
                    if i:
                        pe.wait_ge(rw["snc"], l * RW["snc"] + q)
                    for h in each_head():
                        nc.tensor.matmul(ps[4][h, 0:64], MK[h, c, 0:64], VT[h, c, :], start=True, stop=False)
                        last = nc.tensor.matmul(ps[4][h, 0:64], AR[h, c, 0:64], S0[h, :], start=False, stop=True)
                    last.then_inc(rw["rh"], 1)
                    pe.wait_ge(rw["rhc"], l * RW["rhc"] + q + 1)
                    for h in each_head():
                        last = nc.tensor.matmul(ps[5][h, 0:64], X[h, cc], RH[h, i % 2, :], start=True, stop=True)
                    last.then_inc(rw["uu"], 1)
                    for h in each_head():
                        nc.tensor.matmul(ps[6][h, 0:64], ident[h, h], S0[h, :], start=True, stop=False)
                        nc.tensor.matmul(ps[6][h, 0:64], KT[h, c, :], VT[h, c, :], start=False, stop=False)
                        if h.start == 0:
                            pe.wait_ge(rw["uc"], l * RW["uc"] + q + 1)
                        last = nc.tensor.matmul(ps[6][h, 0:64], BT[h, c, :], UU[h, i % 2, :], start=False, stop=True)
                    last.then_inc(rw["sn"], 1)
                    for h in each_head():
                        nc.tensor.matmul(ps[7][h, cc], S0[h, :], AR[h, c, 64:128], start=True, stop=False)
                        nc.tensor.matmul(ps[7][h, cc], VT[h, c, :], MK[h, c, 64:128], start=False, stop=False)
                        last = nc.tensor.matmul(ps[7][h, cc], UU[h, i % 2, :], MB[h, c, 64:128], start=False, stop=True)
                    if i == NC - 1:
                        last.then_inc(rw["y"], 1)
            pe.wait_ge(rw["yc"], l * RW["yc"] + 4)
            pe.wait_ge(rw["snc"], l * RW["snc"] + 32)
            pe.wait_ge(rw["bo"], l * RW["bo"] + 1)
            for pr in range(2):
                nc.tensor.matmul(ps[pr][:, :], bd, KDS[:, pr, :], start=True, stop=True).then_inc(rw["bs"], 1)
            for pr in range(2):
                last = nc.tensor.matmul(ps[2 + pr][:, :], bd, YA[:, pr, :], start=True, stop=True)
                last.then_inc(rw["ym"], 1)
            for pr in range(2):
                nc.tensor.matmul(ps[6 + pr][:, :], WS[:, WS_G2 + pr * P:WS_G2 + (pr + 1) * P], Zs[:, 8, :], start=True, stop=True).then_inc(rw["g"], 1)
            for pr in range(2):
                pe.wait_ge(rw["yq"], l * RW["yq"] + pr + 1)
                nc.tensor.matmul(ps[4 + pr][:, :], bd, sq_[pr], start=True, stop=True).then_inc(rw["ys"], 1)

        sq_ = (beta, kappa)

        def rw_act(act, ch, l):
            for j in range(9):
                act.wait_ge(rw["z"], l * RW["z"] + j + 1)
                if j >= 2:
                    act.wait_ge(rw["sh"], l * RW["sh"] + j - 1)
                if j == 0:
                    act.wait_ge(rw["pad"], l * RW["pad"] + 1)
                dst = ZP[:, j % 2, :].rearrange("p (s t) -> p s t", s=2)[:, :, 1:257]
                nc.scalar.activation(dst, ps[j % 4][:, :].rearrange("p (s t) -> p s t", s=2), ACT.Copy).then_inc(rw["zev"], 1)
            act.wait_ge(rw["sh"], l * RW["sh"] + 9)
            nc.scalar.activation(Zs[:, 6, :], Zs[:, 6, :], ACT.Tanh).then_inc(rw["tl"], 1)
            nc.scalar.activation(Zs[:, 8, :], Zs[:, 8, :], ACT.Sigmoid).then_inc(rw["tl"], 1)
            act.wait_ge(rw["kc"], l * RW["kc"] + 1)
            nc.scalar.activation(YA[:, :, :], KK[:, :, :], ACT.Square).then_inc(rw["kc"], 1)
            act.wait_ge(rw["kc"], l * RW["kc"] + 4)
            ch.link(nc.scalar.activation(KDS[:, :, :], KDS[:, :, :], ACT.Ln))
            nc.scalar.activation(KDS[:, :, :], KDS[:, :, :], ACT.Exp, scale=-0.5).then_inc(rw["kc"], 1)
            for n, (d, pr) in enumerate(UNITS):
                if n:
                    act.wait_ge(rw["y"], l * RW["y"] + n)
                act.wait_ge(rw["lr"], l * RW["lr"] + 2 * n + 1)
                nc.scalar.activation(sgm, ps[0][:, :], ACT.Sigmoid, bias=sm("w0", 2 * d + pr)).then_inc(rw["sg"], 1)
                act.wait_ge(rw["lr"], l * RW["lr"] + 2 * n + 2)
                nc.scalar.activation(aa, ps[1][:, :], ACT.Sigmoid, bias=sm("a0", 2 * d + pr)).then_inc(rw["sg"], 1)
                act.wait_ge(rw["gc"], l * RW["gc"] + n + 1)
                nc.scalar.activation(ex1, Gp, ACT.Exp, scale=-DEC).then_inc(rw["ex"], 1)
                nc.scalar.activation(ex2, Gc, ACT.Exp, scale=DEC).then_inc(rw["ex"], 1)
                nc.scalar.activation(ex3, Gc, ACT.Exp, scale=-DEC).then_inc(rw["ex"], 1)
                mod_copy(act, *MOD_AT[l][n][0], 0, MOD_BANKS[0])
                act.wait_ge(rw["tok"], l * RW["tok"] + n + 1)
                for b, dst in enumerate((VT, BT, KT)):
                    nc.scalar.activation(dst[:, :, :], ps[2 + b][:, :].rearrange("p (c f) -> p c f", c=NC), ACT.Copy).then_inc(rw["tokc"], 1)
                for v in range(1, 6):
                    for b in range(2):
                        act.wait_ge(rw["zt"], l * RW["zt"] + 12 * n + 2 * v + b + 1)
                        if v > 1 or n > 0:
                            act.wait_ge(rw["xu"], l * RW["xu"] + 10 * n + (2 * v + b - 3 if v > 1 else 0))
                        nc.scalar.activation(ZT[:, HALF[b]], ps[ZT_BANK[b]][:, 0:4 * C], ACT.Copy).then_inc(rw["ztc"], 1)
                    if v == 3:
                        mod_copy(act, *MOD_AT[l][n][1], 1, MOD_BANKS[1])
                if len(MOD_AT[l][n]) > 2:
                    mod_copy(act, *MOD_AT[l][n][2], 2, MOD_BANKS[2])
                for i, c in enumerate(ORDER[d]):
                    q = 8 * n + i
                    act.wait_ge(rw["rh"], l * RW["rh"] + q + 1)
                    nc.scalar.activation(RH[:, i % 2, :], ps[4][:, 0:64], ACT.Copy, scale=-1.0).then_inc(rw["rhc"], 1)
                    act.wait_ge(rw["sn"], l * RW["sn"] + q + 1)
                    pl = c * C + (C - 1 if d == 0 else 0)
                    nc.scalar.activation(ST[:, (i + 1) % 2, :], ps[6][:, 0:64], ACT.Copy, scale=ex3[:, pl:pl + 1]).then_inc(rw["snc"], 1)
            for pr in range(2):
                act.wait_ge(rw["yd"], l * RW["yd"] + pr + 1)
                nc.scalar.activation(sq_[pr], YA[:, pr, :], ACT.Square).then_inc(rw["yq"], 1)
            for pr in range(2):
                act.wait_ge(rw["ys"], l * RW["ys"] + pr + 1)
                ch.link(nc.scalar.activation(sq_[pr], ps[4 + pr][:, :], ACT.Ln, scale=1.0 / RN, bias=cn("eps", 1, 1)))
                nc.scalar.activation(sq_[pr], sq_[pr], ACT.Exp, scale=-0.5).then_inc(rw["yr"], 1)

        def rw_dve(dve, ch, l):
            dve.wait_ge(ml["out"], l * ML["out"] + 2)
            ch.add(nc.vector.tensor_scalar(hmu, sm("mu", 0, 9), 0.5, None, ALU.mult))
            ch.link(nc.vector.tensor_scalar(omu, sm("mu", 0, 9), -1.0, 1.0, ALU.mult, ALU.add))
            nc.vector.memset(ZP[:, :, :], 0.0).then_inc(rw["pad"], 1)
            for j in range(9):
                z = ZP[:, j % 2, :].rearrange("p (s t) -> p s t", s=2)
                dve.wait_ge(rw["zev"], l * RW["zev"] + j + 1)
                t = seg(tsh)
                if j:
                    dve.wait_ge(rw["sh"], l * RW["sh"] + j)
                ch.link(nc.vector.tensor_tensor(t, z[:, :, 0:256], z[:, :, 2:258], ALU.add))
                ch.link(nc.vector.tensor_scalar(t, t, hmu[:, j:j + 1], None, ALU.mult))
                nc.vector.scalar_tensor_tensor(seg(Zs[:, j, :]), z[:, :, 1:257], omu[:, j:j + 1], t, ALU.mult, ALU.add).then_inc(rw["sh"], 1)
            dve.wait_ge(rw["sh"], l * RW["sh"] + 9)
            for pr in range(2):
                last = nc.vector.tensor_scalar(KK[:, pr, :], Zs[:, 2 + pr, :], sm("k_k", pr), None, ALU.mult)
                if pr == 0:
                    ch.add(last)
            last.then_inc(rw["kc"], 1)
            dve.wait_ge(rw["kc"], l * RW["kc"] + 3)
            for pr in range(2):
                last = nc.vector.tensor_scalar(KDS[:, pr, :], ps[4 + pr][:, :], 1e-24, None, ALU.max)
                if pr == 0:
                    ch.add(last)
            last.then_inc(rw["kc"], 1)
            dve.wait_ge(rw["kc"], l * RW["kc"] + 5)
            nc.vector.tensor_tensor(KK[:, :, :], KK[:, :, :], KDS[:, :, :], ALU.mult).then_inc(rw["kc"], 1)
            dve.wait_ge(rw["kc"], l * RW["kc"] + 6)
            for n, (d, pr) in enumerate(UNITS):
                step = 1 if d == 0 else -1
                dve.wait_ge(rw["sg"], l * RW["sg"] + 2 * n + 1)
                if n:
                    dve.wait_ge(rw["y"], l * RW["y"] + n)
                ch.link(nc.vector.tensor_tensor_scan(out=Gc[:, ::step], data0=cn("reset", T), data1=sgm[:, ::step], initial=0.0,
                                                     op0=ALU.mult, op1=ALU.add))
                nc.vector.tensor_tensor(Gp, Gc, sgm, ALU.subtract).then_inc(rw["gc"], 1)
                dve.wait_ge(rw["sg"], l * RW["sg"] + 2 * n + 2)
                ch.link(nc.vector.tensor_tensor(beta, KK[:, pr, :], aa, ALU.mult))
                ch.link(nc.vector.tensor_scalar(aa, aa, -1.0, sm("k_a", pr), ALU.add, ALU.mult))
                ch.link(nc.vector.scalar_tensor_tensor(kappa, aa, 1.0, Zs[:, 2 + pr, :], ALU.add, ALU.mult))
                if d == 0:
                    ch.add(nc.vector.tensor_copy(KDS[:, pr, :], kappa))
                else:
                    ch.add(nc.vector.tensor_tensor(KDS[:, pr, :], KDS[:, pr, :], kappa, ALU.add))
                ch.settle()

                def chunks(v):
                    return v.rearrange("p (c t) -> p c t", t=C)
                dve.wait_ge(rw["ex"], l * RW["ex"] + 3 * n + 3)
                ch.add(nc.vector.tensor_tensor(AR[:, :, 0:64], chunks(KK[:, pr, :]), chunks(ex1), ALU.mult))
                ch.add(nc.vector.tensor_tensor(AR[:, :, 64:128], chunks(Zs[:, pr, :]), chunks(ex3), ALU.mult))
                ch.add(nc.vector.tensor_tensor(beta, beta, ex2, ALU.mult))
                ch.add(nc.vector.memset(ST[:, 0, :], 0.0))
                nc.vector.tensor_tensor(kappa, kappa, ex2, ALU.mult).then_inc(rw["prep"], 1)
                dve.wait_ge(rw["prep"], l * RW["prep"] + n + 1)
                for x in (X, XT):
                    for h in each_head():
                        ch.add(nc.vector.tensor_copy(chunks(x)[h, :, :], bcast(ident[h, h], 1, NC)))
                mask = cn("rwmask", P, d * P)
                banks = (5, 6, 7, 0)
                for g in range(4):
                    dve.wait_ge(rw["sc"], l * RW["sc"] + 4 * n + g + 1)
                    dst = (MB if g < 2 else MK)[:, 4 * (g % 2):4 * (g % 2) + 4, :]
                    nc.vector.tensor_tensor(dst, ps[banks[g]][:, :].rearrange("p (c t) -> p c t", c=4),
                                                          bcast(mask, 1, 4), ALU.mult).then_inc(rw["msk"], 1)
                dve.wait_ge(rw["msk"], l * RW["msk"] + 4 * n + 4)
                def blocks(v, b):
                    nc.vector.tensor_tensor(chunks(NL)[:, 4 * b:4 * b + 4, :], MB[:, 4 * b:4 * b + 4, 0:64],
                                            bcast(cn("lev", 64, 64 * v), 1, 4), ALU.mult).then_inc(rw["nl"], 1)
                for b in range(2):
                    blocks(0, b)
                for b in range(2):
                    dve.wait_ge(rw["zt"], l * RW["zt"] + 12 * n + b + 1)
                    ch.add(nc.vector.tensor_tensor(XT[:, HALF[b]], XT[:, HALF[b]], ps[ZT_BANK[b]][:, 0:4 * C], ALU.subtract))
                    dve.wait_ge(rw["nl"], l * RW["nl"] + 12 * n + b + 1)
                    nc.vector.tensor_tensor(X[:, HALF[b]], X[:, HALF[b]], NL[:, HALF[b]], ALU.subtract).then_inc(rw["xd"], 1)
                    dve.wait_ge(rw["xd"], l * RW["xd"] + 12 * n + b + 1)
                    blocks(1, b)
                for v in range(1, 6):
                    for b in range(2):
                        dve.wait_ge(rw["xd"], l * RW["xd"] + 12 * n + 2 * v + b - 1)
                        dve.wait_ge(rw["xu"], l * RW["xu"] + 10 * n + 2 * v + b - 1)
                        if v < 5:
                            ch.add(nc.vector.tensor_tensor(XT[:, HALF[b]], XT[:, HALF[b]], ps[2 + b][:, 4 * C:8 * C], ALU.subtract))
                        nc.vector.tensor_tensor(X[:, HALF[b]], X[:, HALF[b]], ps[2 + b][:, 0:4 * C], ALU.subtract).then_inc(rw["xd"], 1)
                        if v < 5:
                            blocks(v + 1, b)
                for i in range(NC):
                    if i == 3:
                        mod_dve(dve, ch, MOD_AT[l][n], 1)
                    q = 8 * n + i
                    dve.wait_ge(rw["uu"], l * RW["uu"] + q + 1)
                    nc.vector.tensor_copy(UU[:, i % 2, :], ps[5][:, 0:64]).then_inc(rw["uc"], 1)
                dve.wait_ge(rw["y"], l * RW["y"] + n + 1)
                if d == 0:
                    nc.vector.tensor_copy(YA[:, pr, :], ps[7][:, :]).then_inc(rw["yc"], 1)
                else:
                    nc.vector.tensor_tensor(YA[:, pr, :], YA[:, pr, :], ps[7][:, :], ALU.add).then_inc(rw["yc"], 1)
            dve.wait_ge(rw["yc"], l * RW["yc"] + 4)
            for pr in range(2):
                last = nc.vector.scalar_tensor_tensor(KDS[:, pr, :], Zs[:, pr, :], sm("r_k", pr), KDS[:, pr, :], ALU.mult, ALU.mult)
                if pr == 0:
                    ch.add(last)
            last.then_inc(rw["bo"], 1)
            for pr in range(2):
                dve.wait_ge(rw["bs"], l * RW["bs"] + pr + 1)
                nc.vector.tensor_tensor(KK[:, pr, :], ps[pr][:, :], Zs[:, 4 + pr, :], ALU.mult).then_inc(rw["bc"], 1)
            for pr in range(2):
                dve.wait_ge(rw["ym"], l * RW["ym"] + 2)
                nc.vector.scalar_tensor_tensor(YA[:, pr, :], ps[2 + pr][:, :], -1.0 / RN, YA[:, pr, :], ALU.mult, ALU.add).then_inc(rw["yd"], 1)
            dve.wait_ge(rw["yd"], l * RW["yd"] + 2)
            for pr in range(2):
                dve.wait_ge(rw["yr"], l * RW["yr"] + pr + 1)
                ch.link(nc.vector.scalar_tensor_tensor(YA[:, pr, :], YA[:, pr, :], sm("lnx_w", pr), sq_[pr], ALU.mult, ALU.mult))
                dve.wait_ge(rw["bc"], l * RW["bc"] + 2)
                ch.link(nc.vector.scalar_tensor_tensor(YA[:, pr, :], YA[:, pr, :], sm("lnx_b", pr), KK[:, pr, :], ALU.add, ALU.add))
                dve.wait_ge(rw["g"], l * RW["g"] + pr + 1)
                nc.vector.tensor_tensor(BR[:, 6 + pr, :], YA[:, pr, :], ps[6 + pr][:, :], ALU.mult).then_inc(rw["out"], 1)

        YM = arena(0, KD, T)
        gate = arena(4096, 2, T)
        gprod = arena(5120, 2, T)
        mg, MG = signals("mg", g=24, b=24, sg=24, m=24, o=8, r=8)
        BR_TILES = ((0, 4), (4, 6), (6, 8))

        def mg_pe(pe, l):
            c0 = 0 if l == 0 else TC
            for m in range(KD):
                wait_chunk(pe, l, CH_MERGE + m)
                w = chunk(CH_MERGE + m)
                wg = w[:, 0:3072].rearrange("p (k m) -> p k m", k=KD)
                wb = w[:, 3072:4096].rearrange("p (k m) -> p k m", k=KD)
                for i in range(3):
                    n = 3 * m + i
                    if n == 2:
                        pe.wait_ge(rw["out"], l * RW["out"] + 2)
                    if n >= 4:
                        pe.wait_ge(mg["m"], l * MG["m"] + n - 3)
                    for k in range(KD):
                        last = nc.tensor.matmul(ps[2 * (n % 4)][:, c0:], wg[:, k, i * P:(i + 1) * P], H[:, k, c0:],
                                                start=(k == 0), stop=(k == KD - 1))
                    last.then_inc(mg["g"], 1)
                    b0, b1 = BR_TILES[i]
                    for k in range(b0, b1):
                        last = nc.tensor.matmul(ps[2 * (n % 4) + 1][:, c0:], wb[:, k, :], BR[:, k, c0:], start=(k == b0), stop=(k == b1 - 1))
                    last.then_inc(mg["b"], 1)
            pe.wait_ge(mg["m"], l * MG["m"] + 24)
            for m in range(KD):
                if m % 4 == 0:
                    wait_chunk(pe, l, CH_OUT + m // 4)
                w = cols(CH_OUT + m // 4, KD)
                if m >= 4:
                    pe.wait_ge(mg["r"], l * MG["r"] + m - 3)
                for k in range(KD):
                    last = nc.tensor.matmul(ps[m % 4][:, c0:], w[:, k, (m % 4) * P:(m % 4 + 1) * P], YM[:, k, c0:],
                                            start=(k == 0), stop=(k == KD - 1))
                last.then_inc(mg["o"], 1)

        def mg_act(act, l):
            c0 = 0 if l == 0 else TC
            for n in range(24):
                act.wait_ge(mg["g"], l * MG["g"] + n + 1)
                if n == 0:
                    act.wait_ge(rw["out"], l * RW["out"] + 2)
                if n >= 2:
                    act.wait_ge(mg["m"], l * MG["m"] + n - 1)
                nc.scalar.activation(gate[:, n % 2, c0:], ps[2 * (n % 4)][:, c0:], ACT.Sigmoid).then_inc(mg["sg"], 1)

        def mg_dve(dve, ch, l):
            c0 = 0 if l == 0 else TC
            dve.wait_ge(rw["out"], l * RW["out"] + 2)
            for n in range(24):
                m, i = divmod(n, 3)
                dve.wait_ge(mg["sg"], l * MG["sg"] + n + 1)
                dve.wait_ge(mg["b"], l * MG["b"] + n + 1)
                br = ps[2 * (n % 4) + 1][:, c0:]
                if i == 0:
                    nc.vector.tensor_tensor(YM[:, m, c0:], br, gate[:, n % 2, c0:], ALU.mult).then_inc(mg["m"], 1)
                else:
                    if n >= 2:
                        dve.wait_ge(mg["m"], l * MG["m"] + n - 1)
                    ch.link(nc.vector.tensor_tensor(gprod[:, n % 2, c0:], br, gate[:, n % 2, c0:], ALU.mult))
                    dve.wait_ge(mg["m"], l * MG["m"] + n)
                    nc.vector.tensor_tensor(YM[:, m, c0:], YM[:, m, c0:], gprod[:, n % 2, c0:], ALU.add).then_inc(mg["m"], 1)
            for m in range(KD):
                dve.wait_ge(mg["o"], l * MG["o"] + m + 1)
                for half in range(c0 // TC, 2):
                    part = slice(half * TC, (half + 1) * TC)
                    last = nc.vector.scalar_tensor_tensor(R[:, m, part], ps[m % 4][:, part], MOD[:, 16 + m, half:half + 1],
                                                          R[:, m, part], ALU.mult, ALU.add)
                    if half == 1:
                        last.then_inc(mg["r"], 1)
                    else:
                        ch.add(last)

        r_sc, r_bi = arena(8192, TT, E), arena(8448, TT, E)
        r_mx = arena(8704, TT * NG, 8)
        r_gs = arena(8960, TT, NG)
        r_cmp, r_eq = arena(8992, TT, NG * NG), arena(9248, TT, NG * NG)
        r_rank, r_pen = arena(9504, TT, NG), arena(9536, TT, NG)
        r_msk, r_rep = arena(9568, TT, E), arena(9824, TT, E)
        r_top, r_sum, r_rec = arena(10080, TT, 8), arena(10112, TT), arena(10116, TT)
        r_sel = arena(10120, TT, E)
        r_q = arena(10376, TT, 2, E)
        r_ej = arena(12288, NOV, E)
        r_qk = arena(12288, TT, 2, E)
        r_pos, r_over, r_at, r_blk, r_cs, r_hot = (arena(14336 + 256 * i, TT, E) for i in range(6))
        r_nov, r_incl, r_excl = (arena(15872 + 64 * i, E) for i in range(3))
        r_dk = arena(16064, TT, 2, TOPK)
        r_few = arena(16160, NOV)
        HTB = arena(16384, 2, D)
        ro, RO = signals("ro", ht=8, hc=8, hs0=32, hs1=32, mm=1, sg=1, sel=1, pos=1, dk=1, sc=512, il=16)

        def ro_pe(pe, l):
            t0 = 0 if l == 0 else TC // P
            for t in range(t0, TT):
                for k in range(KD):
                    if t == t0:
                        pe.wait_ge(norm["h"], nth("ffn", l) * NORM["h"] + (k + 1) * (2 if l == 0 else 1))
                    last = nc.tensor.matmul(ps[0][:, t * E:(t + 1) * E], H[:, k, t * P:(t + 1) * P],
                                            WS[:, WS_RT + k * E:WS_RT + (k + 1) * E], start=(k == 0), stop=(k == KD - 1))
            last.then_inc(ro["mm"], 1)
            for n, t in enumerate(range(t0, TT)):
                for half in range(2):
                    if n >= 2:
                        pe.wait_ge(ro["hc"], l * RO["hc"] + 2 * (n - 2) + half + 1)
                    for k in range(4):
                        last = nc.tensor.transpose(ps[4 + 2 * (n % 2) + half][:, k * P:(k + 1) * P],
                                                   H[:, 4 * half + k, t * P:(t + 1) * P], ident)
                    last.then_inc(ro["ht"], 1)
            pe.wait_ge(ro["sel"], l * RO["sel"] + 1)
            for t in range(t0, TT):
                for u in range(t0, t + 1):
                    nc.tensor.matmul(ps[2][:, t * E:(t + 1) * E], cn("before", P) if u == t else ones, r_sel[:, u, :],
                                     start=(u == t0), stop=(u == t))
            for t in range(t0, TT):
                last = nc.tensor.matmul(ps[3][:, 0:E], ones, r_sel[:, t, :], start=(t == t0), stop=(t == TT - 1))
            last.then_inc(ro["pos"], 1)

        def ro_act(act, l):
            t0 = 0 if l == 0 else TC // P
            act.wait_ge(ro["mm"], l * RO["mm"] + 1)
            nc.scalar.activation(r_sc[:, t0:, :], ps[0][:, t0 * E:TT * E].rearrange("p (t e) -> p t e", e=E), ACT.Sigmoid).then_inc(ro["sg"], 1)
            for n, t in enumerate(range(t0, TT)):
                for half in range(2):
                    act.wait_ge(ro["ht"], l * RO["ht"] + 2 * n + half + 1)
                    if n >= 2 and half == 0:
                        act.wait_ge(ro[f"hs{n % 2}"], 16)
                    nc.scalar.activation(HTB[:, n % 2, half * 512:(half + 1) * 512], ps[4 + 2 * (n % 2) + half][:, :],
                                         ACT.Copy).then_inc(ro["hc"], 1)

        def ro_dve(dve, ch, l):
            t0 = 0 if l == 0 else TC // P
            n = TT - t0
            V = nc.vector
            dve.wait_ge(ro["sg"], l * RO["sg"] + 1)
            ch.link(V.tensor_tensor(r_bi[:, t0:, :], r_sc[:, t0:, :], bcast(sm("rb", 0, E), 1, n), ALU.add))
            for t in range(t0, TT):
                for g in range(NG):
                    ch.add(V.max(r_mx[:, t * NG + g, :], r_bi[:, t, g * 8:(g + 1) * 8]))
            ch.settle()
            ch.link(V.tensor_tensor(r_gs[:, t0:, :], r_mx[:, t0 * NG:, 0].rearrange("p (t g) -> p t g", g=NG),
                                    r_mx[:, t0 * NG:, 1].rearrange("p (t g) -> p t g", g=NG), ALU.add))
            for t in range(t0, TT):
                other, own = bcast(r_gs[:, t, :], 1, NG), bcast(r_gs[:, t, :], 2, NG)
                ch.add(V.tensor_tensor(r_cmp[:, t, :].rearrange("p (g o) -> p g o", o=NG), other, own, ALU.is_gt))
                ch.add(V.tensor_tensor(r_eq[:, t, :].rearrange("p (g o) -> p g o", o=NG), other, own, ALU.is_equal))
            ch.settle()
            ch.link(V.tensor_tensor(r_eq[:, t0:, :], r_eq[:, t0:, :], bcast(cn("tri", NG * NG), 1, n), ALU.mult))
            ch.link(V.tensor_tensor(r_cmp[:, t0:, :], r_cmp[:, t0:, :], r_eq[:, t0:, :], ALU.add))
            ch.link(V.tensor_reduce(r_rank[:, t0:, :], r_cmp[:, t0:, :].rearrange("p t (g o) -> p t g o", o=NG), AX_X, ALU.add))
            ch.link(V.tensor_scalar(r_rank[:, t0:, :], r_rank[:, t0:, :], float(TOPG), None, ALU.is_lt))
            ch.link(V.tensor_scalar(r_pen[:, t0:, :], r_rank[:, t0:, :], BIG, -BIG, ALU.mult, ALU.add))

            def wide(v):
                return bcast(v, 2, 8)
            for t in range(t0, TT):
                ch.link(V.tensor_tensor(r_msk[:, t, :].rearrange("p (g o) -> p g o", o=8), r_bi[:, t, :].rearrange("p (g o) -> p g o", o=8),
                                        wide(r_rank[:, t, :]), ALU.mult))
                ch.link(V.tensor_tensor(r_msk[:, t, :].rearrange("p (g o) -> p g o", o=8), r_msk[:, t, :].rearrange("p (g o) -> p g o", o=8),
                                        wide(r_pen[:, t, :]), ALU.add))
                ch.link(V.max(r_top[:, t, :], r_msk[:, t, :]))
                ch.link(V.match_replace(r_rep[:, t, :], r_top[:, t, :], r_msk[:, t, :], -2 * BIG))
            V.tensor_tensor(r_sel[:, t0:, :], r_rep[:, t0:, :], r_msk[:, t0:, :], ALU.not_equal).then_inc(ro["sel"], 1)
            dve.wait_ge(ro["sel"], l * RO["sel"] + 1)
            weight = r_q[:, t0:, 1, :]
            ch.link(V.tensor_tensor(weight, r_sel[:, t0:, :], r_sc[:, t0:, :], ALU.mult))
            ch.link(V.tensor_reduce(r_sum[:, t0:], weight, AX_X, ALU.add))
            ch.link(V.tensor_scalar(r_sum[:, t0:], r_sum[:, t0:], 1e-20, None, ALU.add))
            ch.link(V.reciprocal(r_rec[:, t0:], r_sum[:, t0:]))
            ch.link(V.tensor_scalar(r_rec[:, t0:], r_rec[:, t0:], ROUTED_SCALE, None, ALU.mult))
            ch.link(V.tensor_tensor(weight, weight, bcast(r_rec[:, t0:], 2, E), ALU.mult))
            for t in range(t0, TT):
                ch.add(V.tensor_tensor_scan(out=r_cs[:, t, :], data0=ones[:, 0:E], data1=r_sel[:, t, :], initial=0.0, op0=ALU.mult, op1=ALU.add))
            B = BLOCK[l]
            dve.wait_ge(ro["pos"], l * RO["pos"] + 1)
            ch.add(V.tensor_copy(r_pos[:, t0:, :], ps[2][:, t0 * E:TT * E].rearrange("p (t e) -> p t e", e=E)))
            ch.link(V.tensor_copy(r_excl, ps[3][:, 0:E]))
            ch.add(V.tensor_scalar(r_over[:, t0:, :], r_pos[:, t0:, :], float(B), None, ALU.is_ge))
            ch.link(V.tensor_scalar(r_nov, r_excl, float(B), None, ALU.is_gt))
            for j in (2, 3):
                ch.add(V.scalar_tensor_tensor(r_over[:, t0:, :], r_pos[:, t0:, :], float(j * B), r_over[:, t0:, :], ALU.is_ge, ALU.add))
                ch.link(V.scalar_tensor_tensor(r_nov, r_excl, float(j * B), r_nov, ALU.is_gt, ALU.add))
            ch.link(V.tensor_tensor_scan(out=r_incl, data0=ones[:, 0:E], data1=r_nov, initial=0.0, op0=ALU.mult, op1=ALU.add))
            ch.link(V.tensor_tensor(r_excl, r_incl, r_nov, ALU.subtract))
            ch.link(V.tensor_tensor(r_excl, r_excl, cn("past", E), ALU.add))
            ch.add(V.scalar_tensor_tensor(r_at[:, t0:, :], r_over[:, t0:, :], -float(B), r_pos[:, t0:, :], ALU.mult, ALU.add))
            ch.add(V.tensor_tensor(r_blk[:, t0:, :], r_over[:, t0:, :], bcast(r_excl, 1, n), ALU.add))
            ch.link(V.tensor_scalar(r_hot[:, t0:, :], r_over[:, t0:, :], 0.0, None, ALU.is_gt))
            ch.link(V.tensor_tensor(r_blk[:, t0:, :], r_blk[:, t0:, :], r_hot[:, t0:, :], ALU.mult))
            ch.link(V.tensor_tensor(r_blk[:, t0:, :], r_blk[:, t0:, :], bcast(cn("e", E), 1, n), ALU.add))
            ch.link(V.scalar_tensor_tensor(r_q[:, t0:, 0, :], r_at[:, t0:, :], float(NBLK), r_blk[:, t0:, :], ALU.mult, ALU.add))
            for k in range(TOPK):
                ch.link(V.scalar_tensor_tensor(r_hot[:, t0:, :], r_cs[:, t0:, :], float(k + 1), r_sel[:, t0:, :], ALU.is_equal, ALU.mult))
                ch.link(V.tensor_tensor(r_qk[:, t0:, :, :], r_q[:, t0:, :, :], bcast(r_hot[:, t0:, :], 2, 2), ALU.mult))
                ch.link(V.tensor_reduce(r_dk[:, t0:, :, k], r_qk[:, t0:, :, :], AX_X, ALU.add))
            ch.add(V.tensor_copy(ADRI[:, t0 * TOPK:].rearrange("p (t k) -> p t k", k=TOPK), r_dk[:, t0:, 0, :]))
            ch.add(V.tensor_copy(WK[:, t0:, :], r_dk[:, t0:, 1, :]))
            ch.link(V.tensor_tensor(r_ej[:, :, :], bcast(r_incl, 1, NOV), bcast(cn("j", NOV), 2, E), ALU.is_le))
            ch.link(V.tensor_reduce(r_few, r_ej[:, :, :], AX_X, ALU.add))
            ch.add(V.tensor_copy(EJI[:, 0:E], cn("e", E)))
            ch.link(V.tensor_copy(EJI[:, E:], r_few))
            ch.link(V.tensor_scalar(r_few[:, 0:NOV // 4], cn("j", NOV)[:, ::4], r_incl[:, E - 1:E], None, ALU.is_lt))
            ch.link(V.tensor_reduce(r_sum[:, 0:1], r_few[:, 0:NOV // 4], AX_X, ALU.add))
            V.tensor_copy(BEYOND[:, :], r_sum[:, 0:1]).then_inc(ro["dk"], 1)

        SH = arena(0, 2 * T)
        XG, XT_ = arena(1024, 2, D), arena(3072, 2, KD * P)
        SG, HD = arena(5120, 2, 2 * P), arena(5632, 2, 2 * P)
        YB = arena(6144, 2, D)
        sgl = arena(11264, 2, T)
        ACC = arena(12288, TT, D)
        GB = arena(1024, 2, 4, D)
        GU_W = [W[:, i * CHUNK:(i + 1) * CHUNK] for i in range(3)] + [BR[:, :, :].rearrange("p k t -> p (k t)")]
        DN_W = [W[:, 3 * CHUNK:3 * CHUNK + 2 * D], W[:, 3 * CHUNK + 2 * D:4 * CHUNK], arena(8192, 2 * D), arena(8192 + 2048, 2 * D)]
        GU_N = 2 * KD * FE
        gu_in = [sem(f"gate_up_in{j}") for j in range(4)]
        dn_in = [sem(f"down_in{j}") for j in range(4)]
        x_got = [sem(f"rows_in{j}") for j in range(2)]
        y_out = [sem(f"rows_out{j}") for j in range(2)]
        g_got = [sem(f"combine_in{j}") for j in range(2)]
        slots_blank = sem("slots_blank")
        bk = {n: sem(f"block_{n}") for n in ("ig", "iy", "t", "tc", "gu", "sig", "silu", "hid", "dn", "ya", "yd")}
        sh, SHN = signals("shared", w=32, gu=2, sig=2, silu=2, hid=2, dn=8, res=8)
        cb, CB = signals("combine", c=32, flip=8)
        resid2 = sem("resid2")

        def groups_of(eng):
            return eng.value_load(BEYOND[0:1, 0:1], min_val=0, max_val=NOV // 4) + E // 4

        def tiles_of(l):
            return range(TT - TOKENS[l] // P, TT)

        def ex_sync(sp, l, before):
            tiles = tiles_of(l)
            for n, t in enumerate(tiles):
                sp.wait_ge(ro["hc"], l * RO["hc"] + 2 * n + 2)
                sp.dma_start(hx[l][n * P:(n + 1) * P, :], HTB[:, n % 2, :]).then_inc(ro[f"hs{n % 2}"], 16)

            def weights(e, s):
                sp.dma_start(GU_W[s], wexp[l, bass.ds(e, 1), :, 0:GU_N].rearrange("a p n -> p (a n)")).then_inc(gu_in[s], 16)

            def weights_down(e, s):
                sp.dma_start(DN_W[s], wexp[l, bass.ds(e, 1), :, GU_N:].rearrange("a p n -> p (a n)")).then_inc(dn_in[s], 16)

            sp.wait_ge(mg["o"], l * MG["o"] + KD)
            sp.dma_start(GU_W[3], wexp[l, E, :, 0:GU_N]).then_inc(sh["w"], 16)
            for s in range(3):
                weights(s, s)
            for s in range(2):
                weights_down(s, s)
            sp.wait_ge(sh["gu"], l * SHN["gu"] + 2)
            weights(3, 3)
            sp.wait_ge(ro["dk"], l * RO["dk"] + 1)
            sp.wait_ge(sh["hid"], l * SHN["hid"] + 2)
            sp.dma_start(DN_W[3], wexp[l, E, :, GU_N:]).then_inc(sh["w"], 16)
            weights_down(2, 2)
            sp.wait_ge(sh["dn"], l * SHN["dn"] + KD)
            weights_down(3, 3)
            groups = groups_of(sp)
            with sp.Fori(1, groups) as i:
                q = i * 4 + (before * 4 if l else 0)
                for s in range(4):
                    e = sp.value_load(EJI[0:1, bass.ds(i * 4 + s, 1)], min_val=0, max_val=E)
                    sp.wait_ge(bk["gu"], q + (s - 3))
                    weights(e, s)
                    sp.wait_ge(bk["dn"], q * 2 + (2 * s - 6))
                    weights_down(e, s)
            q = (groups + before if l else groups) * 4
            for s in range(2):
                sp.wait_ge(y_out[s], q * 8)
            for j in range(2 * len(tiles)):
                if j >= 2:
                    sp.wait_ge(cb["c"], l * CB["c"] + 4 * (j - 1))
                src = yrows[l][(j // 2) * P * TOPK:(j // 2 + 1) * P * TOPK, :].rearrange("(p k) d -> p k d", k=TOPK)
                sp.dma_start(GB[:, j % 2, :, :], src[:, (j % 2) * 4:(j % 2) * 4 + 4, :]).then_inc(g_got[j % 2], 16)
            return groups

        def ex_pool(pool, l, before):
            tiles, B = tiles_of(l), BLOCK[l]
            choice = IDS[:, l, :].rearrange("p (t k c) -> p t k c", k=TOPK, c=2)
            pool.wait_ge(slots_blank, 16 * L)
            pool.wait_ge(ro["dk"], l * RO["dk"] + 1)
            for t in tiles:
                for k in range(TOPK):
                    pool.indirect_dma_start(slots[l], bass.IndirectOffsetOnAxis(ap=ADRI[:, t * TOPK + k:t * TOPK + k + 1], axis=0),
                                            choice[:, t, k, :], None).then_inc(ro["sc"], 16)
            pool.wait_ge(ro["sc"], l * RO["sc"] + 16 * TOPK * len(tiles))
            pool.dma_start(IDX[:, :, :], slots[l].rearrange("(p b) a -> p b a", p=P)).then_inc(ro["il"], 16)
            pool.wait_ge(ro["il"], 16 * (l + 1))
            for n in range(2):
                pool.wait_ge(ro[f"hs{n}"], l * RO[f"hs{n}"] + 16 * (len(tiles) // 2))
            groups = groups_of(pool)

            used, flipped_rows, ready = (pool.alloc_register(f"{n}{l}") for n in ("used", "flipped_rows", "ready"))

            def fetch(n, q, s, first=False):
                pool.reg_mov(ready, q + (s + 1))
                if not first:
                    pool.reg_mov(used, q * 8)
                    pool.reg_mov(flipped_rows, q * 2 + (2 * s - 2))
                pool.wait_ge(ro["il"], 16 * (l + 1))
                if not first:
                    pool.wait_ge(x_got[s], used)
                    pool.wait_ge(bk["t"], flipped_rows)
                pool.tensor_copy(IDG[0:B, s:s + 1], IDX[0:B, bass.ds(n, 1), 0]).then_inc(bk["ig"], 1)
                pool.wait_ge(ro["hs1"], l * RO["hs1"] + 16 * (len(tiles) // 2))
                pool.wait_ge(bk["ig"], ready)
                pool.indirect_dma_start(XG[0:B, s, :], None, hx[l], bass.IndirectOffsetOnAxis(ap=IDG[0:B, s:s + 1], axis=0)).then_inc(x_got[s], 16)

            def store(n, q, s, first=False):
                pool.reg_mov(ready, q + (s + 1))
                if not first:
                    pool.reg_mov(used, q * 8)
                pool.wait_ge(ro["il"], 16 * (l + 1))
                if not first:
                    pool.wait_ge(y_out[s], used)
                pool.tensor_copy(IDY[0:B, s:s + 1], IDX[0:B, bass.ds(n, 1), 1]).then_inc(bk["iy"], 1)
                pool.wait_ge(ro["dk"], l * RO["dk"] + 1)
                pool.wait_ge(bk["iy"], ready)
                pool.wait_ge(bk["ya"], ready)
                pool.wait_ge(bk["yd"], ready)
                pool.indirect_dma_start(yrows[l], bass.IndirectOffsetOnAxis(ap=IDY[0:B, s:s + 1], axis=0), YB[0:B, s, :], None).then_inc(y_out[s], 16)

            q0 = before * 4 if l else 0
            for s in range(2):
                fetch(s, q0, s, first=l == 0)
            for s in range(2):
                fetch(s + 2, q0 + 2, s)
            for s in range(2):
                store(s, q0, s, first=l == 0)
            with pool.Fori(1, groups * 2 - 1) as i:
                for s in range(2):
                    fetch(i * 2 + (s + 2), i * 2 + (q0 + 2), s)
                for s in range(2):
                    store(i * 2 + s, i * 2 + q0, s)
            for s in range(2):
                store(groups * 4 + (s - 2), groups * 4 + (q0 - 2), s)
            return groups

        def ex_pe(pe, l, before):
            tiles, B = tiles_of(l), BLOCK[l]
            c0 = tiles[0] * P
            pe.wait_ge(sh["w"], l * SHN["w"] + 16)
            w = GU_W[3].rearrange("p (k m) -> p k m", k=KD)
            pe.wait_ge(ro["hc"], l * RO["hc"] + 2 * len(tiles))
            for m in range(2):
                for up in range(2):
                    for k in range(KD):
                        last = nc.tensor.matmul(ps[4 + 2 * up + m][:, c0:], w[:, k, up * FE + m * P:up * FE + (m + 1) * P], H[:, k, c0:],
                                                start=(k == 0), stop=(k == KD - 1))
                last.then_inc(sh["gu"], 1)
            pe.wait_ge(ro["dk"], l * RO["dk"] + 1)
            pe.wait_ge(sh["hid"], l * SHN["hid"] + 2)
            pe.wait_ge(sh["w"], l * SHN["w"] + 32)
            wt = DN_W[3].rearrange("p (k m) -> p k m", k=2)
            for m in range(KD):
                for k in range(2):
                    last = nc.tensor.matmul(ps[m][:, c0:], wt[:, k, m * P:(m + 1) * P], SH[:, k * T + c0:(k + 1) * T], start=(k == 0), stop=(k == 1))
                last.then_inc(sh["dn"], 1)
            groups = groups_of(pe)
            pe.wait_ge(sh["res"], l * SHN["res"] + KD)

            def flip(q, s, first=False):
                pe.wait_ge(x_got[s], q * 8 + 16)
                for half in range(2):
                    if not (first and s == 0):
                        pe.wait_ge(bk["tc"], q * 2 + (2 * s + half - 1))
                    for k in range(4):
                        rows = XG[0:B, s, (4 * half + k) * P:(4 * half + k + 1) * P]
                        flip_by = nc.tensor.transpose if k or B == P else nc.tensor.matmul
                        last = flip_by(ps[half][:, k * B:(k + 1) * B], rows, ident[0:B, 0:B])
                    last.then_inc(bk["t"], 1)

            def gate_up(q, s, w, filled, first=False):
                pe.wait_ge(gu_in[w], filled)
                pe.wait_ge(bk["tc"], q * 2 + (2 * s + 2))
                if not first:
                    pe.wait_ge(bk["hid"], q + (s - 1))
                wt = GU_W[w].rearrange("p (k m) -> p k m", k=KD)
                for m in range(4):
                    for k in range(KD):
                        last = nc.tensor.matmul(ps[2 + s][:, m * B:(m + 1) * B], wt[:, k, m * P:(m + 1) * P],
                                                XT_[:, s, k * B:(k + 1) * B], start=(k == 0), stop=(k == KD - 1))
                last.then_inc(bk["gu"], 1)

            def down(q, s, w, filled, first=False):
                pe.wait_ge(dn_in[w], filled)
                pe.wait_ge(bk["hid"], q + (s + 1))
                if not first:
                    pe.wait_ge(bk["ya"], q + (s - 1))
                    pe.wait_ge(bk["yd"], q + (s - 1))
                wt = DN_W[w].rearrange("p (k m) -> p k m", k=2)
                for half in range(2):
                    for k in range(2):
                        last = nc.tensor.matmul(ps[4 + 2 * s + half][0:B, :], HD[:, s, k * B:(k + 1) * B],
                                                wt[:, k, half * 512:(half + 1) * 512], start=(k == 0), stop=(k == 1))
                    last.then_inc(bk["dn"], 1)

            def pair(q, w, filled, first=False):
                for s in range(2):
                    flip(q, s, first)
                for s in range(2):
                    gate_up(q, s, w + s, filled, first)
                for s in range(2):
                    down(q, s, w + s, filled, first)

            q0 = before * 4 if l else 0
            for w in (0, 2):
                pair(q0 + w, w, q0 * 4 + 16, first=(l == 0 and w == 0))
            with pe.Fori(1, groups) as i:
                for w in (0, 2):
                    pair(i * 4 + (q0 + w), w, i * 16 + (q0 * 4 + 16))
            q = (groups + before if l else groups) * 4
            pe.wait_ge(bk["ya"], q)
            pe.wait_ge(bk["yd"], q)
            for n, t in enumerate(tiles):
                pe.wait_ge(cb["c"], l * CB["c"] + TOPK * (n + 1))
                for m in range(KD):
                    last = nc.tensor.transpose(ps[m][:, t * P:(t + 1) * P], ACC[:, t, m * P:(m + 1) * P], ident)
                    if n == len(tiles) - 1:
                        last.then_inc(cb["flip"], 1)
            return groups

        def ex_act(act, l, before):
            B, c0 = BLOCK[l], tiles_of(l)[0] * P
            for m in range(2):
                act.wait_ge(sh["gu"], l * SHN["gu"] + m + 1)
                nc.scalar.activation(sgl[:, m, c0:], ps[4 + m][:, c0:], ACT.Sigmoid).then_inc(sh["sig"], 1)
            act.wait_ge(ro["dk"], l * RO["dk"] + 1)
            groups = groups_of(act)

            def pair(q, first=False):
                for s in range(2):
                    for half in range(2):
                        act.wait_ge(bk["t"], q * 2 + (2 * s + half + 1))
                        if half == 0 and not first:
                            act.wait_ge(bk["gu"], q + (s - 1))
                        nc.scalar.activation(XT_[:, s, half * 4 * B:(half + 1) * 4 * B], ps[half][:, 0:4 * B], ACT.Copy).then_inc(bk["tc"], 1)
                for s in range(2):
                    act.wait_ge(bk["gu"], q + (s + 1))
                    if not first:
                        act.wait_ge(bk["hid"], q + (s - 1))
                    nc.scalar.activation(SG[:, s, 0:2 * B], ps[2 + s][:, 0:2 * B], ACT.Sigmoid).then_inc(bk["sig"], 1)
                for s in range(2):
                    act.wait_ge(bk["dn"], q * 2 + (2 * s + 1))
                    if not first:
                        act.wait_ge(y_out[s], q * 8)
                    nc.scalar.activation(YB[0:B, s, 0:512], ps[4 + 2 * s][0:B, :], ACT.Copy).then_inc(bk["ya"], 1)

            q0 = before * 4 if l else 0
            pair(q0, first=(l == 0))
            with act.Fori(1, groups * 2) as i:
                pair(i * 2 + q0)
            return groups

        def ex_dve(dve, ch, l, before):
            tiles, B = tiles_of(l), BLOCK[l]
            c0 = tiles[0] * P
            V = nc.vector

            def add_to_residual(m, c0):
                for half in range(c0 // TC, 2):
                    part = slice(half * TC, (half + 1) * TC)
                    last = V.scalar_tensor_tensor(R[:, m, part], ps[m][:, part], MOD[:, 40 + m, half:half + 1], R[:, m, part], ALU.mult, ALU.add)
                    if half == 0:
                        ch.add(last)
                return last

            for m in range(2):
                dve.wait_ge(sh["sig"], l * SHN["sig"] + m + 1)
                V.tensor_tensor(sgl[:, m, c0:], ps[4 + m][:, c0:], sgl[:, m, c0:], ALU.mult).then_inc(sh["silu"], 1)
                dve.wait_ge(sh["silu"], l * SHN["silu"] + m + 1)
                V.tensor_tensor(SH[:, m * T + c0:(m + 1) * T], ps[6 + m][:, c0:], sgl[:, m, c0:], ALU.mult).then_inc(sh["hid"], 1)
            for m in range(KD):
                dve.wait_ge(sh["dn"], l * SHN["dn"] + m + 1)
                add_to_residual(m, c0).then_inc(sh["res"], 1)
            groups = groups_of(dve)

            def pair(q, first=False):
                for s in range(2):
                    dve.wait_ge(bk["sig"], q + (s + 1))
                    V.tensor_tensor(SG[:, s, 0:2 * B], ps[2 + s][:, 0:2 * B], SG[:, s, 0:2 * B], ALU.mult).then_inc(bk["silu"], 1)
                    dve.wait_ge(bk["silu"], q + (s + 1))
                    if not first:
                        dve.wait_ge(bk["dn"], q * 2 + (2 * s - 2))
                    V.tensor_tensor(HD[:, s, 0:2 * B], ps[2 + s][:, 2 * B:4 * B], SG[:, s, 0:2 * B], ALU.mult).then_inc(bk["hid"], 1)
                for s in range(2):
                    dve.wait_ge(bk["dn"], q * 2 + (2 * s + 2))
                    if not first:
                        dve.wait_ge(y_out[s], q * 8)
                    V.tensor_copy(YB[0:B, s, 512:D], ps[5 + 2 * s][0:B, :]).then_inc(bk["yd"], 1)

            q0 = before * 4 if l else 0
            pair(q0, first=(l == 0))
            with dve.Fori(1, groups * 2) as i:
                pair(i * 2 + q0)
            for j in range(2 * len(tiles)):
                t = tiles[j // 2]
                past = 4 if l else 0
                dve.wait_ge(g_got[j % 2], 16 * (past + j // 2 + 1))
                for k in range(4):
                    wk = WK[:, t, (j % 2) * 4 + k:(j % 2) * 4 + k + 1]
                    if k == 0 and j % 2 == 0:
                        V.tensor_scalar(ACC[:, t, :], GB[:, 0, k, :], wk, None, ALU.mult).then_inc(cb["c"], 1)
                    else:
                        dve.wait_ge(cb["c"], l * CB["c"] + j * 4 + k)
                        V.scalar_tensor_tensor(ACC[:, t, :], GB[:, j % 2, k, :], wk, ACC[:, t, :], ALU.mult, ALU.add).then_inc(cb["c"], 1)
            for m in range(KD):
                dve.wait_ge(sh["res"], l * SHN["res"] + m + 1)
                dve.wait_ge(cb["flip"], l * CB["flip"] + m + 1)
                add_to_residual(m, c0).then_inc(resid2, 1)
            return groups

        XS = arena(0, TT, D)
        OUT = arena(8192, TX // P, D)
        released = {CH_MLA: (mla["z"], MLA["z"], 4), CH_MLA + 1: (mla["p"], MLA["p"], 20), CH_UQ: (mla["p"], MLA["p"], 8),
                    CH_ML: (ml["z"], ML["z"], 4), CH_ML + 1: (ml["z"], ML["z"], 7),
                    CH_RW: (rw["z"], RW["z"], 4), CH_RW + 1: (rw["z"], RW["z"], 8), CH_RW + 2: (rw["z"], RW["z"], 9),
                    CH_OUT: (mg["o"], MG["o"], 4), CH_OUT + 1: (mg["o"], MG["o"], 8)}
        for m in range(KD):
            released[CH_MERGE + m] = (mg["b"], MG["b"], 3 * (m + 1))

        def wait_released(sp, l, j):
            before = [c for c in ALL_CHUNKS[:ALL_CHUNKS.index((l, j))] if c[1] % RING == j % RING]
            if before and before[-1][1] < N_MOD_CH:
                sp.wait_ge(mod_mm, MOD_CHUNKS.index(before[-1]) + 1)
            elif before:
                used, per_layer, k = released[before[-1][1]]
                sp.wait_ge(used, before[-1][0] * per_layer + k)

        block = es.enter_context(nc.Block())

        @block.sync
        def _(sp):
            sp.dma_start(CT[:, :], consts).then_inc(consts_in, 16)
            sp.dma_start(IDS[:, :, :], ids[:, :, 0:2 * TT * TOPK]).then_inc(ids_in, 16)
            sp.dma_start(XS[:, :, :], xin.rearrange("(t p) d -> p t d", p=P)).then_inc(x_moved, 16)
            for l in range(L):
                sp.dma_start(slots[l].rearrange("(p b) c -> p (b c)", p=P), ids[:, l, 2 * TT * TOPK:]).then_inc(slots_blank, 16)
            done = 0
            for l in range(L):
                if l:
                    sp.wait_ge(resid2, (l - 1) * KD + KD)
                sp.dma_start(S_[:, :], smalls[l, :, :]).then_inc(smalls_in, 16)
                sp.dma_start(WS[:, :], wsm[l, :, :]).then_inc(smalls_in, 16)
                for m, j in ORDER_OF_USE[l]:
                    wait_released(sp, m, j)
                    sp.dma_start(chunk(j)[:, 0:CH_COLS[j]], wst[m, j, :, 0:CH_COLS[j]]).then_inc(chunk_in[j % RING], 16)
                done = ex_sync(sp, l, done)
            sp.wait_ge(flip_copied, 2 * KD)
            sp.dma_start(out.rearrange("(t p) d -> p t d", p=P), OUT[:, :, :]).then_inc(x_moved, 16)
            sp.wait_ge(x_moved, 32)

        @block.gpsimd
        def _(pool):
            pool.wait_ge(ids_in, 16)
            done = 0
            for l in range(L):
                done = ex_pool(pool, l, done)

        @block.tensor
        def _(pe):
            pe.wait_ge(consts_in, 16)
            pe.wait_ge(x_moved, 16)
            for k in range(KD):
                for t in range(TT):
                    last = nc.tensor.transpose(ps[k][:, t * P:(t + 1) * P], XS[:, t, k * P:(k + 1) * P], ident)
                last.then_inc(flipped, 1)
            pe.wait_ge(flip_copied, KD)
            done = 0
            for l in range(L):
                if l == 0:
                    pe.wait_ge(cond_ready, 2)
                    for j in range(MOD_FIRST):
                        for k in range(KD):
                            mod_rows(pe, 0, j, k, j)
                    mod_turn(pe, ALL_CHUNKS[:MOD_FIRST], 4)
                norm_pe(pe, l, "mix", 0)
                mla_pe(pe, l)
                ml_pe(pe, l)
                rw_pe(pe, l)
                mg_pe(pe, l)
                norm_pe(pe, l, "ffn", 0 if l == 0 else TC)
                ro_pe(pe, l)
                done = ex_pe(pe, l, done)
            norm_pe(pe, 0, "fin", TC)
            for k in range(KD):
                pe.wait_ge(norm["n"], nth("fin", 0) * KD + k + 1)
                if k >= 4:
                    pe.wait_ge(flip_copied, KD + k - 3)
                for t in range(2):
                    last = nc.tensor.transpose(ps[k % 4][:, t * P:(t + 1) * P], H[:, k, TC + t * P:TC + (t + 1) * P], ident)
                last.then_inc(flipped, 1)

        @block.scalar
        def _(act):
            ch = Chain(act, act_sem)
            act.wait_ge(consts_in, 16)
            nc.scalar.activation(COND[:, :, :], cn("cond", 16).rearrange("p (k c) -> p k c", c=2), ACT.Sigmoid).then_inc(cond_ready, 1)
            for k in range(0, KD, 2):
                act.wait_ge(flipped, k + 1)
                nc.scalar.activation(R[:, k, :], ps[k][:, :], ACT.Copy).then_inc(flip_copied, 1)
            act.wait_ge(flip_copied, KD)
            done = 0
            for l in range(L):
                if l:
                    act.wait_ge(resid2, (l - 1) * KD + KD)
                norm_act_square(act, l, "mix", 0)
                if l == 0:
                    for j in range(MOD_FIRST):
                        mod_copy(act, 0, j, j, j)
                norm_act_rs(act, ch, l, "mix", 0)
                norm_act_modulate(act, l, "mix", 0)
                mla_act(act, ch, l)
                ml_act(act, ch, l)
                rw_act(act, ch, l)
                mg_act(act, l)
                act.wait_ge(mg["r"], l * MG["r"] + KD)
                c0 = 0 if l == 0 else TC
                norm_act_square(act, l, "ffn", c0)
                norm_act_rs(act, ch, l, "ffn", c0)
                norm_act_modulate(act, l, "ffn", c0)
                ro_act(act, l)
                done = ex_act(act, l, done)
            act.wait_ge(resid2, (L - 1) * KD + KD)
            norm_act_square(act, 0, "fin", TC)
            norm_act_rs(act, ch, 0, "fin", TC)

        @block.vector
        def _(dve):
            ch = Chain(dve, dve_sem)
            dve.wait_ge(cond_ready, 1)
            nc.vector.tensor_tensor(COND[:, :, :], COND[:, :, :], cn("cond", 16).rearrange("p (k c) -> p k c", c=2), ALU.mult).then_inc(cond_ready, 1)
            for k in range(1, KD, 2):
                dve.wait_ge(flipped, k + 1)
                nc.vector.tensor_copy(R[:, k, :], ps[k][:, :]).then_inc(flip_copied, 1)
            done = 0
            for l in range(L):
                if l == 0:
                    mod_dve(dve, ch, ALL_CHUNKS[:MOD_FIRST], 4)
                dve.wait_ge(smalls_in, l * 32 + 32)
                norm_dve(dve, l, "mix", 0)
                mla_dve(dve, ch, l)
                ml_dve(dve, ch, l)
                rw_dve(dve, ch, l)
                mg_dve(dve, ch, l)
                norm_dve(dve, l, "ffn", 0 if l == 0 else TC)
                ro_dve(dve, ch, l)
                done = ex_dve(dve, ch, l, done)
            dve.wait_ge(norm["rs"], nth("fin", 0) + 1)
            for k in range(KD):
                nc.vector.scalar_tensor_tensor(H[:, k, TC:], R[:, k, TC:], cn("g_final", 1, k), RS[:, TC:], ALU.mult, ALU.mult).then_inc(norm["n"], 1)
            for k in range(KD):
                dve.wait_ge(flipped, KD + k + 1)
                nc.vector.tensor_copy(OUT[:, :, k * P:(k + 1) * P], ps[k % 4][:, 0:2 * P].rearrange("p (t m) -> p t m", t=2)).then_inc(flip_copied, 1)


def constants(c, c_ctx, g_final, b_mod, g_mix, g_ffn):
    f = np.zeros((P, CN_N), np.float32)

    def put(name, v, r0=0):
        f[r0:r0 + v.shape[0], CN[name]:CN[name] + v.shape[1]] = v
    i = np.arange(P)
    put("ident", np.eye(P, dtype=np.float32))
    put("ones", np.ones((P, P), np.float32))
    put("bd", (i[:, None] // 64 == i[None, :] // 64).astype(np.float32))
    m = np.concatenate([np.where(i[:, None] <= i[None, :], 0, -BIG), np.where(i[:, None] >= i[None, :], 0, -BIG)], 1)
    put("mlmask", m.astype(np.float32))
    s, t = i[:, None] % 64, np.arange(64)[None, :]
    put("rwmask", np.concatenate([s < t, s <= t, s > t, s >= t], 1).astype(np.float32))
    put("lev", np.concatenate([(s // (2 * b) == t // (2 * b)) & (s // b != t // b) for b in (1, 2, 4, 8, 16, 32)], 1).astype(np.float32))
    put("reset", np.tile((np.arange(T) % C != 0).astype(np.float32), (P, 1)))
    n = np.arange(TX)
    half = ROPE // 2
    inv = (np.float32(10000.0) ** (-np.arange(0, half, 2, dtype=np.float32) / half)).astype(np.float32)
    ang = np.stack([(n // 64).astype(np.float32)[:, None] * inv, (n % 64).astype(np.float32)[:, None] * inv], 1)
    cos, sin = np.ones((ROPE, T), np.float32), np.zeros((ROPE, T), np.float32)
    for a in range(2):
        for b in range(2):
            rows = slice(a * 16 + b * 8, a * 16 + b * 8 + 8)
            cos[rows, TC:] = np.cos(ang[:, a, :]).T
            sin[rows, TC:] = np.sin(ang[:, a, :]).T * (1 if b else -1)
    put("cs", np.concatenate([cos, sin, cos, sin], 0))
    sel = np.zeros((64, 8, P), np.float32)
    for u in range(8):
        sel[32 * (u // 4) + u % 4, u, :] = 1
    put("sel", sel.reshape(64, 8 * P))
    put("dup", (i[:64, None] % 32 == i[None, :64] % 32).astype(np.float32))
    g = np.arange(NG)
    put("tri", np.tile((g[None, :] < g[:, None]).astype(np.float32).reshape(1, -1), (P, 1)))
    put("eps", np.tile(np.array([[EPS, RW_EPS]], np.float32), (P, 1)))
    put("cond", np.stack([c_ctx.reshape(KD, P).T, c.reshape(KD, P).T], 2).reshape(P, 16))
    for l in range(L):
        f[:, CN["b_mod"] + 48 * l:CN["b_mod"] + 48 * (l + 1)] = b_mod[l].reshape(48, P).T
        f[:, CN["g_norm"] + 16 * l:CN["g_norm"] + 16 * (l + 1)] = np.stack([g_mix[l], g_ffn[l]]).reshape(16, P).T
    put("g_final", g_final.reshape(KD, P).T)
    put("before", (i[:, None] < i[None, :]).astype(np.float32))
    put("e", np.tile(np.arange(E, dtype=np.float32), (P, 1)))
    put("past", np.tile((E - 1 - np.arange(E)).astype(np.float32), (P, 1)))
    put("j", np.tile(np.arange(NOV, dtype=np.float32), (P, 1)))
    return f


def slot_ids():
    ids = np.zeros((P, L, ID_N), np.int32)
    for l in range(L):
        token = (np.arange(P)[:, None, None] + P * np.arange(TT)[None, :, None] - (T - TOKENS[l])).astype(np.int32)
        choice = ids[:, l, 0:2 * TT * TOPK].reshape(P, TT, TOPK, 2)
        choice[..., 0] = token
        choice[..., 1] = token * TOPK + np.arange(TOPK)
        slot = np.arange(P * NBLK).reshape(P, NBLK)
        ids[:, l, 2 * TT * TOPK + 1::2] = TOKENS[l] * TOPK + slot // NBLK + P * (slot % 2)
    return ids


def lay_out(q):
    z = np.zeros
    swap = np.arange(ROPE) ^ 8
    smalls, wsm, wst = z((L, P, SM_N), np.float32), z((L, P, WS_N), np.float32), z((L, N_CH, P, CHUNK), np.float32)
    wexp = z((L, E + 1, P, EXPERT), np.float32)

    def tiles(w, m):
        k, n = w.shape[0] // P, w.shape[1] // m
        return w.reshape(k, P, n, m).transpose(2, 1, 0, 3).reshape(n, P, k * m)

    for l in range(L):
        def col(name, v):
            v = np.asarray(v).reshape(-1, P).T
            smalls[l, :, SM[name]:SM[name] + v.shape[1]] = v
        for a, b in (("g_cq", "g_cq"), ("g_ckv", "g_ckv"), ("ml_g", "ml_g_norm"),
                     ("mu", "rw_mu"), ("w0", "rw_w0"), ("a0", "rw_a0"), ("k_k", "rw_k_k"), ("k_a", "rw_k_a"), ("r_k", "rw_r_k"),
                     ("lnx_w", "rw_lnx_w"), ("lnx_b", "rw_lnx_b")):
            col(a, q[b][l])
        for r, name in ((0, "ml_b_i"), (64, "ml_b_f")):
            for d in range(2):
                smalls[l, r + 32 * d:r + 32 * d + 4, SM["ml_b"]] = q[name][l, d]
        smalls[l, :, SM["rb"]:SM["rb"] + E] = q["router_bias"][l][None, :]
        wsm[l, :, WS_W2:WS_W2 + 256] = q["rw_w2"][l].reshape(P, 256)
        wsm[l, :, WS_A2:WS_A2 + 256] = q["rw_a2"][l].reshape(P, 256)
        wsm[l, :, WS_G2:WS_G2 + 256] = q["rw_g2"][l]
        wsm[l, :, WS_RT:WS_RT + KD * E] = q["w_router"][l].reshape(KD, P, E).transpose(1, 0, 2).reshape(P, KD * E)
        wst[l, 0:12] = tiles(q["w_mod"][l], 512)
        w = q["w_in"][l]
        rope = w[:, 640:672]
        small = np.concatenate([rope, rope[:, swap], z((D, 64), np.float32)], 1)
        mla = np.concatenate([w[:, 0:640], small], 1)
        wst[l, CH_MLA] = tiles(mla[:, 0:512], 512)[0]
        wst[l, CH_MLA + 1, :, 0:2048] = tiles(mla[:, 512:768], 256)[0]
        wst[l, CH_MLA + 1, :, 2048:3072] = tiles(q["w_uk"][l], 512)[0]
        wst[l, CH_MLA + 1, :, 3072:4096] = tiles(q["w_uv"][l], 512)[0]
        uq = q["w_uq"][l].reshape(QL, HEADS, NOPE + ROPE)
        uq = np.concatenate([uq, uq[:, :, NOPE:][:, :, swap]], 2).reshape(QL, HEADS * P)
        wst[l, CH_UQ, :, 0:3072] = tiles(uq, HEADS * P)[0]
        gates = z((D, P), np.float32)
        for r, c in ((0, 1440), (32, 1444), (64, 1448), (96, 1452)):
            gates[:, r:r + 4] = w[:, c:c + 4]
        mlw = np.concatenate([w[:, 672:1440], gates], 1)
        wst[l, CH_ML] = tiles(mlw[:, 0:512], 512)[0]
        wst[l, CH_ML + 1, :, 0:3072] = tiles(mlw[:, 512:896], 384)[0]
        wst[l, CH_RW:CH_RW + 2] = tiles(w[:, 1456:1456 + 1024], 512)
        wst[l, CH_RW + 2, :, 0:1024] = tiles(w[:, 2480:2608], 128)[0]
        gw = w[:, 2608:].reshape(KD, P, 3, KD, P)
        br = np.concatenate([q["w_br_mla"][l], q["w_br_ml"][l], q["w_br_rw"][l]], 0).reshape(KD, P, KD, P)
        wst[l, CH_MERGE:CH_MERGE + 8, :, 0:3072] = gw.transpose(3, 1, 0, 2, 4).reshape(KD, P, 3072)
        wst[l, CH_MERGE:CH_MERGE + 8, :, 3072:] = br.transpose(2, 1, 0, 3).reshape(KD, P, 1024)
        wst[l, CH_OUT:CH_OUT + 2] = tiles(q["w_out"][l], 512)
        half = 2 * KD * FE
        gu = wexp[l, :, :, 0:half].reshape(E + 1, P, KD, 2, FE)
        for at, names in ((0, ("w_e_gate", "w_s_gate")), (1, ("w_e_up", "w_s_up"))):
            gu[0:E, :, :, at] = q[names[0]][l].reshape(E, KD, P, FE).transpose(0, 2, 1, 3)
            gu[E, :, :, at] = q[names[1]][l].reshape(KD, P, FE).transpose(1, 0, 2)
        dn = np.concatenate([q["w_e_down"][l], q["w_s_down"][l][None]], 0)
        wexp[l, :, :, 0:half] = gu.reshape(E + 1, P, half)
        wexp[l, :, :, half:] = dn.reshape(E + 1, 2, P, D).transpose(0, 2, 1, 3).reshape(E + 1, P, 2 * D)
    x = np.concatenate([q["ctx"][0], q["x"][0]], 0)
    return dict(xin=x, ids=slot_ids(), consts=constants(q["c"][0], q["c_ctx"], q["g_final"], q["b_mod"], q["g_mix"], q["g_ffn"]), smalls=smalls, wsm=wsm, wst=wst, wexp=wexp)


def kernel(**inputs):
    import concourse.bacc as _bacc
    from concourse.bass_utils import run_bass_kernel_spmd as _run

    arrays = lay_out({k: np.asarray(v) for k, v in inputs.items()})
    nc = _bacc.Bacc("TRN2", target_bir_lowering=False, num_devices=1)
    args = {n: nc.dram_tensor(f"in_{n}", a.shape, mybir.dt.from_np(a.dtype), kind="ExternalInput").ap() for n, a in arrays.items()}
    out = nc.dram_tensor("out_0", (TX, D), F32, kind="ExternalOutput").ap()
    build(nc, out=out, **args)
    r = _run(nc, [{f"in_{n}": a for n, a in arrays.items()}], core_ids=[0])
    return r.results[0]["out_0"].reshape(1, TX, D)
```
